# Optimizing a Trainium2 kernel written in Bass

```python
import math
import jax, jax.numpy as jnp
from jax import lax
import numpy as np

D_MODEL = 1024
BATCH = 1
SEQ = 1024
DEPTH = 2
DEC_BATCH = 8
DEC_SEQ = 16
PAST_LEN = 512

CHUNK = 64
HEAD_DIM = 64
ROPE_THETA = 10000.0
RMS_EPS = 1e-6
NEG_INF = -1e30
ATTN_SCALE = HEAD_DIM ** -0.5
Q_BLOCK = 128
A_HEADS = D_MODEL // (4 * HEAD_DIM)
A_WIDTH = A_HEADS * 2 * HEAD_DIM
B_HEADS = D_MODEL // (2 * HEAD_DIM)
B_KV_HEADS = B_HEADS // 4
B_GROUP = B_HEADS // B_KV_HEADS
B_WIDTH = B_HEADS * HEAD_DIM
WINDOW = 128
SWA_PREV_CHUNKS = WINDOW // CHUNK
IN_EVEN = 3 * A_WIDTH + (B_HEADS + 2 * B_KV_HEADS) * HEAD_DIM
MIX_EVEN = A_WIDTH + B_WIDTH
C_HEADS = D_MODEL // HEAD_DIM
MIX_ODD = C_HEADS * HEAD_DIM
C_PREV_CHUNKS = 8
REL_CLIP = 128
D_FF = ((8 * D_MODEL // 3 + 127) // 128) * 128
CONV_W = 3
N_EVEN = (DEPTH + 1) // 2
N_ODD = DEPTH // 2

kernel_name = "streaming_hybrid_encoder_step"

def rmsnorm(x, g):
    xf = x.astype(jnp.float32)
    y = xf * lax.rsqrt(jnp.mean(xf * xf, axis=-1, keepdims=True) + RMS_EPS)
    return (y * g.astype(jnp.float32)).astype(x.dtype)

def ada_norm(x, c, w, b, g):
    m = jax.nn.silu(c) @ w + b
    shift, scale, gate = jnp.split(m[:, None, :], 3, axis=-1)
    return rmsnorm(x, g) * (1 + scale) + shift, gate

def rope(x, pos):
    half = HEAD_DIM // 2
    inv = ROPE_THETA ** (-jnp.arange(half, dtype=jnp.float32) / half)
    ang = pos.astype(jnp.float32)[:, None] * inv[None, :]
    shape = (pos.shape[0],) + (1,) * (x.ndim - 3) + (half,)
    cos = jnp.cos(ang).reshape(shape)
    sin = jnp.sin(ang).reshape(shape)
    xf = x.astype(jnp.float32)
    x1, x2 = xf[..., :half], xf[..., half:]
    return jnp.concatenate([x1 * cos - x2 * sin, x2 * cos + x1 * sin], axis=-1).astype(x.dtype)

def split_even(proj):
    b, t = proj.shape[:2]
    cuts = [A_WIDTH, 2 * A_WIDTH, 3 * A_WIDTH, 3 * A_WIDTH + B_HEADS * HEAD_DIM,
            3 * A_WIDTH + (B_HEADS + B_KV_HEADS) * HEAD_DIM]
    qa, ka, va, qb, kb, vb = jnp.split(proj, cuts, axis=-1)
    qa = qa.reshape(b, t, A_HEADS, 2, HEAD_DIM)
    ka = ka.reshape(b, t, A_HEADS, 2, HEAD_DIM)
    va = va.reshape(b, t, A_HEADS, 2 * HEAD_DIM)
    qb = qb.reshape(b, t, B_HEADS, HEAD_DIM)
    kb = kb.reshape(b, t, B_KV_HEADS, HEAD_DIM)
    vb = vb.reshape(b, t, B_KV_HEADS, HEAD_DIM)
    return qa, ka, va, qb, kb, vb

def diff_core(q, k, v, lam, mask):
    s = jnp.einsum('bqhcd,bkhcd->bhcqk', q, k).astype(jnp.float32) * ATTN_SCALE
    if mask is not None:
        s = jnp.where(mask, s, NEG_INF)
    p = jax.nn.softmax(s, axis=-1)
    w = p[:, :, 0] - lam * p[:, :, 1]
    return jnp.einsum('bhqk,bkhe->bqhe', w.astype(v.dtype), v)

def diff_attn_prompt(q, k, v, lam):
    b, t = q.shape[:2]
    nb = t // Q_BLOCK
    qblocks = jnp.moveaxis(q.reshape(b, nb, Q_BLOCK, A_HEADS, 2, HEAD_DIM), 1, 0)
    key_chunk = jnp.arange(t) // CHUNK

    def one_block(args):
        qblk, bi = args
        q_chunk = (bi * Q_BLOCK + jnp.arange(Q_BLOCK)) // CHUNK
        return diff_core(qblk, k, v, lam, key_chunk[None, :] <= q_chunk[:, None])

    o = lax.map(one_block, (qblocks, jnp.arange(nb)))
    return jnp.moveaxis(o, 0, 1).reshape(b, t, A_HEADS, 2 * HEAD_DIM)

def sink_core(q, k, v, sinks, mask):
    b, nq = q.shape[:2]
    qg = q.reshape(b, nq, B_KV_HEADS, B_GROUP, HEAD_DIM)
    s = jnp.einsum('bqngd,bknd->bngqk', qg, k).astype(jnp.float32) * ATTN_SCALE
    if mask is not None:
        s = jnp.where(mask, s, NEG_INF)
    sink = jnp.broadcast_to(sinks.astype(jnp.float32).reshape(1, B_KV_HEADS, B_GROUP, 1, 1),
                            s.shape[:-1] + (1,))
    p = jax.nn.softmax(jnp.concatenate([s, sink], axis=-1), axis=-1)[..., :-1]
    o = jnp.einsum('bngqk,bknd->bqngd', p.astype(v.dtype), v)
    return o.reshape(b, nq, B_HEADS * HEAD_DIM)

def swa_prompt(q, k, v, sinks):
    b, t = q.shape[:2]
    nc = t // CHUNK
    pad = SWA_PREV_CHUNKS * CHUNK
    band = pad + CHUNK
    kp = jnp.pad(k, ((0, 0), (pad, 0), (0, 0), (0, 0)))
    vp = jnp.pad(v, ((0, 0), (pad, 0), (0, 0), (0, 0)))
    qc = jnp.moveaxis(q.reshape(b, nc, CHUNK, B_HEADS, HEAD_DIM), 1, 0)

    def one_chunk(args):
        qi, ci = args
        kb = lax.dynamic_slice_in_dim(kp, ci * CHUNK, band, axis=1)
        vb = lax.dynamic_slice_in_dim(vp, ci * CHUNK, band, axis=1)
        valid = (ci * CHUNK - pad + jnp.arange(band)) >= 0
        return sink_core(qi, kb, vb, sinks, valid[None, :])

    o = lax.map(one_chunk, (qc, jnp.arange(nc)))
    return jnp.moveaxis(o, 0, 1).reshape(b, t, B_WIDTH)

def relbias_core(q, k, v, table, qpos, kpos, mask):
    b, nq = q.shape[:2]
    s = jnp.einsum('bqhd,bkhd->bhqk', q, k).astype(jnp.float32) * ATTN_SCALE
    rel = jnp.clip(qpos[:, None] - kpos[None, :], -REL_CLIP, REL_CLIP) + REL_CLIP
    s = s + table.astype(jnp.float32)[:, rel][None]
    if mask is not None:
        s = jnp.where(mask, s, NEG_INF)
    p = jax.nn.softmax(s, axis=-1)
    o = jnp.einsum('bhqk,bkhd->bqhd', p.astype(v.dtype), v)
    return o.reshape(b, nq, MIX_ODD)

def band_prompt(q, k, v, table):
    b, t = q.shape[:2]
    nc = t // CHUNK
    pad = C_PREV_CHUNKS * CHUNK
    band = pad + CHUNK
    kp = jnp.pad(k, ((0, 0), (pad, 0), (0, 0), (0, 0)))
    vp = jnp.pad(v, ((0, 0), (pad, 0), (0, 0), (0, 0)))
    qc = jnp.moveaxis(q.reshape(b, nc, CHUNK, C_HEADS, HEAD_DIM), 1, 0)

    def one_chunk(args):
        qi, ci = args
        kb = lax.dynamic_slice_in_dim(kp, ci * CHUNK, band, axis=1)
        vb = lax.dynamic_slice_in_dim(vp, ci * CHUNK, band, axis=1)
        qpos = ci * CHUNK + jnp.arange(CHUNK)
        kpos = ci * CHUNK - pad + jnp.arange(band)
        return relbias_core(qi, kb, vb, table, qpos, kpos, (kpos >= 0)[None, :])

    o = lax.map(one_chunk, (qc, jnp.arange(nc)))
    return jnp.moveaxis(o, 0, 1).reshape(b, t, MIX_ODD)

def even_mixer(h, pos, lam, lam_init, g_sub, sinks, w_in, w_out, cache):
    b, t = h.shape[:2]
    qa, ka, va, qb, kb, vb = split_even(h @ w_in)
    qa, ka, qb, kb = rope(qa, pos), rope(ka, pos), rope(qb, pos), rope(kb, pos)
    if cache is None:
        oa = diff_attn_prompt(qa, ka, va, lam)
        ob = swa_prompt(qb, kb, vb, sinks)
        rows = min(WINDOW, t)
        kb_new, vb_new = kb[:, -rows:], vb[:, -rows:]
    else:
        ck_a, cv_a, ck_b, cv_b = cache
        k_all = jnp.concatenate([ck_a.reshape(b, -1, A_HEADS, 2, HEAD_DIM), ka], axis=1)
        v_all = jnp.concatenate([cv_a, va], axis=1)
        oa = diff_core(qa, k_all, v_all, lam, None)
        kb_all = jnp.concatenate([ck_b, kb], axis=1)
        vb_all = jnp.concatenate([cv_b, vb], axis=1)
        ob = sink_core(qb, kb_all, vb_all, sinks, None)
        rows = ck_b.shape[1]
        kb_new, vb_new = kb_all[:, -rows:], vb_all[:, -rows:]
    oa = rmsnorm(oa, g_sub) * (1 - lam_init)
    y = jnp.concatenate([oa.reshape(b, t, A_WIDTH), ob], axis=-1) @ w_out
    return y, (ka.reshape(b, t, A_HEADS, 2 * HEAD_DIM), va, kb_new, vb_new)

def odd_mixer(h, pos, table, w_in, w_out, cache):
    b, t = h.shape[:2]
    q, k, v = [z.reshape(b, t, C_HEADS, HEAD_DIM) for z in jnp.split(h @ w_in, 3, axis=-1)]
    if cache is None:
        o = band_prompt(q, k, v, table)
        rows = min(C_PREV_CHUNKS * CHUNK, t)
        k_new, v_new = k[:, -rows:], v[:, -rows:]
    else:
        ck, cv = cache
        rows = ck.shape[1]
        k_all = jnp.concatenate([ck, k], axis=1)
        v_all = jnp.concatenate([cv, v], axis=1)
        kpos = PAST_LEN - rows + jnp.arange(rows + t)
        o = relbias_core(q, k_all, v_all, table, pos, kpos, None)
        k_new, v_new = k_all[:, -rows:], v_all[:, -rows:]
    return o @ w_out, (k_new, v_new)

def conv_ffn(h, conv_state, w_up, conv_w, conv_b, w_down):
    t = h.shape[1]
    u = h @ w_up
    up = jnp.concatenate([conv_state, u], axis=1)
    y = conv_b
    for j in range(CONV_W):
        y = y + up[:, j:j + t] * conv_w[j]
    a, g = jnp.split(y, 2, axis=-1)
    return (jax.nn.silu(g) * a) @ w_down, up[:, -(CONV_W - 1):]

def setup_inputs(seed: int = 0) -> dict:
    key = jax.random.key(seed)
    ks = iter(jax.random.split(key, 32))

    def nrm(shape, scale):
        return jax.random.normal(next(ks), shape, jnp.float32) * scale

    b_rows = min(WINDOW, PAST_LEN)
    c_rows = min(C_PREV_CHUNKS * CHUNK, PAST_LEN)
    return {
        "x_prompt": nrm((BATCH, SEQ, D_MODEL), 1.0),
        "x_sample": nrm((DEC_BATCH, DEC_SEQ, D_MODEL), 1.0),
        "c_prompt": nrm((BATCH, D_MODEL), 1.0),
        "c_sample": nrm((DEC_BATCH, D_MODEL), 1.0),
        "cache_a_k": nrm((N_EVEN, DEC_BATCH, PAST_LEN, A_HEADS, 2 * HEAD_DIM), 1.0),
        "cache_a_v": nrm((N_EVEN, DEC_BATCH, PAST_LEN, A_HEADS, 2 * HEAD_DIM), 1.0),
        "cache_b_k": nrm((N_EVEN, DEC_BATCH, b_rows, B_KV_HEADS, HEAD_DIM), 1.0),
        "cache_b_v": nrm((N_EVEN, DEC_BATCH, b_rows, B_KV_HEADS, HEAD_DIM), 1.0),
        "cache_c_k": nrm((N_ODD, DEC_BATCH, c_rows, C_HEADS, HEAD_DIM), 1.0),
        "cache_c_v": nrm((N_ODD, DEC_BATCH, c_rows, C_HEADS, HEAD_DIM), 1.0),
        "state_conv": nrm((DEPTH, DEC_BATCH, CONV_W - 1, 2 * D_FF), 1.0),
        "ada_w": nrm((DEPTH, 2, D_MODEL, 3 * D_MODEL), 0.5 * D_MODEL ** -0.5),
        "ada_b": nrm((DEPTH, 2, 3 * D_MODEL), 0.02),
        "norm_g": 1.0 + nrm((DEPTH, 2, D_MODEL), 0.05),
        "final_g": 1.0 + nrm((D_MODEL,), 0.05),
        "w_in_even": nrm((N_EVEN, D_MODEL, IN_EVEN), D_MODEL ** -0.5),
        "w_out_even": nrm((N_EVEN, MIX_EVEN, D_MODEL), MIX_EVEN ** -0.5),
        "lam_q1": nrm((N_EVEN, HEAD_DIM), 0.1),
        "lam_k1": nrm((N_EVEN, HEAD_DIM), 0.1),
        "lam_q2": nrm((N_EVEN, HEAD_DIM), 0.1),
        "lam_k2": nrm((N_EVEN, HEAD_DIM), 0.1),
        "subln_g": 1.0 + nrm((N_EVEN, 2 * HEAD_DIM), 0.05),
        "sinks": nrm((N_EVEN, B_HEADS), 0.5),
        "w_in_odd": nrm((N_ODD, D_MODEL, 3 * MIX_ODD), D_MODEL ** -0.5),
        "w_out_odd": nrm((N_ODD, MIX_ODD, D_MODEL), MIX_ODD ** -0.5),
        "rel_bias": nrm((N_ODD, C_HEADS, 2 * REL_CLIP + 1), 0.5),
        "w_up": nrm((DEPTH, D_MODEL, 2 * D_FF), D_MODEL ** -0.5),
        "conv_w": nrm((DEPTH, CONV_W, 2 * D_FF), CONV_W ** -0.5),
        "conv_b": nrm((DEPTH, 2 * D_FF), 0.02),
        "w_down": nrm((DEPTH, D_FF, D_MODEL), D_FF ** -0.5),
    }

def reference(x_prompt, x_sample, c_prompt, c_sample, cache_a_k, cache_a_v, cache_b_k, cache_b_v,
              cache_c_k, cache_c_v, state_conv, ada_w, ada_b, norm_g, final_g, w_in_even, w_out_even,
              lam_q1, lam_k1, lam_q2, lam_k2, subln_g, sinks, w_in_odd, w_out_odd, rel_bias,
              w_up, conv_w, conv_b, w_down):
    bp, t_p = x_prompt.shape[:2]
    t_s = x_sample.shape[1]
    pos_p = jnp.arange(t_p, dtype=jnp.int32)
    pos_s = PAST_LEN + jnp.arange(t_s, dtype=jnp.int32)
    xp, xs = x_prompt, x_sample
    akp, avp, aks, avs, bkp, bvp, bks, bvs = [], [], [], [], [], [], [], []
    ckp, cvp, cks, cvs, convp, convs = [], [], [], [], [], []
    for l in range(DEPTH):
        i = l // 2
        hp, gp = ada_norm(xp, c_prompt, ada_w[l, 0], ada_b[l, 0], norm_g[l, 0])
        hs, gs = ada_norm(xs, c_sample, ada_w[l, 0], ada_b[l, 0], norm_g[l, 0])
        if l % 2 == 0:
            lam_init = 0.8 - 0.6 * math.exp(-0.3 * l)
            lam = (jnp.exp(jnp.sum(lam_q1[i].astype(jnp.float32) * lam_k1[i].astype(jnp.float32)))
                   - jnp.exp(jnp.sum(lam_q2[i].astype(jnp.float32) * lam_k2[i].astype(jnp.float32)))
                   + lam_init)
            yp, (a_k, a_v, b_k, b_v) = even_mixer(hp, pos_p, lam, lam_init, subln_g[i], sinks[i],
                                                  w_in_even[i], w_out_even[i], None)
            ys, (a_k2, a_v2, b_k2, b_v2) = even_mixer(
                hs, pos_s, lam, lam_init, subln_g[i], sinks[i], w_in_even[i], w_out_even[i],
                (cache_a_k[i], cache_a_v[i], cache_b_k[i], cache_b_v[i]))
            akp.append(a_k); avp.append(a_v); bkp.append(b_k); bvp.append(b_v)
            aks.append(a_k2); avs.append(a_v2); bks.append(b_k2); bvs.append(b_v2)
        else:
            yp, (c_k, c_v) = odd_mixer(hp, pos_p, rel_bias[i], w_in_odd[i], w_out_odd[i], None)
            ys, (c_k2, c_v2) = odd_mixer(hs, pos_s, rel_bias[i], w_in_odd[i], w_out_odd[i],
                                         (cache_c_k[i], cache_c_v[i]))
            ckp.append(c_k); cvp.append(c_v); cks.append(c_k2); cvs.append(c_v2)
        xp = xp + gp * yp
        xs = xs + gs * ys
        hp, gp = ada_norm(xp, c_prompt, ada_w[l, 1], ada_b[l, 1], norm_g[l, 1])
        hs, gs = ada_norm(xs, c_sample, ada_w[l, 1], ada_b[l, 1], norm_g[l, 1])
        zero_state = jnp.zeros((bp, CONV_W - 1, 2 * D_FF), hp.dtype)
        fp, st_p = conv_ffn(hp, zero_state, w_up[l], conv_w[l], conv_b[l], w_down[l])
        fs, st_s = conv_ffn(hs, state_conv[l], w_up[l], conv_w[l], conv_b[l], w_down[l])
        convp.append(st_p); convs.append(st_s)
        xp = xp + gp * fp
        xs = xs + gs * fs
    y_prompt = rmsnorm(xp, final_g)
    y_sample = rmsnorm(xs, final_g)
    return (y_prompt, y_sample,
            jnp.stack(akp), jnp.stack(avp), jnp.stack(aks), jnp.stack(avs),
            jnp.stack(bkp), jnp.stack(bvp), jnp.stack(bks), jnp.stack(bvs),
            jnp.stack(ckp), jnp.stack(cvp), jnp.stack(cks), jnp.stack(cvs),
            jnp.stack(convp), jnp.stack(convs))


_drawn_inputs = setup_inputs


def setup_inputs(seed=0):
    import zlib

    import numpy as np

    out = dict(_drawn_inputs(seed))
    spreads = {}
    factors = {'lam_q1': 6.011,
     'lam_k1': 8.0,
     'lam_q2': 8.0,
     'lam_k2': 8.0,
     'subln_g': 5.698,
     'sinks': 64.0,
     'rel_bias': 4.056,
     'conv_b': 6.809}
    for name, (base, spread) in spreads.items():
        noise = np.random.default_rng([zlib.crc32(name.encode()), seed]).standard_normal(out[name].shape)
        drawn = base * np.exp(spread * noise) if base else spread * noise
        out[name] = __import__('jax').numpy.asarray(drawn.astype(out[name].dtype))
    for name, factor in factors.items():
        out[name] = (out[name] * factor).astype(out[name].dtype)
    return out
```

```python
from contextlib import ExitStack

import numpy as np
import concourse.bass as bass
from concourse import mybir
from concourse.alu_op_type import AluOpType as ALU

F32 = mybir.dt.float32
F32R = mybir.dt.float32r
BF16 = mybir.dt.bfloat16
ACT = mybir.ActivationFunctionType
AX = mybir.AxisListType

P = 128
D = 1024
KT = D // P
SEQ = 1024
NB = 8
NS = 16
TS = NB * NS
TOK = SEQ + TS
TB = TOK // P
QB = SEQ // P
PAST = 512
HD = 64
CHUNK = 64
DFF = 2816
FT = DFF // P
NC9 = 1 + NB
EPS = 1e-6
SCALE = HD ** -0.5
NEG = -1e30
LAM_INIT = 0.2
IN_EVEN = 2304
THETA = 10000.0
COLS = ((0, 512), (512, 1024), (1024, TOK))

C_ID = 0
C_CA = C_ID + P
C_ADA = C_CA + 64
C_L = C_ADA + 10
C_R = C_L + 2 * P
C_MB = C_R + CHUNK
C_RB = C_MB + 2 * P
C_SEL = C_RB + P
C_N = C_SEL + 2
ROPE_N = SEQ + NS


def shape_constants():
    c = np.zeros((P, C_N), np.float32)
    c[:, C_ID:C_ID + P] = np.eye(P)
    r = np.arange(P)
    c[r, C_CA + (r // 32) * NS + r % NS] = 1
    for b in range(NC9):
        c[b, C_ADA + b] = c[NC9 + b, C_ADA + b] = c[2 * NC9, C_ADA + b] = 1
    c[0, C_L:C_L + CHUNK] = 1
    c[0, C_L + P + CHUNK:C_L + 2 * P] = 1
    c[0, C_R:C_R + CHUNK] = NEG
    for b in range(NB):
        for g in range(2):
            c[b, C_MB + g * P:C_MB + (g + 1) * P] = (4 * g + r // 32) == b
        c[b, C_RB:C_RB + P] = np.where(r // NS == b, 0, NEG)
    c[:, C_SEL] = (r % 32) < NS
    c[:, C_SEL + 1] = (r % 32) >= NS
    half = HD // 2
    inv = np.float32(THETA) ** (-np.arange(half, dtype=np.float32) / np.float32(half))
    pos = np.concatenate([np.arange(SEQ), PAST + np.arange(NS)]).astype(np.float32)
    ang = inv[r % half][:, None] * pos[None, :]
    cos = np.cos(ang).astype(np.float32)
    sin = np.where((r % HD < half)[:, None], -np.sin(ang), np.sin(ang)).astype(np.float32)
    return c, np.ascontiguousarray(np.stack([cos, sin], 1))


def top(ap):
    return ap.bitcast(BF16)[:, 1::2]


def mm3(pe, out, w, wl, x, xl, start, stop):
    pe.matmul(out, w, x, start=start, stop=False, skip_group_check=True)
    pe.matmul(out, top(w), xl, start=False, stop=False, skip_group_check=True)
    return pe.matmul(out, wl, top(x), start=False, stop=stop, skip_group_check=True)


class Chain:

    def __init__(self, eng, sem, base=0):
        self.eng, self.sem, self.base, self.n = eng, sem, base, 0

    def then(self, ins):
        self.n += 1
        ins.then_inc(self.sem, 1)
        self.eng.wait_ge(self.sem, self.base + self.n)

    def mark(self, ins):
        self.n += 1
        ins.then_inc(self.sem, 1)
        return self.base + self.n

    def moved(self):
        return self.base + self.n


def settle(eng, S):
    eng.sem_inc(S.settled, 1)


class Ring:

    def __init__(self, nc, ctx, tag, size, landed, high, low, used):
        self.size, self.landed, self.high, self.low, self.used = size, landed, high, low, used
        self.raw = [ctx.enter_context(nc.sbuf_tensor(f"{tag}_raw{s}", [P, 1024], F32)) for s in range(size)]
        self.w = [ctx.enter_context(nc.sbuf_tensor(f"{tag}_high{s}", [P, 1024], F32R)) for s in range(size)]
        self.wl = [ctx.enter_context(nc.sbuf_tensor(f"{tag}_low{s}", [P, 1024], BF16)) for s in range(size)]

    def at(self, c, turns=0):
        return c % self.size, c // self.size + turns

    def load(self, eng, c, src, turns=0, view=None):
        s, n = self.at(c, turns)
        if c >= self.size:
            eng.wait_ge(self.low[s], n)
        dst = self.raw[s][:, :]
        if view is not None:
            dst = dst.rearrange(view[0], **view[1])
        eng.dma_start(dst, src).then_inc(self.landed[s], 16)

    def split_high(self, act, c, turns=0):
        s, n = self.at(c, turns)
        act.wait_ge(self.landed[s], 16 * (n + 1))
        if c >= self.size:
            act.wait_ge(self.used[s], n)
        act.copy(self.w[s][:, :], self.raw[s][:, :]).then_inc(self.high[s], 1)

    def split_low(self, dve, c, turns=0):
        s, n = self.at(c, turns)
        dve.wait_ge(self.high[s], n + 1)
        dve.tensor_tensor(self.wl[s][:, :], self.raw[s][:, :], self.w[s][:, :].bitcast(F32),
                          ALU.subtract).then_inc(self.low[s], 1)

    def done(self, eng, c, turns=0):
        s, n = self.at(c, turns)
        eng.wait_ge(self.used[s], n + 1)

    def ready(self, pe, c, turns=0):
        s, n = self.at(c, turns)
        pe.wait_ge(self.low[s], n + 1)
        return self.w[s][:, :], self.wl[s][:, :]


def setup(nc, S, G, ins, ctx):
    def sb(name, shape, dt=F32):
        return ctx.enter_context(nc.sbuf_tensor(name, shape, dt))

    ring = Ring(nc, ctx, "ada", 3, S.f_landed, S.f_high, S.f_low, S.f_used)
    xrow = sb("xrow", [P, TB, D])
    crow = sb("crow", [NC9, D])
    csil = sb("csil", [NC9, D])
    cT = sb("cT", [P, KT * 10])
    cst = sb("cst", [P, KT, P], F32R)
    cb = sb("cb", [P, KT, P], BF16)
    msb = sb("msb", [32, 3 * D])
    vrow = sb("vrow", [64, P])
    crow2 = sb("crow2", [88, 4, P])
    lamv = sb("lamv", [P, 4, HD])
    lamp = sb("lamp", [P, 2, HD])
    lams = sb("lams", [P, 4])
    tab = sb("tab", [16, 257])
    rev = sb("rev", [16, 384])
    ps = G.psum
    xT, mod, gs, gT, cvT, K = G.xT, G.mod, G.gs, G.gT, G.cvT, G.consts
    ident = K[:, C_ID:C_ID + P]
    block = ctx.enter_context(nc.Block())
    ada_w = ins["ada_w"].rearrange("l s (k p) (j n) -> (l s) j k p n", p=P, j=3)
    ada_b = ins["ada_b"].rearrange("l s n -> (l s) n")

    @block.sync
    def _(sp):
        sp.dma_start(K[:, :], ins["consts"]).then_inc(S.const_in, 16)
        sp.dma_start(crow[0:1, :], ins["c_prompt"]).then_inc(S.c_in, 16)
        sp.dma_start(crow[1:NC9, :], ins["c_sample"]).then_inc(S.c_in, 16)
        sp.dma_start(vrow[0:32, :], ins["norm_g"].rearrange("l s (k p) -> (l s k) p", p=P)).then_inc(S.vec_in, 16)
        sp.dma_start(vrow[32:40, :], ins["final_g"].rearrange("(k p) -> k p", p=P)).then_inc(S.vec_in, 16)
        sp.dma_start(vrow[40:41, :], ins["subln_g"]).then_inc(S.vec_in, 16)
        for l in range(2):
            w = ins["conv_w"][l].rearrange("j (t p) -> (j t) p", p=P)
            b = ins["conv_b"][l].rearrange("(t p) -> t p", p=P)
            sp.dma_start(crow2[:, 2 * l, :], w[0:88, :]).then_inc(S.vec_in, 16)
            sp.dma_start(crow2[0:44, 2 * l + 1, :], w[88:132, :]).then_inc(S.vec_in, 16)
            sp.dma_start(crow2[44:88, 2 * l + 1, :], b).then_inc(S.vec_in, 16)
        for j, n in enumerate(("lam_q1", "lam_k1", "lam_q2", "lam_k2")):
            sp.dma_start(lamv[:, j, :], ins[n].broadcast_to([P, HD])).then_inc(S.lam_in, 16)
        sp.dma_start(tab[:, :], ins["rel_bias"][0]).then_inc(S.tab_in, 16)
        sp.dma_start(G.sinkp[:, :], ins["sinks"].broadcast_to([P, 8])).then_inc(S.sink_in, 16)
        for t in range(QB):
            sp.dma_start(xrow[:, t, :], ins["x_prompt"][0, t * P:(t + 1) * P, :]).then_inc(S.x_in[t], 16)
        sp.dma_start(xrow[:, QB, :], ins["x_sample"].rearrange("b t d -> (b t) d")).then_inc(S.x_in[QB], 16)
        for a in range(4):
            for j in range(3):
                for k in range(KT):
                    ring.load(sp, a * 24 + j * KT + k, ada_w[a, j, k])
        sp.wait_ge(S.rev_made, 2)
        sp.dma_start(G.rev_dram, rev[:, :]).then_inc(S.rev_out, 16)
        sp.wait_ge(S.rev_out, 16)
        sp.dma_start(G.bias_dram, bass.AP(G.rev_dram.tensor, P - 1, [[384, 16], [-1, P], [1, 256]])).then_inc(S.rev_out, 16)
        sp.wait_ge(S.rev_out, 32)

    @block.gpsimd
    def _(pool):
        pool.memset(G.ones[:, :], 1.0).then_inc(S.set_ones, 1)
        pool.memset(G.eps[:, :], EPS).then_inc(S.set_ones, 1)
        pool.memset(cst[:, :, :].bitcast(F32), 0.0).then_inc(S.set_zero, 1)
        pool.memset(cb[:, :, :], 0.0).then_inc(S.set_zero, 1)
        pool.memset(rev[:, 0:P], 0.0).then_inc(S.rev_made, 1)
        pool.memset(G.mhalf[:, :], -0.5).then_inc(S.set_ones, 1)
        for a in range(4):
            if a:
                pool.wait_ge(S.mod_mm, a)
            pool.dma_start(msb[2 * NC9:2 * NC9 + 1, :], ada_b[a:a + 1, :]).then_inc(S.adab_in, 16)

    @block.scalar
    def _(act):
        act.wait_ge(S.c_in, 32)
        act.activation(csil[:, :], crow[:, :], ACT.Silu).then_inc(S.csil, 1)
        act.wait_ge(S.lam_dot, 2)
        act.activation(lams[:, 2:4], lams[:, 0:2], ACT.Exp).then_inc(S.lam_exp, 1)
        act.wait_ge(S.cT_ready, 1)
        act.wait_ge(S.set_zero, 1)
        act.copy(cst[:, :, 0:NC9], cT[:, :].rearrange("p (k c) -> p k c", k=KT)[:, :, 0:NC9]).then_inc(S.c_high, 1)
        for c in range(3):
            ring.split_high(act, c)
        for q in range(18):
            act.wait_ge(S.x_turned, q + 1)
            t, half = q // 2, q % 2
            act.copy(xT[:, 4 * half:4 * half + 4, t * P:(t + 1) * P],
                     ps[:, 6 - 2 * (q % 2), :].rearrange("p (k t) -> p k t", k=4)).then_inc(S.x_evac, 1)
        for a in range(4):
            for j in range(3):
                for k in range(KT):
                    c = a * 24 + j * KT + k
                    if c + 3 < 96:
                        ring.split_high(act, c + 3)
                last = a * 24 + j * KT + KT - 1
                act.wait_ge(S.f_used[last % 3], last // 3 + 1)
                if a and j == 0:
                    act.wait_ge(S.mod_mm, a)
                act.copy(msb[0:2 * NC9, j * D:(j + 1) * D],
                         ps[0:2 * NC9, 2 * ((3 * a + j) % 2):2 * ((3 * a + j) % 2) + 2, :]
                         .rearrange("p b n -> p (b n)")).then_inc(S.ada_evac, 1)

    @block.tensor
    def _(pe):
        pe.wait_ge(S.const_in, 16)
        pe.wait_ge(S.csil, 1)
        for k in range(KT):
            mm = pe.transpose(ps[:, 7, 10 * k:10 * k + NC9], csil[:, k * P:(k + 1) * P], ident[0:NC9, 0:NC9])
        mm.then_inc(S.small_ready, 1)
        pe.wait_ge(S.vec_in, 16 * 9)
        pe.wait_ge(S.cT_ready, 1)
        pe.transpose(ps[:, 7, 0:41], vrow[0:41, :], ident[0:41, 0:41])
        for j in range(4):
            mm = pe.transpose(ps[:, 7, 64 + 88 * j:64 + 88 * (j + 1)], crow2[:, j, :], ident[0:88, 0:88])
        mm.then_inc(S.small_ready, 1)
        for q in range(18):
            t, half = q // 2, q % 2
            pe.wait_ge(S.x_in[t], 16)
            if q >= 2:
                pe.wait_ge(S.x_evac, q - 1)
            for k in range(4):
                kk = 4 * half + k
                mm = pe.transpose(ps[:, 6 - 2 * (q % 2), k * P:(k + 1) * P], xrow[:, t, kk * P:(kk + 1) * P], ident)
            mm.then_inc(S.x_turned, 1)
        pe.wait_ge(S.c_low, 2)
        pe.wait_ge(S.small_evac, 1)
        for a in range(4):
            for j in range(3):
                u = 3 * a + j
                if u >= 2:
                    pe.wait_ge(S.ada_evac, u - 1)
                for k in range(KT):
                    c = a * 24 + j * KT + k
                    w, wl = ring.ready(pe, c)
                    for h in range(2):
                        pe.matmul(ps[:, 2 * (u % 2) + h, :], cst[:, k, :], w[:, h * 512:(h + 1) * 512],
                                  start=(k == 0), stop=False)
                        mm = pe.matmul(ps[:, 2 * (u % 2) + h, :], cb[:, k, :], wl[:, h * 512:(h + 1) * 512],
                                       start=False, stop=(k == KT - 1))
                    mm.then_inc(S.f_used[c % 3], 1)
            pe.wait_ge(S.ada_evac, 3 * (a + 1))
            pe.wait_ge(S.adab_in, 16 * (a + 1))
            if a:
                pe.wait_ge(S.mod_evac, a)
            for n in range(24):
                mm = pe.matmul(ps[:, 7, 10 * n:10 * n + 10], msb[0:2 * NC9 + 1, n * P:(n + 1) * P],
                               K[0:2 * NC9 + 1, C_ADA:C_ADA + 10], start=(n == 0), stop=(n == 23),
                               skip_group_check=True)
            mm.then_inc(S.mod_mm, 1)

    @block.vector
    def _(dve):
        ch = Chain(dve, S.set_step)
        dve.wait_ge(S.lam_in, 64)
        for j in range(2):
            dve.tensor_tensor_reduce(out=lamp[:, j, :], in0=lamv[:, 2 * j, :], in1=lamv[:, 2 * j + 1, :], scale=1.0,
                                     scalar=0.0, op0=ALU.mult, op1=ALU.add,
                                     accum_out=lams[:, j:j + 1]).then_inc(S.lam_dot, 1)
        dve.wait_ge(S.tab_in, 16)
        dve.tensor_scalar(rev[:, P:384], tab[:, 255::-1], tab[:, 256:257], 1.0 / SCALE, ALU.subtract,
                          ALU.mult).then_inc(S.rev_made, 1)
        dve.wait_ge(S.small_ready, 1)
        dve.tensor_copy(cT[:, :].rearrange("p (k c) -> p k c", k=KT)[:, :, 0:NC9],
                        ps[:, 7, 0:80].rearrange("p (k c) -> p k c", k=KT)[:, :, 0:NC9]).then_inc(S.cT_ready, 1)
        dve.wait_ge(S.cT_ready, 1)
        for c in range(3):
            ring.split_low(dve, c)
        dve.wait_ge(S.c_high, 1)
        cT3 = cT[:, :].rearrange("p (k c) -> p k c", k=KT)[:, :, 0:NC9]
        dve.tensor_tensor(cst[:, :, NC9:2 * NC9], cT3, cst[:, :, 0:NC9].bitcast(F32), ALU.subtract).then_inc(S.c_low, 1)
        dve.wait_ge(S.set_zero, 2)
        dve.tensor_copy(cb[:, :, 0:NC9], cst[:, :, 0:NC9].bitcast(F32)).then_inc(S.c_low, 1)
        dve.wait_ge(S.lam_exp, 1)
        ch.then(dve.tensor_tensor(lams[:, 0:1], lams[:, 3:4], lams[:, 2:3], ALU.subtract))
        ch.then(dve.tensor_scalar(G.nlam[:, :], lams[:, 0:1], -LAM_INIT, None, ALU.add))
        dve.wait_ge(S.const_in, 16)
        dve.scalar_tensor_tensor(out=G.cfac[:, :], in0=K[:, C_SEL + 1:C_SEL + 2], scalar=G.nlam[:, 0:1],
                                 in1=K[:, C_SEL:C_SEL + 1], op0=ALU.mult, op1=ALU.add)
        dve.wait_ge(S.sink_in, 16)
        ch.then(dve.tensor_scalar(G.sinks_s[:, :], G.sinkp[:, 0::2], K[:, C_SEL:C_SEL + 1], None, ALU.mult))
        ch.then(dve.scalar_tensor_tensor(out=G.sinks_s[:, :], in0=G.sinkp[:, 1::2], scalar=K[:, C_SEL + 1:C_SEL + 2],
                                         in1=G.sinks_s[:, :], op0=ALU.mult, op1=ALU.add))
        dve.wait_ge(S.small_ready, 2)
        ch.then(dve.tensor_copy(gT[:, :], ps[:, 7, 0:41]))
        ch.then(dve.tensor_copy(cvT[:, :, :, :].rearrange("p l j t -> p (l j t)"), ps[:, 7, 64:416]))
        dve.tensor_scalar(G.gsub[:, :], gT[:, 40:41], 1.0 - LAM_INIT, None, ALU.mult).then_inc(S.small_evac, 1)
        for a in range(4):
            for j in range(3):
                for k in range(KT):
                    c = a * 24 + j * KT + k
                    if c + 3 < 96:
                        ring.split_low(dve, c + 3)
            dve.wait_ge(S.mod_mm, a + 1)
            ch.then(dve.tensor_copy(mod[:, a, :, :],
                                    ps[:, 7, 0:240].rearrange("p (n c) -> p n c", n=24)[:, :, 0:NC9]))
            dve.scalar_tensor_tensor(out=gs[:, a, :, :], in0=mod[:, a, 8:16, :], scalar=1.0,
                                     in1=gT[:, 8 * a:8 * a + 8].unsqueeze(2).broadcast_to([P, 8, NC9]),
                                     op0=ALU.add, op1=ALU.mult).then_inc(S.mod_evac, 1)


def norm_pe(pe, S, G, m, sq):
    for n in range(KT):
        pe.wait_ge(S.sq_ready, KT * m + n + 1)
        for b, (lo, hi) in enumerate(COLS):
            mm = pe.matmul(G.psum[:, b, 0:hi - lo], G.ones[:, :], sq[n % 2][:, lo:hi],
                           start=(n == 0), stop=(n == KT - 1))
        mm.then_inc(S.sq_used, 1)


def norm_act(act, S, G, m, sq, rs):
    for n in range(KT):
        if n >= 2:
            act.wait_ge(S.sq_used, KT * m + n - 1)
        act.activation(sq[n % 2][:, 0:TOK], G.xT[:, n, :], ACT.Square).then_inc(S.sq_ready, 1)
    act.wait_ge(S.sq_used, KT * (m + 1))
    act.activation(rs[:, 0:TOK], G.psum[:, 0:3, :].rearrange("p b n -> p (b n)")[:, 0:TOK], ACT.Sqrt,
                   scale=1.0 / D, bias=G.eps[:, 0:1]).then_inc(S.root, 1)


def mod_act(act, S, G, m, a, tmp, ts):
    act.wait_ge(S.hs_ready, m + 1)
    act.copy(G.h[:, :, SEQ:TOK], ts[:, 0:KT * TS].rearrange("p (k t) -> p k t", k=KT)).then_inc(S.hs_high, 1)
    for k in range(KT):
        act.wait_ge(S.hp_ready, KT * m + k + 1)
        act.activation(G.h[:, k, 0:SEQ], tmp[k % 2][:, 0:SEQ], ACT.Identity,
                       bias=G.mod[:, a, k, 0:1], scale=1.0).then_inc(S.hp_high, 1)


def mod_dve(dve, ch, S, G, m, a, tmp, rs, ts):
    dve.wait_ge(S.root, m + 1)
    ch.then(dve.reciprocal(rs[:, 0:TOK], rs[:, 0:TOK]))
    t4 = ts[:, 0:KT * TS].rearrange("p (k b q) -> p k b q", k=KT, b=NB)
    t3 = ts[:, 0:KT * TS].rearrange("p (k t) -> p k t", k=KT)
    ch.then(dve.tensor_tensor(t3, G.xT[:, :, SEQ:TOK], rs[:, SEQ:TOK].unsqueeze(1).broadcast_to([P, KT, TS]), ALU.mult))
    ch.then(dve.tensor_tensor(t4, t4, G.gs[:, a, :, 1:NC9].unsqueeze(3).broadcast_to([P, KT, NB, NS]), ALU.mult))
    dve.tensor_tensor(t4, t4, G.mod[:, a, 0:KT, 1:NC9].unsqueeze(3).broadcast_to([P, KT, NB, NS]),
                      ALU.add).then_inc(S.hs_ready, 1)

    def scaled(k):
        if k >= 2:
            dve.wait_ge(S.hp_low, KT * m + k - 1)
        dve.scalar_tensor_tensor(out=tmp[k % 2][:, 0:SEQ], in0=G.xT[:, k, 0:SEQ], scalar=G.gs[:, a, k, 0:1],
                                 in1=rs[:, 0:SEQ], op0=ALU.mult, op1=ALU.mult).then_inc(S.hp_ready, 1)

    scaled(0)
    dve.wait_ge(S.hs_high, m + 1)
    dve.tensor_tensor(G.hl[:, :, SEQ:TOK], t3, G.h[:, :, SEQ:TOK].bitcast(F32), ALU.subtract).then_inc(S.hs_low, 1)
    for k in range(KT):
        if k + 1 < KT:
            scaled(k + 1)
        dve.wait_ge(S.hp_high, KT * m + k + 1)
        dve.scalar_tensor_tensor(out=G.hl[:, k, 0:SEQ], in0=tmp[k % 2][:, 0:SEQ], scalar=G.mod[:, a, k, 0:1],
                                 in1=G.h[:, k, 0:SEQ].bitcast(F32), op0=ALU.add,
                                 op1=ALU.subtract).then_inc(S.hp_low, 1)


def h_ready(pe, S, m, k):
    if k == 0:
        pe.wait_ge(S.hs_low, m + 1)
    pe.wait_ge(S.hp_low, KT * m + k + 1)


def residual(dve, ch, S, G, n, a, acc, tmp):
    y = G.psum[:, acc:acc + 3, :].rearrange("p b n -> p (b n)")
    ys = y[:, SEQ:TOK].rearrange("p (b q) -> p b q", b=NB)
    ch.then(dve.tensor_tensor(tmp.rearrange("p (b q) -> p b q", b=NB), ys,
                              G.mod[:, a, 16 + n, 1:NC9].unsqueeze(2).broadcast_to([P, NB, NS]), ALU.mult))
    dve.tensor_tensor(G.xT[:, n, SEQ:TOK], G.xT[:, n, SEQ:TOK], tmp, ALU.add)
    return dve.scalar_tensor_tensor(out=G.xT[:, n, 0:SEQ], in0=y[:, 0:SEQ], scalar=G.mod[:, a, 16 + n, 0:1],
                                    in1=G.xT[:, n, 0:SEQ], op0=ALU.mult, op1=ALU.add)


UP = 2 + SEQ + NB * (NS + 2)
FBASE = 96
FCH = 6 * (FT // 2)
NG = FT // 2
HALO = FT * P


def ffn(nc, S, G, ins, outs, l):
    ctx = ExitStack()
    with ctx:
        def sb(name, shape, dt=F32):
            return ctx.enter_context(nc.sbuf_tensor(f"{name}{l}", shape, dt))

        ring = Ring(nc, ctx, f"ffn{l}", 3, S.f_landed, S.f_high, S.f_low, S.f_used)
        actr = sb("actr", [P, 2, TOK], F32R)
        actl = sb("actl", [P, 2, TOK], BF16)
        U = [sb(f"u{j}_", [P, UP]) for j in range(2)]
        Y = [sb(f"y{j}_", [P, UP]) for j in range(2)]
        st_raw = sb("st_raw", [16, 4, P])
        stT = sb("stT", [P, 64])
        so = sb("so", [P, 4, 18])
        sout = sb("sout", [18, 4, P])
        rtmp = sb("rtmp", [P, 2, TS])
        ps, h, hl = G.psum, G.h, G.hl
        ident = G.consts[:, C_ID:C_ID + P]
        m = 2 * l + 1
        fb = FBASE + l * FCH
        block = ctx.enter_context(nc.Block())
        w_up = ins["w_up"][l].rearrange("(k p) n -> p k n", p=P)
        w_down = ins["w_down"][l]
        state = ins["state_conv"][l].rearrange("b r (h f) -> (b r) h f", h=2)
        oprompt = outs["conv_p"][l, 0].rearrange("r (h f) -> r h f", h=2)
        osample = outs["conv_s"][l].rearrange("b r (h f) -> (b r) h f", h=2)
        U_s = [u[:, 2 + SEQ:UP].rearrange("p (b q) -> p b q", b=NB) for u in U]
        Y_s = [y[:, 2 + SEQ:UP].rearrange("p (b q) -> p b q", b=NB) for y in Y]

        def chunks(i):
            if isinstance(i, int):
                return (fb if i == 0 else fb + 4 + 6 * (i - 1)), 0
            return fb + 4, 2 * (i - 1)

        def groups(eng, body):
            body(0)
            with eng.Fori(1, NG - 1) as i:
                body(i)
            body(NG - 1)

        @block.sync
        def _(sp):
            def up(i, c, turns, j, gate):
                ring.load(sp, c, w_up[:, :, bass.ds(gate * HALO + (2 * i + j) * P, P)], turns,
                          ("p (k n) -> p k n", dict(k=KT)))

            def down(i, c, turns, j):
                ring.load(sp, c, w_down[bass.ds((2 * i + j) * P, P), :], turns)

            def body(i):
                c, t = chunks(i)
                up(i, c, t, 0, 0)
                c += 1
                if not (isinstance(i, int) and i == 0):
                    down(i - 1, c, t, 0)
                    down(i - 1, c + 1, t, 1)
                    c += 2
                up(i, c, t, 0, 1)
                up(i, c + 1, t, 1, 0)
                up(i, c + 2, t, 1, 1)

            groups(sp, body)
            c = fb + FCH - 2
            down(NG - 1, c, 0, 0)
            down(NG - 1, c + 1, 0, 1)

        @block.gpsimd
        def _(pool):
            def earlier(i):
                pool.dma_start(st_raw[:, :, :].rearrange("r (h j) f -> r h (j f)", h=2),
                               state[:, :, bass.ds(2 * i * P, 2 * P)]).then_inc(S.st_in, 16)

            def store(i):
                pool.wait_ge(S.so_evac, NG * l + i + 1)
                settle(pool, S)
                v = sout[:, :, :].rearrange("r (h j) f -> r h (j f)", h=2)
                pool.dma_start(oprompt[:, :, bass.ds(2 * i * P, 2 * P)], v[0:2]).then_inc(S.so_out, 16)
                pool.dma_start(osample[:, :, bass.ds(2 * i * P, 2 * P)], v[2:18]).then_inc(S.so_out, 16)

            if l == 0:
                pool.sem_inc(S.so_free, 1)
            earlier(0)

            def body(i):
                first = isinstance(i, int) and i == 0
                last = isinstance(i, int) and i == NG - 1
                n = NG * l + i
                for p in range(4):
                    j, g = p // 2, p % 2
                    pool.wait_ge(S.u_evac, 4 * n + p + 1)
                    settle(pool, S)
                    if p == 0 and not first:
                        pool.wait_ge(S.so_turned, n)
                        settle(pool, S)
                    pool.tensor_copy(so[:, 2 * g + j, 0:2], U[g][:, SEQ:SEQ + 2])
                    pool.tensor_copy(so[:, 2 * g + j, 2:18].rearrange("p (b r) -> p b r", b=NB),
                                     U_s[g][:, :, NS:NS + 2]).then_inc(S.u_last, 1)
                    if p == 0:
                        if not last:
                            pool.wait_ge(S.st_turned, n + 1)
                            settle(pool, S)
                            earlier(i + 1)
                        if not first:
                            store(i - 1)
                if not first:
                    pool.wait_ge(S.so_out, 32 * n)
                    pool.sem_inc(S.so_free, 1)

            groups(pool, body)
            store(NG - 1)
            pool.wait_ge(S.so_out, 32 * NG * (l + 1))
            pool.sem_inc(S.so_free, 1)

        @block.tensor
        def _(pe):
            norm_pe(pe, S, G, m, U)
            ring_used = S.f_used

            def up_tile(c, turns, acc, first=False):
                w, wl = ring.ready(pe, c, turns)
                for k in range(KT):
                    if first:
                        h_ready(pe, S, m, k)
                    for b, (lo, hi) in enumerate(COLS):
                        mm = mm3(pe, ps[:, acc + b, 0:hi - lo], w[:, k * P:(k + 1) * P], wl[:, k * P:(k + 1) * P],
                                 h[:, k, lo:hi], hl[:, k, lo:hi], k == 0, k == KT - 1)
                mm.then_inc(ring_used[c % 3], 1)

            def down(c, turns, i, last=False):
                d = KT * (NG * l + i)
                (w0, wl0), (w1, wl1) = ring.ready(pe, c, turns), ring.ready(pe, c + 1, turns)
                pe.wait_ge(S.act_low_f, 2 * (NG * l + i) + 2)
                for n in range(KT):
                    if n == 0:
                        pe.wait_ge(S.u_evac, 4 * (NG * l + i) + 4)
                    elif n == 1 and not last:
                        pe.wait_ge(S.u_evac, 4 * (NG * l + i) + 5)
                    elif n >= 2:
                        pe.wait_ge(S.d_evac, d + n - 1)
                    acc = 3 * ((1 + n) % 2)
                    for j, (w, wl) in enumerate(((w0, wl0), (w1, wl1))):
                        for b, (lo, hi) in enumerate(COLS):
                            mm = mm3(pe, ps[:, acc + b, 0:hi - lo], w[:, n * P:(n + 1) * P],
                                     wl[:, n * P:(n + 1) * P], actr[:, j, lo:hi], actl[:, j, lo:hi],
                                     j == 0, j == 1)
                        if n == KT - 1:
                            mm.then_inc(ring_used[(c + j) % 3], 1)
                    if n < KT - 1:
                        mm.then_inc(S.d_ready, 1)

            def last_rows(g):
                pe.wait_ge(S.u_last, 4 * g + 4)
                for q in range(4):
                    mm = pe.transpose(ps[0:18, 6, q * P:(q + 1) * P], so[:, q, :], ident)
                mm.then_inc(S.so_turned, 1)

            def body(i):
                c, t = chunks(i)
                first = isinstance(i, int) and i == 0
                g = NG * l + i
                pe.wait_ge(S.st_in, 16 * (g + 1))
                if not (first and l == 0):
                    pe.wait_ge(S.st_evac, g)
                if not first:
                    pe.wait_ge(S.u_evac, 4 * g - 1)
                else:
                    pe.wait_ge(S.root, m + 1)
                up_tile(c, t, 0, first)
                c += 1
                for q in range(4):
                    mm = pe.transpose(ps[:, 7, 16 * q:16 * q + 16], st_raw[:, q, :], ident[0:16, 0:16])
                mm.then_inc(S.st_turned, 1)
                if not first:
                    last_rows(g - 1)
                    down(c, t, i - 1)
                    c += 2
                    pe.wait_ge(S.d_evac, 8 * (g - 1) + 7)
                up_tile(c, t, 3)
                if first:
                    pe.wait_ge(S.u_evac, 4 * g + 1)
                else:
                    pe.wait_ge(S.d_evac, 8 * g)
                up_tile(c + 1, t, 0)
                pe.wait_ge(S.u_evac, 4 * g + 2)
                up_tile(c + 2, t, 3)

            groups(pe, body)
            last_rows(NG * (l + 1) - 1)
            down(fb + FCH - 2, 0, NG - 1, last=True)

        @block.scalar
        def _(act):
            norm_act(act, S, G, m, U, Y[0])
            for s in range(3):
                ring.split_high(act, fb + s)
            mod_act(act, S, G, m, m, U, Y[1])
            act.wait_ge(S.hp_low, KT * (m + 1))
            for j in range(2):
                act.activation(U[j][:, 0:2], G.ones[:, 0:2], ACT.Copy, scale=0.0).then_inc(S.u_zero, 1)

            def body(i):
                c, t = chunks(i)
                first = isinstance(i, int) and i == 0
                last = isinstance(i, int) and i == NG - 1
                g = NG * l + i
                act.wait_ge(S.st_turned, g + 1)
                if not (first and l == 0):
                    act.wait_ge(S.pads, 4 * g)
                act.copy(stT[:, :], ps[:, 7, 0:64]).then_inc(S.st_evac, 1)
                for p in range(4):
                    j, gate = p // 2, p % 2
                    at = p if first else (0, 3, 4, 5)[p]
                    s = (c + at) % 3
                    act.wait_ge(S.f_used[s], (c + at) // 3 + t + 1)
                    if not (first and l == 0 and p < 2):
                        act.wait_ge(S.conv, 4 * g + p - 1)
                        act.wait_ge(S.u_last, 4 * g + p - 1)
                    act.copy(U[gate][:, 2:2 + SEQ], ps[:, 3 * gate:3 * gate + 2, :].rearrange("p b n -> p (b n)"))
                    act.copy(U_s[gate][:, :, 2:2 + NS],
                             ps[:, 3 * gate + 2, 0:TS].rearrange("p (b q) -> p b q", b=NB)).then_inc(S.u_evac, 1)
                    if p == 0:
                        act.wait_ge(S.st_evac, g + 1)
                    q = 2 * gate + j
                    act.copy(U_s[gate][:, :, 0:2],
                             stT[:, 16 * q:16 * q + 16].rearrange("p (b r) -> p b r", b=NB)).then_inc(S.pads, 1)
                    nxt = c + at + 3
                    if not last or nxt < fb + FCH:
                        ring.split_high(act, nxt, t)
                    if p == 0 and not first:
                        last_rows(g - 1)
                        ring.split_high(act, c + 4, t)
                        ring.split_high(act, c + 5, t)
                    if gate:
                        act.wait_ge(S.conv, 4 * g + p + 1)
                        act.activation(Y[1][:, 0:UP - 2], Y[1][:, 0:UP - 2], ACT.Silu).then_inc(S.silu, 1)
                        act.wait_ge(S.prod, 2 * g + j + 1)
                        act.copy(actr[:, j, 0:SEQ], Y[0][:, 0:SEQ])
                        act.copy(actr[:, j, SEQ:TOK].rearrange("p (b q) -> p b q", b=NB),
                                 Y_s[0][:, :, 0:NS]).then_inc(S.act_high_f, 1)

            def last_rows(g):
                act.wait_ge(S.so_turned, g + 1)
                act.wait_ge(S.so_free, g + 1)
                act.copy(sout[:, :, :].rearrange("r q f -> r (q f)"), ps[0:18, 6, :]).then_inc(S.so_evac, 1)

            groups(act, body)
            last_rows(NG * (l + 1) - 1)

        @block.vector
        def _(dve):
            ch = Chain(dve, S.dve_step[m])
            for s in range(3):
                ring.split_low(dve, fb + s)
            mod_dve(dve, ch, S, G, m, m, U, Y[0], Y[1])
            cv = G.cvT

            def body(i):
                c, t = chunks(i)
                first = isinstance(i, int) and i == 0
                last = isinstance(i, int) and i == NG - 1
                g = NG * l + i
                for p in range(4):
                    j, gate = p // 2, p % 2
                    f = gate * FT + 2 * i + j
                    at = p if first else (0, 3, 4, 5)[p]
                    dve.wait_ge(S.pads, 4 * g + p + 1)
                    if not gate and not (first and l == 0 and j == 0):
                        dve.wait_ge(S.act_low_f, 2 * g + j)
                    n = UP - 2
                    u, y = U[gate], Y[gate]
                    ch.then(dve.tensor_scalar(y[:, 0:n], u[:, 2:2 + n], cv[:, l, 2, bass.ds(f, 1)],
                                              cv[:, l, 3, bass.ds(f, 1)], ALU.mult, ALU.add))
                    ch.then(dve.scalar_tensor_tensor(out=y[:, 0:n], in0=u[:, 1:1 + n], scalar=cv[:, l, 1, bass.ds(f, 1)],
                                                     in1=y[:, 0:n], op0=ALU.mult, op1=ALU.add))
                    dve.scalar_tensor_tensor(out=y[:, 0:n], in0=u[:, 0:n], scalar=cv[:, l, 0, bass.ds(f, 1)],
                                             in1=y[:, 0:n], op0=ALU.mult, op1=ALU.add).then_inc(S.conv, 1)
                    nxt = c + at + 3
                    if not last or nxt < fb + FCH:
                        ring.split_low(dve, nxt, t)
                    if p == 0 and not first:
                        down_evac(i - 1, c + 1, t)
                        ring.split_low(dve, c + 4, t)
                        ring.split_low(dve, c + 5, t)
                    if gate:
                        dve.wait_ge(S.silu, 2 * g + j + 1)
                        dve.tensor_tensor(Y[0][:, 0:n], Y[0][:, 0:n], Y[1][:, 0:n], ALU.mult).then_inc(S.prod, 1)
                        dve.wait_ge(S.act_high_f, 2 * g + j + 1)
                        dve.tensor_tensor(actl[:, j, 0:SEQ], Y[0][:, 0:SEQ], actr[:, j, 0:SEQ].bitcast(F32), ALU.subtract)
                        dve.tensor_tensor(actl[:, j, SEQ:TOK].rearrange("p (b q) -> p b q", b=NB), Y_s[0][:, :, 0:NS],
                                          actr[:, j, SEQ:TOK].bitcast(F32).rearrange("p (b q) -> p b q", b=NB),
                                          ALU.subtract).then_inc(S.act_low_f, 1)

            def down_evac(i, c, turns):
                for n in range(KT):
                    if n < KT - 1:
                        dve.wait_ge(S.d_ready, (KT - 1) * (NG * l + i) + n + 1)
                    else:
                        ring.done(dve, c + 1, turns)
                    if n >= 2:
                        dve.wait_ge(S.d_evac, KT * (NG * l + i) + n - 1)
                    residual(dve, ch, S, G, n, m, 3 * ((1 + n) % 2), rtmp[:, n % 2, :]).then_inc(S.d_evac, 1)

            body(0)
            start = ch.n
            with dve.Fori(1, NG - 1) as i:
                per = FFN_DVE_STEPS
                ch.base, ch.n = start + (i - 1) * per, 0
                body(i)
                assert ch.n == per, ch.n
            ch.base, ch.n = start + per * (NG - 2), 0
            body(NG - 1)
            down_evac(NG - 1, fb + FCH - 2, 0)


FFN_DVE_STEPS = 16


WIN = {"A": QB, "B": 1, "C": 4}
FIRST_TILE = {"A": 0, "B": 4, "C": 8}
CACHE_B = {"A": 4, "B": 1, "C": 4}
UNITS = QB + 2
KV_OF_C = 2


def kv(kind, T):
    return T if kind == "A" else 4 + (T - 4) // 2 if kind == "B" else T - KV_OF_C


def new_kv(kind, T):
    return kind != "B" or T % 2 == 0


def width(kind, u):
    return P * (min(u, WIN[kind]) + 1)


def first_key(kind, u):
    return P * max(0, u - WIN[kind])


def stream_width(kind):
    return P * (CACHE_B[kind] + 1)


def tile_steps(kind, fill, out, keys):
    steps = [("CQ",)]
    if keys:
        steps += [("CK",), ("VT",)]
    if out:
        steps += [("OUT",)]
    if keys:
        steps += [("KT",)]
    body = []
    for u in range(QB):
        body += [("S", u)] + ([("N", u - 1), ("O", u - 1)] if u else []) + [2, ("T", u), 1, ("V", u)]
    body += [("QZ", 0), ("N", QB - 1), ("O", QB - 1)]
    for g in range(2):
        u = QB + g
        body += [("K", g, 0), ("K", g, 1), 1, ("SK", g, 0), ("K", g, 2), ("SK", g, 1), ("K", g, 3), ("SK", g, 2), 1,
                 ("SK", g, 3), ("X", u), ("VI", g, 0), ("VI", g, 1)] + ([("QZ", 1)] if g == 0 else []) + \
                [2, ("T", u), 1, ("PV", g, 0), ("VI", g, 2), ("PV", g, 1), ("VI", g, 3), ("PV", g, 2), 1, ("PV", g, 3),
                 ("V", u), 1, ("N", u), ("O", u)]
    total = sum(s for s in body if isinstance(s, int))
    todo = [("F", name, k) for name in fill for k in range(KT)]
    seen = sent = 0
    turn = []
    for s in body:
        if not isinstance(s, int):
            steps.append(s)
            continue
        seen += s
        upto = -(-len(todo) * seen // total)
        if upto > sent:
            steps += turn
            turn = []
        steps += todo[sent:upto]
        turn += [("R", f[1]) for f in todo[sent:upto] if f[2] == KT - 1 and f[1] != "v"]
        sent = upto
    assert sent == len(todo)
    return steps + turn


def first_steps():
    f = {n: [("F", n, k) for k in range(KT)] for n in "qkv"}
    return f["q"] + f["k"] + [("R", "q")] + f["v"] + [("R", "k")]


def plan(kinds):
    tiles = [(k, T) for k in kinds for T in range(FIRST_TILE[k], FIRST_TILE[k] + {"A": 4, "B": 4, "C": 8}[k])]
    c = 3
    out = []
    for n, (k, T) in enumerate(tiles):
        fill = ""
        if n + 1 < len(tiles):
            fill = "qkv" if new_kv(*tiles[n + 1]) else "q"
        out.append((k, T, fill, c))
        c += len(fill) + (n > 0)
    return out, c + 1


AB_CHUNKS = plan("AB")[1]


def attention(nc, S, G, ins, outs, kinds):
    ctx = ExitStack()
    with ctx:
        def sb(name, shape, dt=F32):
            return ctx.enter_context(nc.sbuf_tensor(f"{name}_{kinds}", shape, dt))

        odd = kinds == "C"
        ring = Ring(nc, ctx, f"att{kinds}", 2, S.t_landed, S.t_high, S.t_low, S.t_used)
        F = {n: sb(f"f_{n}", [P, TOK]) for n in "qkv"}
        sw = sb("sw", [P, TOK])
        q, ql = sb("q", [P, TOK], F32R), sb("ql", [P, TOK], BF16)
        kk, kl = sb("k", [P, TOK], F32R), sb("kl", [P, TOK], BF16)
        v, vl = sb("v", [P, TOK], F32R), sb("vl", [P, TOK], BF16)
        E = sb("E", [P, 2048])
        W, Wl = sb("W", [P, 1280], F32R), sb("Wl", [P, 1280], BF16)
        actr, actl = sb("actr", [P, TOK], F32R), sb("actl", [P, TOK], BF16)
        raw = [sb(f"raw{s}", [P, 4, P]) for s in range(2)]
        kc = [sb(f"kc{s}", [P, 512], F32R) for s in range(2)]
        kcl = [sb(f"kcl{s}", [P, 512], BF16) for s in range(2)]
        Qz, Qzl = sb("Qz", [P, 5, P], F32R), sb("Qzl", [P, 5, P], BF16)
        osb, osb2 = sb("osb", [P, P]), sb("osb2", [P, P])
        st = sb("st", [P, 16])
        mx, nm, sm, rc, coef = st[:, 0:2], st[:, 2:4], st[:, 4:6], st[:, 6:8], st[:, 8:9]
        ss, ms, rstd, es = st[:, 9:10], st[:, 10:11], st[:, 11:12], st[:, 12:14]
        if odd:
            bt, bs = sb("bt", [P, 2, 256]), sb("bs", [P, 144])
        else:
            rope = sb("rope", [P, 2, ROPE_N])
        ps, h, hl, K = G.psum, G.h, G.hl, G.consts
        ident = K[:, C_ID:C_ID + P]
        m = 2 if odd else 0
        a = m
        tiles, total = plan(kinds)
        cb = AB_CHUNKS if odd else 0
        assert cb % 2 == 0
        T0 = tiles[0][1]
        block = ctx.enter_context(nc.Block())
        pair = ps[:, 3:7, :].rearrange("p (s b) n -> p s (b n)", s=2)
        w_in = ins["w_in_odd" if odd else "w_in_even"][0].rearrange("(k p) n -> p k n", p=P)
        w_out = ins["w_out_odd" if odd else "w_out_even"][0]

        def un(T, u):
            return UNITS * T + u + 1

        def item(T, g, x):
            return 16 * T + 8 * g + x

        def turned_o(kind, T, u):
            return UNITS * T + u + 1 if kind == "A" else UNITS * 4 + QB * (T - 4) + u + 1

        def run(eng, do):
            do_steps(do, "A" if not odd else "C", T0 - 1, first_steps(), cb, 0)
            if not odd:
                for n, (kind, T, fill, c) in enumerate(tiles):
                    do_steps(do, kind, T, tile_steps(kind, fill, n > 0, new_kv(kind, T)), cb + c, 0)
            else:
                do_steps(do, "C", T0, tile_steps("C", "qkv", False, True), cb + 3, 0)
                with eng.Fori(T0 + 1, T0 + 7) as T:
                    do_steps(do, "C", T, tile_steps("C", "qkv", True, True), cb + 6, 2 * (T - T0 - 1), loop=True)
                do_steps(do, "C", T0 + 7, tile_steps("C", "", True, True), cb + 30, 0)

        def do_steps(do, kind, T, steps, c, turns, loop=False):
            if loop:
                do("LOOP", kind, T, (0,), c, turns)
            for s in steps:
                do(s[0], kind, T, s, c, turns)
                if s[0] == "OUT" or s[0] == "F" and s[2] == KT - 1:
                    c += 1
            if loop:
                do("END", kind, T, (0,), c, turns)

        def next_tile(kind, T):
            if not isinstance(T, int) or odd:
                return kind, T + 1
            return ("A" if T + 1 < 4 else "B"), T + 1

        def rope_no(kind, T, isq):
            n = kv(kind, T)
            if isq:
                return T + (n if new_kv(kind, T) else n + 1) + 1
            return T + n + 2

        def w_free(eng, kind, T, u):
            if u == 0:
                eng.wait_ge(S.item_used, 16 * T)
            elif u <= QB:
                eng.wait_ge(S.pv, QB * T + u)
            else:
                eng.wait_ge(S.item_used, item(T, 0, 7) + 1)

        def prob_views(kind, u):
            if u >= QB:
                n = 320 if kind == "A" else stream_width(kind)
                return [(lambda w: w[:, 0:n], pair[:, 0, 0:n])]
            n = width(kind, u)
            if kind == "A":
                return [(lambda w: w[:, 0:n], pair[:, 0, 0:n])]
            return [(lambda w: w[:, :].rearrange("p (z n) -> p z n", z=2)[:, :, 0:n], pair[:, :, 0:n])]

        @block.sync
        def _(sp):
            if not odd:
                sp.dma_start(rope[:, :, :], ins["rope"]).then_inc(S.rope_in, 16)

            twice = [0]

            def w_cols(name, kind, T):
                if kind == "A":
                    off = {"q": 0, "k": 512, "v": 1024}[name] + T * P
                elif kind == "B":
                    if name == "q":
                        off = 1536 + (T - 4) * P
                    else:
                        off = {"k": 2048, "v": 2176}[name] + (T - 4) // 2 * HD
                        return w_in[:, :, off:off + HD]
                else:
                    off = {"q": 0, "k": 1024, "v": 2048}[name] + (T - 8) * P
                return w_in[:, :, bass.ds(off, P)]

            def do(what, kind, T, s, c, turns):
                if what == "OUT":
                    row = (T - 1 - (8 if odd else 0)) * P
                    ring.load(sp, c, w_out[bass.ds(row, P), :], turns)
                elif what == "F" and s[2] == KT - 1:
                    nk, nT = next_tile(kind, T)
                    src = w_cols(s[1], nk, nT)
                    if nk == "B" and s[1] != "q":
                        sl, n = ring.at(c)
                        sp.wait_ge(ring.low[sl], n)
                        both = ring.raw[sl][:, :].rearrange("p (k z n) -> p k z n", k=KT, z=2)
                        sp.dma_start(both[:, :, 0, :], src).then_inc(S.dup_in, 16)
                        twice[0] += 1
                        sp.wait_ge(S.dup_in, 16 * twice[0])
                        sp.dma_start(both[:, :, 1, :], src).then_inc(ring.landed[sl], 16)
                    else:
                        ring.load(sp, c, src, turns, ("p (k n) -> p k n", dict(k=KT)))

            run(sp, do)
            ring.load(sp, cb + total - 1, w_out[7 * P:8 * P, :])

        @block.gpsimd
        def _(pool):
            pool.memset(Qz[:, :, :].bitcast(F32), 0.0).then_inc(S.qz_zero, 1)
            pool.memset(Qzl[:, :, :], 0.0).then_inc(S.qz_zero, 1)
            pool.wait_ge(S.qz_zero, 4 if odd else 2)
            settle(pool, S)

            def cached(kind, T, m_, slot, cache, b):
                if kind == "A":
                    return ins[f"cache_a_{cache}"][0, b, :, T, :].rearrange("(j p) d -> p j d", p=P)
                if kind == "B":
                    src = ins[f"cache_b_{cache}"][0, b, :, (T - 4) // 2, :]
                    return bass.AP(src.tensor, src.offset, [[2 * HD, P], [0, 2], [1, HD]])
                return ins[f"cache_c_{cache}"][0, b].rearrange("(j p) h d -> p j (h d)", p=P)[
                    :, :, bass.ds((T - 8) * P, P)]

            def load_item(kind, T, g, x):
                it = item(T, g, x)
                slot = x % 2
                if not (isinstance(T, int) and T == 0 and g == 0 and x < 2):
                    pool.wait_ge(S.item_low, it - 1)
                    settle(pool, S)
                src = cached(kind, T, it, slot, "kv"[x // 4], 4 * g + x % 4)
                dst = raw[slot][:, 0, :].rearrange("p (z d) -> p z d", z=2) if kind == "B" else raw[slot][:, :, :]
                pool.dma_start(dst, src).then_inc(S.raw_in[slot], 16)

            def store(kind, T, which):
                n = kv(kind, T)
                rows = sw[:, :].rearrange("p (t d) -> p t d", d=P)
                pool.wait_ge(S.k_rows if which == "k" else S.v_rows, n + 1)
                settle(pool, S)
                if kind == "A":
                    dp = outs[f"a{which}_p"][0, 0, :, T, :].rearrange("(t p) d -> p t d", p=P)
                    ds_ = outs[f"a{which}_s"][0, :, :, T, :]
                    sp_, ss_ = rows[:, 0:QB, :], rows[:, QB, :]
                elif kind == "B":
                    hh = (T - 4) // 2
                    dp = outs[f"b{which}_p"][0, 0, :, hh, :]
                    ds_ = outs[f"b{which}_s"][0, :, P - NS:P, hh, :]
                    sp_, ss_ = rows[:, QB - 1, 0:HD], rows[:, QB, 0:HD]
                else:
                    cols = bass.ds((T - 8) * P, P)
                    dp = outs[f"c{which}_p"][0, 0].rearrange("(t p) h d -> p t (h d)", p=P)[:, :, cols]
                    ds_ = outs[f"c{which}_s"][0, :, PAST - NS:PAST].rearrange("b q h d -> b q (h d)")[:, :, cols]
                    sp_, ss_ = rows[:, 4:QB, :], rows[:, QB, :]
                pool.dma_start(dp, sp_).then_inc(S.stored, 16)
                pool.dma_start(ds_, ss_).then_inc(S.stored, 16)

            def load_bias(T):
                two = G.bias_dram[bass.ds((T - 8) * 2, 2), :, :]
                pool.dma_start(bt[:, :, :], two.rearrange("h i j -> i h j")).then_inc(S.bias_in, 16)
                for b in range(4):
                    pool.dma_start(bs[32 * b:32 * b + 32, :], two[:, 0:NS, 0:P + NS]).then_inc(S.bias_in, 16)

            def keep(T):
                if odd:
                    for w in "kv":
                        pool.dma_start(outs[f"c{w}_s"][0, bass.ds(T - 8, 1), 0:PAST - NS].rearrange("b q h d -> (b q) (h d)"),
                                       ins[f"cache_c_{w}"][0, bass.ds(T - 8, 1), NS:PAST].rearrange(
                                           "b q h d -> (b q) (h d)")).then_inc(S.kept, 16)
                else:
                    for w in "kv":
                        pool.dma_start(outs[f"b{w}_s"][0, T, 0:P - NS].rearrange("q h d -> q (h d)"),
                                       ins[f"cache_b_{w}"][0, T, NS:P].rearrange("q h d -> q (h d)")).then_inc(S.kept, 16)

            def do(what, kind, T, s, c, turns):
                if what == "CQ":
                    if odd:
                        if not (isinstance(T, int) and T == T0):
                            pool.wait_ge(S.nmax, un(T, 0) - 1)
                            settle(pool, S)
                        load_bias(T)
                elif what == "S" and s[1] == 0:
                    keep(T)
                elif what == "VT":
                    store(kind, T, "v")
                elif what == "KT":
                    store(kind, T, "k")
                elif what == "S" and s[1] == QB - 1:
                    load_item(kind, T, 0, 0)
                    load_item(kind, T, 0, 1)
                elif what == "K":
                    g, b = s[1:]
                    pool.wait_ge(S.item_low, item(T, g, b) + 1)
                    settle(pool, S)
                    load_item(kind, T, g, b + 2)
                elif what == "VI":
                    g, b = s[1:]
                    pool.wait_ge(S.item_low, item(T, g, 4 + b) + 1)
                    settle(pool, S)
                    if b < 2:
                        load_item(kind, T, g, b + 6)
                    elif g == 0:
                        load_item(kind, T, 1, b - 2)
                elif what == "QZ":
                    g = s[1]
                    pool.wait_ge(S.q_low, T + 1)
                    settle(pool, S)
                    if not (isinstance(T, int) and T == T0 and g == 0):
                        pool.wait_ge(S.stream_scores, 2 * T + g)
                        settle(pool, S)
                    if not odd:
                        pool.wait_ge(S.rstd, min(un(T, QB - 2 + g), 4 * UNITS))
                    for z in range(2):
                        r = slice(HD * z, HD * z + HD)
                        for dst, src in ((Qz, q), (Qzl, ql)):
                            s3 = src[r, SEQ + 64 * g:SEQ + 64 * g + 64].rearrange("p (b q) -> p b q", b=4)
                            flat = dst[r, :, :].rearrange("p c n -> p (c n)")
                            diag = flat[:, 0:4 * (P + 32)].rearrange("p (b x) -> p b x", b=4)[:, :, z * NS:z * NS + NS]
                            all_ = dst[r, 4, :].rearrange("p (b x) -> p b x", b=4)[:, :, z * NS:z * NS + NS]
                            if dst is Qz:
                                s3 = s3.bitcast(F32)
                            pool.tensor_copy(diag, s3)
                            last = pool.tensor_copy(all_, s3)
                    last.then_inc(S.qz, 1)
                elif what == "N" and kind == "A":
                    pool.wait_ge(S.ms, un(T, s[1]))
                    settle(pool, S)
                    if 2 * T + max(0, s[1] - QB + 2) > 0:
                        pool.wait_ge(S.qz, 2 * T + min(2, max(0, s[1] - QB + 2)))
                    pool.tensor_tensor(rstd, ms, G.mhalf[:, :], ALU.pow).then_inc(S.rstd, 1)
                elif what == "F" and s[2] == KT - 1 and s[1] != "v" and not odd:
                    nk, nT = next_tile(kind, T)
                    name = s[1]
                    n_kv = kv(nk, nT)
                    if name == "q":
                        pool.wait_ge(S.q_evac, nT + 1)
                        settle(pool, S)
                        if nT > 0:
                            prev = kv(kind, T) + 1
                            pool.wait_ge(S.stored, 64 * prev)
                            pool.wait_ge(S.roped, nT + (n_kv if new_kv(nk, nT) else n_kv + 1))
                            settle(pool, S)
                    else:
                        pool.wait_ge(S.k_evac, n_kv + 1)
                        pool.wait_ge(S.roped, nT + 1 + n_kv)
                        settle(pool, S)
                    for z in range(4):
                        y = z ^ 1
                        pool.dma_start(sw[32 * z:32 * z + 32, :], F[name][32 * y:32 * y + 32, :]).then_inc(S.swapped, 16)

            run(pool, do)
            pool.wait_ge(S.stored, 64 * (kv(*tiles[-1][:2]) + 1))
            pool.wait_ge(S.kept, 16 * 16 * (2 if odd else 1))
            settle(pool, S)

        @block.tensor
        def _(pe):
            norm_pe(pe, S, G, m, [F["q"], F["k"]])

            def do(what, kind, T, s, c, turns):
                n = kv(kind, T)
                first = isinstance(T, int) and T == T0
                if what == "F":
                    nk, nT = next_tile(kind, T)
                    name, k = s[1:]
                    w, wl = ring.ready(pe, c, turns) if k == 0 else (ring.w[c % 2][:, :], ring.wl[c % 2][:, :])
                    if k == 0:
                        if isinstance(T, int) and T == T0 - 1:
                            if name == "q":
                                pe.wait_ge(S.root, m + 1)
                            elif name == "k":
                                pe.wait_ge(S.q_evac, nT + 1)
                            else:
                                pe.wait_ge(S.k_evac, kv(nk, nT) + 1)
                        elif name == "q":
                            if first:
                                pe.wait_ge(S.v_rows, n + 1)
                            else:
                                pe.wait_ge(S.out_evac, KT * T)
                        elif name == "k":
                            pe.wait_ge(S.q_evac, nT + 1)
                        else:
                            pe.wait_ge(S.k_evac, kv(nk, nT) + 1)
                    if isinstance(T, int) and T == T0 - 1 and name == "q":
                        h_ready(pe, S, m, k)
                    for b, (lo, hi) in enumerate(COLS):
                        mm = mm3(pe, ps[:, b, 0:hi - lo], w[:, k * P:(k + 1) * P], wl[:, k * P:(k + 1) * P],
                                 h[:, k, lo:hi], hl[:, k, lo:hi], k == 0, k == KT - 1)
                    if k == KT - 1:
                        mm.then_inc(S.t_used[c % 2], 1)
                elif what == "VT":
                    pe.wait_ge(S.v_evac, n + 1)
                    for t in range(TB):
                        mm = pe.transpose(ps[:, t // 4, (t % 4) * P:(t % 4 + 1) * P], F["v"][:, t * P:(t + 1) * P], ident)
                    mm.then_inc(S.v_turned, 1)
                elif what == "KT":
                    if odd:
                        pe.wait_ge(S.k_evac, n + 1)
                    else:
                        pe.wait_ge(S.roped, T + n + 2)
                    if not first:
                        pe.wait_ge(S.out_evac, KT * T)
                    for t in range(TB):
                        mm = pe.transpose(ps[:, 3 + t // 4, (t % 4) * P:(t % 4 + 1) * P], F["k"][:, t * P:(t + 1) * P],
                                          ident)
                    mm.then_inc(S.k_turned, 1)
                elif what == "OUT":
                    out_tile(T - 1, c, turns)
                elif what == "S":
                    scores(kind, T, s[1], n)
                elif what == "K":
                    g, b = s[1:]
                    it = item(T, g, b)
                    pe.wait_ge(S.raw_in[b % 2], 16 * (8 * T + 4 * g + b // 2 + 1))
                    if not (isinstance(T, int) and T == 0 and g == 0 and b < 2):
                        pe.wait_ge(S.item_low, it - 1)
                    if g == 0 and b == 0:
                        pe.wait_ge(S.w_low, un(T, QB - 1))
                    for j in range(CACHE_B[kind]):
                        mm = pe.transpose(ps[:, 5 + b % 2, j * P:(j + 1) * P], raw[b % 2][:, j, :], ident)
                    mm.then_inc(S.kc_turned, 1)
                elif what == "SK":
                    g, b = s[1:]
                    nk = CACHE_B[kind] * P
                    it = item(T, g, b)
                    pe.wait_ge(S.item_low, it + 1)
                    if b == 0:
                        pe.wait_ge(S.qz, 2 * T + g + 1)
                        pe.wait_ge(S.w_low, un(T, QB + g - 1))
                    mm = mm3(pe, ps[:, 3, 0:nk], Qz[:, b, :], Qzl[:, b, :], kc[b % 2][:, 0:nk], kcl[b % 2][:, 0:nk],
                             b == 0, b == 3)
                    mm.then_inc(S.item_used, 1)
                    if b == 3:
                        new = pair[:, 0, nk:nk + P]
                        mm3(pe, new, Qz[:, 4, :], Qzl[:, 4, :], kk[:, SEQ:TOK], kl[:, SEQ:TOK], True, False)
                        pe.matmul(new, K[0:NB, C_MB + g * P:C_MB + (g + 1) * P], K[0:NB, C_RB:C_RB + P],
                                  start=False, stop=True, skip_group_check=True).then_inc(S.stream_scores, 1)
                elif what == "T":
                    u = s[1]
                    pe.wait_ge(S.probs, un(T, u))
                    if u >= QB and kind == "A":
                        for j in range(5):
                            mm = pe.matmul(ps[:, 3, 64 * j:64 * j + 64], E[:, j * P:(j + 1) * P], K[:, C_CA:C_CA + 64],
                                           start=(j == 0), stop=(j == 4), skip_group_check=True)
                    elif u >= QB:
                        for j in range(CACHE_B[kind] + 1):
                            mm = pe.transpose(pair[:, 0, j * P:(j + 1) * P], E[:, j * P:(j + 1) * P], ident)
                    elif kind == "A":
                        for j in range(u + 1):
                            mm = pe.transpose(pair[:, 0, j * P:(j + 1) * P], E[:, j * P:(j + 1) * P], ident)
                    else:
                        for z in range(2):
                            for j in range(width(kind, u) // P):
                                mm = pe.transpose(pair[:, z, j * P:(j + 1) * P], E[:, z * 640 + j * P:z * 640 + (j + 1) * P],
                                                  ident)
                    mm.then_inc(S.turned, 1)
                elif what == "V" and s[1] < QB:
                    u = s[1]
                    pe.wait_ge(S.w_low, un(T, u))
                    if u == 0:
                        pe.wait_ge(S.v_low, n + 1)
                    if not (first and u == 0):
                        o_bank_free(kind, T, u)
                    k0 = first_key(kind, u) // P
                    nb = width(kind, u) // P
                    for z in range(1 if kind == "A" else 2):
                        cols = slice(0, P) if kind == "A" else slice(HD * z, HD * z + HD)
                        for j in range(nb):
                            x = slice(z * 640 + j * P, z * 640 + (j + 1) * P)
                            y = slice((k0 + j) * P + cols.start, (k0 + j) * P + cols.stop)
                            mm = mm3(pe, ps[:, 7, cols], W[:, x], Wl[:, x], v[:, y], vl[:, y], j == 0, j == nb - 1)
                    mm.then_inc(S.pv, 1)
                elif what == "V" and kind == "A":
                    pe.wait_ge(S.od, 2 * T + s[1] - QB + 1)
                    pe.transpose(ps[0:64, 7, P:2 * P], E[:, 1024:1024 + 64], ident).then_inc(S.od_turned, 1)
                elif what == "PV":
                    g, b = s[1:]
                    it = item(T, g, 4 + b)
                    rows = NS if kind == "A" else 2 * NS
                    all_ = 4 * rows
                    nc_ = CACHE_B[kind]
                    if b == 0:
                        pe.wait_ge(S.w_low, un(T, QB + g))
                        o_bank_free(kind, T, QB + g)
                        mm3(pe, ps[:, 7, 0:all_], v[:, QB * P:TOK], vl[:, QB * P:TOK], W[:, nc_ * all_:(nc_ + 1) * all_],
                            Wl[:, nc_ * all_:(nc_ + 1) * all_], True, False)
                    pe.wait_ge(S.item_low, it + 1)
                    for j in range(nc_):
                        x = slice(j * all_ + b * rows, j * all_ + (b + 1) * rows)
                        mm = mm3(pe, ps[:, 7, b * rows:(b + 1) * rows], kc[b % 2][:, j * P:(j + 1) * P],
                                 kcl[b % 2][:, j * P:(j + 1) * P], W[:, x], Wl[:, x], False, b == 3 and j == nc_ - 1)
                    mm.then_inc(S.item_used, 1)
                elif what == "O" and (s[1] < QB or kind == "A"):
                    u = s[1]
                    rows = P if u < QB else 64
                    pe.wait_ge(S.o_rows, turned_o(kind, T, u))
                    pe.transpose(ps[:, 7, 256:256 + rows], (osb2 if kind == "A" else osb)[0:rows, :],
                                 ident[0:rows, 0:rows]).then_inc(S.o_turned, 1)

            def o_bank_free(kind, T, u):
                pe.wait_ge(S.act_low, un(T, u) - 1)

            def out_tile(T, c, turns):
                w, wl = ring.ready(pe, c, turns)
                pe.wait_ge(S.act_low, un(T, UNITS - 1))
                pe.wait_ge(S.v_rows, v_rows_before_out(T))
                for n in range(KT):
                    if n >= 2:
                        pe.wait_ge(S.out_evac, KT * T + n - 1)
                    elif n == 1:
                        pe.wait_ge(S.item_low, item(T, 1, 3) + 1)
                    acc = 3 * (n % 2)
                    for b, (lo, hi) in enumerate(COLS):
                        mm = mm3(pe, ps[:, acc + b, 0:hi - lo], w[:, n * P:(n + 1) * P], wl[:, n * P:(n + 1) * P],
                                 actr[:, lo:hi], actl[:, lo:hi], True, True)
                    if n < KT - 1:
                        mm.then_inc(S.out_ready, 1)
                mm.then_inc(S.t_used[c % 2], 1)

            def v_rows_before_out(T):
                if odd:
                    return T + 1 - KV_OF_C + 1 if not (isinstance(T, int) and T == 15) else 14
                return min(kv(*next_tile("A", T)), 5) + 1

            def scores(kind, T, u, n):
                if u == 0:
                    pe.wait_ge(S.q_low, T + 1)
                    pe.wait_ge(S.k_low, n + 1)
                    pe.wait_ge(S.k_rows, n + 1)
                    if not (isinstance(T, int) and T == T0):
                        pe.wait_ge(S.out_evac, KT * T)
                else:
                    pe.wait_ge(S.w_low, un(T, u - 1))
                k0, wd = first_key(kind, u), width(kind, u)
                qs = slice(u * P, (u + 1) * P)
                for z in range(2):
                    r = slice(HD * z, HD * z + HD)
                    for lo in range(0, wd, 512):
                        hi = min(lo + 512, wd)
                        dst = pair[:, z, lo:hi]
                        diag = hi == wd
                        early = kind != "A" and u >= WIN[kind] and lo == 0
                        mm = mm3(pe, dst, q[r, qs], ql[r, qs], kk[r, k0 + lo:k0 + hi], kl[r, k0 + lo:k0 + hi],
                                 True, not diag and not early)
                        if diag:
                            mm = pe.matmul(pair[:, z, wd - CHUNK:wd], K[0:1, C_L:C_L + P], K[0:1, C_R:C_R + CHUNK],
                                           start=False, stop=not early, skip_group_check=True)
                        if early:
                            mm = pe.matmul(pair[:, z, 0:CHUNK], K[0:1, C_L + P:C_L + 2 * P], K[0:1, C_R:C_R + CHUNK],
                                           start=False, stop=True, skip_group_check=True)
                mm.then_inc(S.scores, 1)

            run(pe, do)
            out_tile(T0 + 7, cb + total - 1, 0)

        @block.scalar
        def _(act):
            norm_act(act, S, G, m, [F["q"], F["k"]], F["v"])
            for c in range(2):
                ring.split_high(act, cb + c)
            mod_act(act, S, G, m, a, [F["q"], F["k"]], sw)
            act.wait_ge(S.hp_low, KT * (m + 1))
            ch = Chain(act, S.act_step[m // 2])
            acc0 = ps[:, 0:3, :].rearrange("p b n -> p (b n)")[:, 0:TOK]
            acc1 = ps[:, 3:6, :].rearrange("p b n -> p (b n)")[:, 0:TOK]
            start = [0]

            def split(c, turns):
                if c + 2 < cb + total or not isinstance(turns, int):
                    ring.split_high(act, c + 2, turns)

            def do(what, kind, T, s, c, turns):
                n = kv(kind, T)
                first = isinstance(T, int) and T == T0
                if what == "LOOP":
                    start[0] = ch.n
                    ch.base, ch.n = start[0] + (T - T0 - 1) * C_ACT_STEPS, 0
                elif what == "END":
                    assert ch.n == C_ACT_STEPS, ("C_ACT_STEPS", ch.n)
                    ch.base, ch.n = start[0] + 6 * C_ACT_STEPS, 0
                elif what == "F" and s[2] == KT - 1:
                    nk, nT = next_tile(kind, T)
                    name = s[1]
                    ring.done(act, c, turns)
                    if not (isinstance(T, int) and T == T0 - 1):
                        if name == "q":
                            act.wait_ge(S.q_low, T + 1)
                        elif name == "k":
                            act.wait_ge(S.k_low, n + 1)
                            act.wait_ge(S.k_turned, n + 1)
                        else:
                            act.wait_ge(S.v_turned, n + 1)
                    act.copy(F[name][:, :], acc0).then_inc({"q": S.q_evac, "k": S.k_evac, "v": S.v_evac}[name], 1)
                    split(c, turns)
                elif what == "OUT":
                    ring.done(act, c, turns)
                    split(c, turns)
                elif what in ("CQ", "CK"):
                    isq = what == "CQ"
                    src, dst = (F["q"], q) if isq else (F["k"], kk)
                    if odd:
                        act.wait_ge(S.q_evac if isq else S.k_evac, (T if isq else n) + 1)
                    else:
                        act.wait_ge(S.roped, rope_no(kind, T, isq))
                    if not first:
                        act.wait_ge(S.stream_scores, 2 * T)
                    act.copy(dst[:, :], src[:, :]).then_inc(S.q_high if isq else S.k_high, 1)
                elif what == "VT":
                    act.wait_ge(S.v_turned, n + 1)
                    if n_before(n):
                        act.wait_ge(S.stored, 64 * n)
                        act.wait_ge(S.pv, QB * T)
                        act.wait_ge(S.item_used, 16 * T)
                    if not odd:
                        act.wait_ge(S.roped, rope_no(kind, T, False))
                    act.copy(sw[:, :], acc0).then_inc(S.v_rows, 1)
                    act.wait_ge(S.v_rows, n + 1)
                    act.copy(v[:, :], sw[:, :]).then_inc(S.v_high, 1)
                elif what == "KT":
                    act.wait_ge(S.k_turned, n + 1)
                    act.wait_ge(S.stored, 64 * n + 32)
                    act.wait_ge(S.v_low, n + 1)
                    act.copy(sw[:, :], acc1).then_inc(S.k_rows, 1)
                elif what == "S":
                    softmax(kind, T, s[1], width(kind, s[1]), 2)
                elif what == "X":
                    softmax(kind, T, s[1], stream_width(kind), 1)
                elif what == "T":
                    u = s[1]
                    act.wait_ge(S.turned, un(T, u))
                    if not (first and u == 0):
                        w_free(act, kind, T, u)
                    for dst, src in prob_views(kind, u):
                        i_ = act.copy(dst(W), src)
                    i_.then_inc(S.w_high, 1)
                elif what == "K":
                    g, b = s[1:]
                    it = item(T, g, b)
                    nk = CACHE_B[kind] * P
                    act.wait_ge(S.kc_turned, 8 * T + 4 * g + b + 1)
                    if not (isinstance(T, int) and T == 0 and g == 0 and b < 2):
                        act.wait_ge(S.item_used, it - 1)
                    act.copy(kc[b % 2][:, 0:nk], ps[:, 5 + b % 2, 0:nk]).then_inc(S.item_high, 1)
                elif what == "VI":
                    g, b = s[1:]
                    it = item(T, g, 4 + b)
                    nk = CACHE_B[kind]
                    act.wait_ge(S.raw_in[b % 2], 16 * (8 * T + 4 * g + 2 + b // 2 + 1))
                    act.wait_ge(S.item_used, it - 1)
                    act.copy(kc[b % 2][:, 0:nk * P], raw[b % 2][:, 0:nk, :].rearrange("p j d -> p (j d)")).then_inc(
                        S.item_high, 1)
                elif what == "V":
                    outputs(kind, T, s[1])
                elif what == "N" and kind == "A":
                    u = s[1]
                    rows = P if u < QB else 64
                    act.wait_ge(S.rstd, un(T, u))
                    act.activation(osb2[0:rows, :], osb[0:rows, :], ACT.Copy, scale=rstd[0:rows, :]).then_inc(S.o_rows, 1)
                elif what == "O" and (s[1] < QB or kind == "A"):
                    u = s[1]
                    rows = P if u < QB else 64
                    act.wait_ge(S.o_turned, turned_o(kind, T, u))
                    if u == 0 and not first:
                        act_free(T, c, turns)
                    lo = u * P if u < QB else SEQ + 64 * (u - QB)
                    act.activation(actr[:, lo:lo + rows], ps[:, 7, 256:256 + rows], ACT.Copy,
                                   scale=G.gsub[:, 0:1] if kind == "A" else 1.0).then_inc(S.act_high, 1)

            def n_before(n):
                return not (isinstance(n, int) and n == (6 if odd else 0))

            def act_free(T, c, turns):
                act.wait_ge(S.out_evac, KT * T)

            def softmax(kind, T, u, wd, comps):
                act.wait_ge(S.nmax, un(T, u))
                if not (isinstance(T, int) and T == T0 and u == 0):
                    act.wait_ge(S.turned, un(T, u) - 1)
                for z in range(comps):
                    off = z * (1024 if kind == "A" else 640)
                    i_ = act.activation(E[:, off:off + wd], pair[:, z, 0:wd], ACT.Exp, bias=nm[:, z:z + 1], scale=SCALE,
                                        accum_out=sm[:, z:z + 1])
                    if kind == "B":
                        sink = G.sinkp[:, 2 * (T - 4) + z:2 * (T - 4) + z + 1] if comps == 2 else \
                            G.sinks_s[:, T - 4:T - 3]
                        i_ = act.activation(es[:, z:z + 1], sink, ACT.Exp, bias=nm[:, z:z + 1], scale=1.0)
                i_.then_inc(S.exps, 1)

            def outputs(kind, T, u):
                if u < QB:
                    act.wait_ge(S.pv, QB * T + u + 1)
                    if kind == "A":
                        ch.then(act.activation(osb[:, :], ps[:, 7, 0:P], ACT.Copy, scale=rc[:, 0:1]))
                    else:
                        act.activation(osb[:, 0:HD], ps[:, 7, 0:HD], ACT.Copy, scale=rc[:, 0:1])
                        act.activation(osb[:, HD:P], ps[:, 7, HD:P], ACT.Copy, scale=rc[:, 1:2]).then_inc(S.o_rows, 1)
                    rows = P
                else:
                    g = u - QB
                    act.wait_ge(S.item_used, item(T, g, 7) + 1)
                    if kind == "A":
                        act.copy(E[:, 1024:1024 + 64], ps[:, 7, 0:64]).then_inc(S.od, 1)
                        act.wait_ge(S.od_turned, 2 * T + g + 1)
                        ch.then(act.copy(osb[0:64, :], ps[0:64, 7, P:2 * P]))
                    else:
                        for z in range(2):
                            r = slice(HD * z, HD * z + HD)
                            src = ps[r, 7, 0:P].rearrange("p (b x) -> p b x", b=4)[:, :, z * NS:z * NS + NS]
                            i_ = act.copy(actr[r, SEQ + 64 * g:SEQ + 64 * g + 64].rearrange("p (b q) -> p b q", b=4), src)
                        i_.then_inc(S.act_high, 1)
                    rows = 64
                if kind == "A":
                    act.activation(osb2[0:rows, :], osb[0:rows, :], ACT.Square,
                                   accum_out=ss[0:rows, :]).then_inc(S.squares, 1)

            run(act, do)

        @block.vector
        def _(dve):
            ch = Chain(dve, S.dve_step[m])
            for c in range(2):
                ring.split_low(dve, cb + c)
            mod_dve(dve, ch, S, G, m, a, [F["q"], F["k"]], F["v"], sw)
            start = [0]
            def split(c, turns):
                if c + 2 < cb + total or not isinstance(turns, int):
                    ring.split_low(dve, c + 2, turns)

            def do(what, kind, T, s, c, turns):
                n = kv(kind, T)
                first = isinstance(T, int) and T == T0
                if what == "LOOP":
                    start[0] = ch.n
                    ch.base, ch.n = start[0] + (T - T0 - 1) * C_DVE_STEPS, 0
                elif what == "END":
                    assert ch.n == C_DVE_STEPS, ("C_DVE_STEPS", ch.n)
                    ch.base, ch.n = start[0] + 6 * C_DVE_STEPS, 0
                elif what == "F" and s[2] == KT - 1:
                    nk, nT = next_tile(kind, T)
                    split(c, turns)
                elif what == "R" and not odd:
                    rotate(s[1], *next_tile(kind, T))
                elif what == "OUT":
                    out_evac(T - 1, c, turns)
                    split(c, turns)
                elif what == "CQ":
                    dve.wait_ge(S.q_high, T + 1)
                    dve.tensor_tensor(ql[:, :], F["q"][:, :], q[:, :].bitcast(F32), ALU.subtract).then_inc(S.q_low, 1)
                elif what == "CK":
                    dve.wait_ge(S.k_high, n + 1)
                    dve.tensor_tensor(kl[:, :], F["k"][:, :], kk[:, :].bitcast(F32), ALU.subtract).then_inc(S.k_low, 1)
                elif what == "VT":
                    dve.wait_ge(S.v_high, n + 1)
                    dve.tensor_tensor(vl[:, :], sw[:, :], v[:, :].bitcast(F32), ALU.subtract).then_inc(S.v_low, 1)
                elif what == "S":
                    maxima(kind, T, s[1], width(kind, s[1]), 2)
                elif what == "X":
                    maxima(kind, T, s[1], stream_width(kind), 1)
                elif what == "T":
                    u = s[1]
                    factors(kind, T, u)
                    dve.wait_ge(S.w_high, un(T, u))
                    for dst, src in prob_views(kind, u):
                        i_ = dve.tensor_tensor(dst(Wl), src, dst(W).bitcast(F32), ALU.subtract)
                    i_.then_inc(S.w_low, 1)
                elif what in ("K", "VI"):
                    g, b = s[1:]
                    it = item(T, g, b + (4 if what == "VI" else 0))
                    nk = CACHE_B[kind] * P
                    dve.wait_ge(S.item_high, it + 1)
                    src = ps[:, 5 + b % 2, 0:nk] if what == "K" else \
                        raw[b % 2][:, 0:CACHE_B[kind], :].rearrange("p j d -> p (j d)")
                    dve.tensor_tensor(kcl[b % 2][:, 0:nk], src, kc[b % 2][:, 0:nk].bitcast(F32),
                                      ALU.subtract).then_inc(S.item_low, 1)
                elif what == "V" and kind == "A":
                    u = s[1]
                    rows = P if u < QB else 64
                    dve.wait_ge(S.squares, un(T, u))
                    dve.tensor_scalar(ms[0:rows, :], ss[0:rows, :], 1.0 / P, EPS, ALU.mult, ALU.add).then_inc(S.ms, 1)
                elif what == "O":
                    u = s[1]
                    dve.wait_ge(S.act_high, un(T, u))
                    if u < QB or kind == "A":
                        rows = P if u < QB else 64
                        lo = u * P if u < QB else SEQ + 64 * (u - QB)
                        dst, src, hi = actl[:, lo:lo + rows], ps[:, 7, 256:256 + rows], actr[:, lo:lo + rows].bitcast(F32)
                        if kind == "A":
                            i_ = dve.scalar_tensor_tensor(out=dst, in0=src, scalar=G.gsub[:, 0:1], in1=hi, op0=ALU.mult,
                                                          op1=ALU.subtract)
                        else:
                            i_ = dve.tensor_tensor(dst, src, hi, ALU.subtract)
                    else:
                        g = u - QB
                        cs = slice(SEQ + 64 * g, SEQ + 64 * g + 64)
                        for z in range(2):
                            r = slice(HD * z, HD * z + HD)
                            src = ps[r, 7, 0:P].rearrange("p (b x) -> p b x", b=4)[:, :, z * NS:z * NS + NS]
                            i_ = dve.tensor_tensor(actl[r, cs].rearrange("p (b q) -> p b q", b=4), src,
                                                   actr[r, cs].bitcast(F32).rearrange("p (b q) -> p b q", b=4), ALU.subtract)
                    i_.then_inc(S.act_low, 1)

            def rotate(name, nk, nT):
                f = F[name]
                no = rope_no(nk, nT, name == "q")
                if nT == 0 and name == "q":
                    dve.wait_ge(S.rope_in, 16)
                dve.wait_ge(S.swapped, 64 * no)
                for x, j in ((f, 0), (sw, 1)):
                    dve.tensor_tensor(x[:, 0:SEQ], x[:, 0:SEQ], rope[:, j, 0:SEQ], ALU.mult)
                    x3 = x[:, SEQ:TOK].rearrange("p (b q) -> p b q", b=NB)
                    i_ = dve.tensor_tensor(x3, x3, rope[:, j, SEQ:ROPE_N].unsqueeze(1).broadcast_to([P, NB, NS]), ALU.mult)
                ch.then(i_)
                dve.tensor_tensor(f[:, :], f[:, :], sw[:, :], ALU.add).then_inc(S.roped, 1)

            def maxima(kind, T, u, wd, comps):
                if comps == 2:
                    dve.wait_ge(S.scores, QB * T + u + 1)
                else:
                    dve.wait_ge(S.stream_scores, 2 * T + u - QB + 1)
                if kind == "C":
                    if comps == 2:
                        if u == 0:
                            dve.wait_ge(S.bias_in, bias_no(T))
                        n = min(wd, 256)
                        x = pair[:, :, wd - n:wd]
                        ch.then(dve.tensor_tensor(x, x, bt[:, :, 256 - n:256], ALU.add))
                    else:
                        x = pair[:, 0, 384:512]
                        dve.tensor_tensor(x, x, bs[:, 0:P], ALU.add)
                        x = pair[:, 0, 512:640].rearrange("p (b q) -> p b q", b=NB)
                        ch.then(dve.tensor_tensor(x, x, bs[:, P:P + NS].unsqueeze(1).broadcast_to([P, NB, NS]), ALU.add))
                if comps == 2:
                    ch.then(dve.tensor_reduce(mx, pair[:, :, 0:wd], AX.X, ALU.max))
                else:
                    ch.then(dve.tensor_reduce(mx[:, 0:1], pair[:, 0, 0:wd], AX.X, ALU.max))
                if kind == "B":
                    sink = G.sinkp[:, 2 * (T - 4):2 * (T - 4) + 2] if comps == 2 else G.sinks_s[:, T - 4:T - 3]
                    ch.then(dve.scalar_tensor_tensor(out=mx[:, 0:comps], in0=mx[:, 0:comps], scalar=SCALE, in1=sink,
                                                     op0=ALU.mult, op1=ALU.max))
                dve.tensor_scalar(nm[:, 0:comps], mx[:, 0:comps], -1.0 if kind == "B" else -SCALE, None,
                                  ALU.mult).then_inc(S.nmax, 1)

            def factors(kind, T, u):
                dve.wait_ge(S.exps, un(T, u))
                z = 2 if u < QB else 1
                if kind == "B":
                    ch.then(dve.tensor_tensor(sm[:, 0:z], sm[:, 0:z], es[:, 0:z], ALU.add))
                if kind != "A" and u < QB:
                    dve.reciprocal(rc, sm).then_inc(S.probs, 1)
                    return
                ch.then(dve.reciprocal(rc[:, 0:z], sm[:, 0:z]))
                if u < QB:
                    ch.then(dve.scalar_tensor_tensor(out=coef, in0=rc[:, 1:2], scalar=sm[:, 0:1], in1=G.nlam[:, 0:1],
                                                     op0=ALU.mult, op1=ALU.mult))
                    wd = width(kind, u)
                    dve.scalar_tensor_tensor(out=E[:, 0:wd], in0=E[:, 1024:1024 + wd], scalar=coef, in1=E[:, 0:wd],
                                             op0=ALU.mult, op1=ALU.add).then_inc(S.probs, 1)
                else:
                    wd = stream_width(kind)
                    dve.tensor_scalar(E[:, 0:wd], E[:, 0:wd], rc[:, 0:1], G.cfac[:, 0:1] if kind == "A" else None,
                                      ALU.mult, ALU.mult if kind == "A" else ALU.bypass).then_inc(S.probs, 1)

            def bias_no(T):
                return 16 * BIAS_DMAS * (T - T0 + 1)

            def out_evac(T, c, turns):
                for n in range(KT):
                    if n < KT - 1:
                        dve.wait_ge(S.out_ready, (KT - 1) * T + n + 1)
                    else:
                        ring.done(dve, c, turns)
                    if n >= 2:
                        dve.wait_ge(S.out_evac, KT * T + n - 1)
                    residual(dve, ch, S, G, n, a, 3 * (n % 2), rtmp[n % 2]).then_inc(S.out_evac, 1)

            rtmp = E[:, 1792:1792 + TS], E[:, 1792 + TS:2048]
            run(dve, do)
            out_evac(T0 + 7, cb + total - 1, 0)


BIAS_DMAS = 5
C_ACT_STEPS = 0
C_DVE_STEPS = 30


def finish(nc, S, G, outs):
    ctx = ExitStack()
    with ctx:
        def sb(name, shape, dt=F32):
            return ctx.enter_context(nc.sbuf_tensor(name, shape, dt))

        sq = [sb(f"fin_sq{j}", [P, TOK]) for j in range(2)]
        rs = sb("fin_rs", [P, TOK])
        rows = [sb(f"fin_rows{j}", [P, D]) for j in range(3)]
        ps, xT = G.psum, G.xT
        ident = G.consts[:, C_ID:C_ID + P]
        block = ctx.enter_context(nc.Block())

        @block.tensor
        def _(pe):
            norm_pe(pe, S, G, 4, sq)
            pe.wait_ge(S.root, 5)
            for t in range(TB):
                if t == 0:
                    pe.wait_ge(S.fin_scaled, KT)
                if t >= 4:
                    pe.wait_ge(S.fin_rows, t - 3)
                for k in range(KT):
                    mm = pe.transpose(ps[:, 2 * (t % 4) + k // 4, (k % 4) * P:(k % 4 + 1) * P],
                                      xT[:, k, t * P:(t + 1) * P], ident)
                mm.then_inc(S.fin_turned, 1)

        @block.scalar
        def _(act):
            norm_act(act, S, G, 4, sq, rs)
            for t in range(TB):
                act.wait_ge(S.fin_turned, t + 1)
                if t >= 3:
                    act.wait_ge(S.fin_out[t % 3], 16 * (t // 3))
                act.copy(rows[t % 3][:, :], ps[:, 2 * (t % 4):2 * (t % 4) + 2, :].rearrange("p b n -> p (b n)")).then_inc(
                    S.fin_rows, 1)

        @block.vector
        def _(dve):
            dve.wait_ge(S.root, 5)
            dve.reciprocal(rs[:, :], rs[:, :]).then_inc(S.dve_step[4], 1)
            dve.wait_ge(S.dve_step[4], 1)
            for k in range(KT):
                dve.scalar_tensor_tensor(out=xT[:, k, :], in0=xT[:, k, :], scalar=G.gT[:, 32 + k:33 + k], in1=rs[:, :],
                                         op0=ALU.mult, op1=ALU.mult).then_inc(S.fin_scaled, 1)

        @block.sync
        def _(sp):
            y = outs["y_s"].rearrange("b q d -> (b q) d")
            for t in range(TB):
                sp.wait_ge(S.fin_rows, t + 1)
                dst = outs["y_p"][0, t * P:(t + 1) * P, :] if t < QB else y
                sp.dma_start(dst, rows[t % 3][:, :]).then_inc(S.fin_out[t % 3], 16)
            for j in range(3):
                sp.wait_ge(S.fin_out[j], 48)


class Semaphores:

    def __init__(self, nc, ctx):
        def make(names):
            return [ctx.enter_context(nc.semaphore(n)) for n in names.split()]

        def several(name, n):
            return [ctx.enter_context(nc.semaphore(f"{name}{j}")) for j in range(n)]

        (self.settled, self.const_in, self.c_in, self.vec_in, self.lam_in, self.tab_in, self.sink_in, self.rev_made) = make(
            "settled const_in c_in vec_in lam_in tab_in sink_in rev_made")
        (self.rev_out, self.set_ones, self.set_zero, self.adab_in, self.csil, self.lam_dot, self.lam_exp) = make(
            "rev_out set_ones set_zero adab_in csil lam_dot lam_exp")
        (self.cT_ready, self.c_high, self.c_low, self.x_turned, self.x_evac, self.ada_evac, self.small_ready, self.small_evac) = make(
            "cT_ready c_high c_low x_turned x_evac ada_evac small_ready small_evac")
        (self.mod_mm, self.mod_evac, self.set_step) = make(
            "mod_mm mod_evac set_step")
        (self.sq_ready, self.sq_used, self.root, self.hs_ready, self.hs_high, self.hs_low, self.hp_ready, self.hp_high) = make(
            "sq_ready sq_used root hs_ready hs_high hs_low hp_ready hp_high")
        (self.hp_low,) = make(
            "hp_low")
        (self.st_in, self.st_turned, self.st_evac, self.pads, self.u_evac, self.u_last, self.u_zero, self.so_turned) = make(
            "st_in st_turned st_evac pads u_evac u_last u_zero so_turned")
        (self.so_evac, self.so_out, self.so_free, self.conv, self.silu, self.prod, self.act_high_f, self.act_low_f) = make(
            "so_evac so_out so_free conv silu prod act_high_f act_low_f")
        (self.d_ready, self.d_evac) = make(
            "d_ready d_evac")
        (self.rope_in, self.dup_in, self.qz_zero, self.q_evac, self.k_evac, self.v_evac, self.q_high, self.q_low) = make(
            "rope_in dup_in qz_zero q_evac k_evac v_evac q_high q_low")
        (self.k_high, self.k_low, self.v_high, self.v_low, self.v_rows, self.k_rows, self.v_turned, self.k_turned) = make(
            "k_high k_low v_high v_low v_rows k_rows v_turned k_turned")
        (self.stored,) = make(
            "stored")
        (self.swapped, self.roped, self.bias_in, self.kept, self.kc_turned, self.item_high, self.item_low, self.item_used) = make(
            "swapped roped bias_in kept kc_turned item_high item_low item_used")
        (self.qz, self.scores, self.stream_scores, self.nmax, self.exps, self.probs, self.turned) = make(
            "qz scores stream_scores nmax exps probs turned")
        (self.w_high, self.w_low, self.pv, self.od, self.od_turned, self.squares, self.ms, self.rstd) = make(
            "w_high w_low pv od od_turned squares ms rstd")
        (self.o_rows, self.o_turned, self.act_high, self.act_low, self.out_ready, self.out_evac) = make(
            "o_rows o_turned act_high act_low out_ready out_evac")
        (self.fin_scaled, self.fin_turned, self.fin_rows) = make(
            "fin_scaled fin_turned fin_rows")
        self.f_landed = several("f_landed", 3)
        self.f_high = several("f_high", 3)
        self.f_low = several("f_low", 3)
        self.f_used = several("f_used", 3)
        self.t_landed = several("t_landed", 2)
        self.t_high = several("t_high", 2)
        self.t_low = several("t_low", 2)
        self.t_used = several("t_used", 2)
        self.raw_in = several("raw_in", 2)
        self.x_in = several("x_in", TB)
        self.dve_step = several("dve_step", 5)
        self.act_step = several("act_step", 2)
        self.fin_out = several("fin_out", 3)


class Shared:
    pass


def encoder(nc, ins, outs):
    ctx = ExitStack()
    with ctx:
        S, G = Semaphores(nc, ctx), Shared()

        def sb(name, shape, dt=F32):
            return ctx.enter_context(nc.sbuf_tensor(name, shape, dt))

        G.xT = sb("xT", [P, KT, TOK])
        G.mod = sb("mod", [P, 4, 24, NC9])
        G.gs = sb("gs", [P, 4, KT, NC9])
        G.gT = sb("gT", [P, 41])
        G.cvT = sb("cvT", [P, 2, 4, 2 * FT])
        G.consts = sb("consts", [P, C_N])
        G.ones = sb("ones", [P, P])
        G.eps, G.mhalf, G.nlam, G.cfac, G.gsub = (sb(n, [P, 1]) for n in ("eps", "mhalf", "nlam", "cfac", "gsub"))
        G.sinkp, G.sinks_s = sb("sinkp", [P, 8]), sb("sinks_s", [P, 4])
        G.psum = ctx.enter_context(nc.psum_tensor("psum", [P, 8, 512], F32))
        G.rev_dram = nc.dram_tensor("rev_dram", (16, 384), F32, kind="Internal").ap()
        G.bias_dram = nc.dram_tensor("bias_dram", (16, P, 256), F32, kind="Internal").ap()
        with ExitStack() as c:
            setup(nc, S, G, ins, c)
        G.h = sb("h", [P, KT, TOK], F32R)
        G.hl = sb("hl", [P, KT, TOK], BF16)
        attention(nc, S, G, ins, outs, "AB")
        ffn(nc, S, G, ins, outs, 0)
        attention(nc, S, G, ins, outs, "C")
        ffn(nc, S, G, ins, outs, 1)
        finish(nc, S, G, outs)


INS = ["x_prompt", "x_sample", "c_prompt", "c_sample", "cache_a_k", "cache_a_v", "cache_b_k", "cache_b_v",
       "cache_c_k", "cache_c_v", "state_conv", "ada_w", "ada_b", "norm_g", "final_g", "w_in_even", "w_out_even",
       "lam_q1", "lam_k1", "lam_q2", "lam_k2", "subln_g", "sinks", "w_in_odd", "w_out_odd", "rel_bias",
       "w_up", "conv_w", "conv_b", "w_down"]
OUTS = [("y_p", (1, SEQ, D)), ("y_s", (NB, NS, D)),
        ("ak_p", (1, 1, SEQ, 4, P)), ("av_p", (1, 1, SEQ, 4, P)), ("ak_s", (1, NB, NS, 4, P)), ("av_s", (1, NB, NS, 4, P)),
        ("bk_p", (1, 1, P, 2, HD)), ("bv_p", (1, 1, P, 2, HD)), ("bk_s", (1, NB, P, 2, HD)), ("bv_s", (1, NB, P, 2, HD)),
        ("ck_p", (1, 1, PAST, 16, HD)), ("cv_p", (1, 1, PAST, 16, HD)), ("ck_s", (1, NB, PAST, 16, HD)),
        ("cv_s", (1, NB, PAST, 16, HD)),
        ("conv_p", (2, 1, 2, 2 * DFF)), ("conv_s", (2, NB, 2, 2 * DFF))]


def kernel(**inputs):
    import numpy as _np
    import concourse.bacc as _bacc
    from concourse.bass_utils import run_bass_kernel_spmd as _run

    nc = _bacc.Bacc("TRN2", target_bir_lowering=False, num_devices=1)
    arrays, ins, outs = {}, {}, {}
    table, rope = shape_constants()
    given = {n: _np.ascontiguousarray(inputs[n]) for n in INS}
    given["consts"], given["rope"] = table, rope
    for name, arr in given.items():
        arrays[f"in_{name}"] = arr
        ins[name] = nc.dram_tensor(f"in_{name}", arr.shape, mybir.dt.from_np(arr.dtype), kind="ExternalInput").ap()
    for name, shape in OUTS:
        outs[name] = nc.dram_tensor(f"out_{name}", shape, F32, kind="ExternalOutput").ap()
    encoder(nc, ins, outs)
    r = _run(nc, [arrays], core_ids=[0])
    return tuple(r.results[0][f"out_{name}"] for name, _ in OUTS)
```

```python
from contextlib import ExitStack

import numpy as np
import concourse.bass as bass
from concourse import mybir
from concourse.alu_op_type import AluOpType as ALU

F32 = mybir.dt.float32
F32R = mybir.dt.float32r
BF16 = mybir.dt.bfloat16
ACT = mybir.ActivationFunctionType
AX = mybir.AxisListType

P = 128
D = 1024
KT = D // P
SEQ = 1024
NB = 8
NS = 16
TS = NB * NS
TOK = SEQ + TS
TB = TOK // P
QB = SEQ // P
PAST = 512
HD = 64
CHUNK = 64
DFF = 2816
FT = DFF // P
NC9 = 1 + NB
EPS = 1e-6
SCALE = HD ** -0.5
NEG = -1e30
LAM_INIT = 0.2
IN_EVEN = 2304
THETA = 10000.0
COLS = ((0, 512), (512, 1024), (1024, TOK))

C_ID = 0
C_CA = C_ID + P
C_ADA = C_CA + 64
C_L = C_ADA + 10
C_R = C_L + 2 * P
C_MB = C_R + CHUNK
C_RB = C_MB + 2 * P
C_SEL = C_RB + P
C_N = C_SEL + 2
ROPE_N = SEQ + NS


def shape_constants():
    c = np.zeros((P, C_N), np.float32)
    c[:, C_ID:C_ID + P] = np.eye(P)
    r = np.arange(P)
    c[r, C_CA + (r // 32) * NS + r % NS] = 1
    for b in range(NC9):
        c[b, C_ADA + b] = c[NC9 + b, C_ADA + b] = c[2 * NC9, C_ADA + b] = 1
    c[0, C_L:C_L + CHUNK] = 1
    c[0, C_L + P + CHUNK:C_L + 2 * P] = 1
    c[0, C_R:C_R + CHUNK] = NEG
    for b in range(NB):
        for g in range(2):
            c[b, C_MB + g * P:C_MB + (g + 1) * P] = (4 * g + r // 32) == b
        c[b, C_RB:C_RB + P] = np.where(r // NS == b, 0, NEG)
    c[:, C_SEL] = (r % 32) < NS
    c[:, C_SEL + 1] = (r % 32) >= NS
    half = HD // 2
    inv = np.float32(THETA) ** (-np.arange(half, dtype=np.float32) / np.float32(half))
    pos = np.concatenate([np.arange(SEQ), PAST + np.arange(NS)]).astype(np.float32)
    ang = inv[r % half][:, None] * pos[None, :]
    cos = np.cos(ang).astype(np.float32)
    sin = np.where((r % HD < half)[:, None], -np.sin(ang), np.sin(ang)).astype(np.float32)
    return c, np.ascontiguousarray(np.stack([cos, sin], 1))


def top(ap):
    return ap.bitcast(BF16)[:, 1::2]


def mm3(pe, out, w, wl, x, xl, start, stop):
    pe.matmul(out, w, x, start=start, stop=False, skip_group_check=True)
    pe.matmul(out, top(w), xl, start=False, stop=False, skip_group_check=True)
    return pe.matmul(out, wl, top(x), start=False, stop=stop, skip_group_check=True)


class Chain:

    def __init__(self, eng, sem, base=0):
        self.eng, self.sem, self.base, self.n = eng, sem, base, 0

    def then(self, ins):
        self.n += 1
        ins.then_inc(self.sem, 1)
        self.eng.wait_ge(self.sem, self.base + self.n)

    def mark(self, ins):
        self.n += 1
        ins.then_inc(self.sem, 1)
        return self.base + self.n

    def moved(self):
        return self.base + self.n


def settle(eng, S):
    eng.sem_inc(S.settled, 1)


class Ring:

    def __init__(self, nc, ctx, tag, size, landed, high, low, used, n=1024, raws=None, first=0):
        self.size, self.landed, self.high, self.low, self.used = size, landed, high, low, used
        self.raws, self.first = raws or size, first
        self.raw = [ctx.enter_context(nc.sbuf_tensor(f"{tag}_raw{s}", [P, n], F32)) for s in range(self.raws)]
        self.w = [ctx.enter_context(nc.sbuf_tensor(f"{tag}_high{s}", [P, n], F32R)) for s in range(size)]
        self.wl = [ctx.enter_context(nc.sbuf_tensor(f"{tag}_low{s}", [P, n], BF16)) for s in range(size)]

    def at(self, c, turns=0):
        return c % self.size, c // self.size + turns

    def load(self, eng, c, src, turns=0, view=None):
        s, n = self.at(c, turns)
        if c >= self.raws:
            eng.wait_ge(self.low[s], n + 1 - self.raws // self.size)
        dst = self.raw[c % self.raws][:, :]
        if view is not None:
            dst = dst.rearrange(view[0], **view[1])
        eng.dma_start(dst, src).then_inc(self.landed[c % self.raws], 16)

    def split_high(self, act, c, turns=0):
        s, n = self.at(c, turns)
        act.wait_ge(self.landed[c % self.raws], 16 * (c // self.raws + turns + 1 - self.first))
        if c >= self.size:
            act.wait_ge(self.used[s], n)
        act.copy(self.w[s][:, :], self.raw[c % self.raws][:, :]).then_inc(self.high[s], 1)

    def split_low(self, dve, c, turns=0):
        s, n = self.at(c, turns)
        dve.wait_ge(self.high[s], n + 1)
        dve.tensor_tensor(self.wl[s][:, :], self.raw[c % self.raws][:, :], self.w[s][:, :].bitcast(F32),
                          ALU.subtract).then_inc(self.low[s], 1)

    def done(self, eng, c, turns=0):
        s, n = self.at(c, turns)
        eng.wait_ge(self.used[s], n + 1)

    def ready(self, pe, c, turns=0):
        s, n = self.at(c, turns)
        pe.wait_ge(self.low[s], n + 1)
        return self.w[s][:, :], self.wl[s][:, :]


FBASE = 4 * 3 * (KT // 2)


def ada_chunk(a, j, k):
    return (3 * a + j) * (KT // 2) + k


def setup(nc, S, G, ins, ctx):
    def sb(name, shape, dt=F32):
        return ctx.enter_context(nc.sbuf_tensor(name, shape, dt))

    ring = Ring(nc, ctx, "ada", 3, S.ada_landed, S.f_high, S.f_low, S.f_used, 2 * D, raws=6)
    xrow = sb("xrow", [P, TB, D])
    crow = sb("crow", [NC9, D])
    csil = sb("csil", [NC9, D])
    cT = sb("cT", [P, KT * 10])
    cst = sb("cst", [P, KT, P], F32R)
    cb = sb("cb", [P, KT, P], BF16)
    msb = sb("msb", [32, 3 * D])
    vrow = sb("vrow", [64, P])
    crow2 = sb("crow2", [88, 4, P])
    lamv = sb("lamv", [P, 4, HD])
    lamp = sb("lamp", [P, 2, HD])
    lams = sb("lams", [P, 4])
    tab = sb("tab", [16, 257])
    rev = sb("rev", [16, 384])
    ps = G.psum
    xT, mod, gs, gT, cvT, K = G.xT, G.mod, G.gs, G.gT, G.cvT, G.consts
    ident = K[:, C_ID:C_ID + P]
    block = ctx.enter_context(nc.Block())
    ada_w = ins["ada_w"].rearrange("l s (c k p) (j n) -> (l s) j c p k n", p=P, j=3, k=2)
    ada_b = ins["ada_b"].rearrange("l s n -> (l s) n")

    @block.sync
    def _(sp):
        sp.dma_start(K[:, :], ins["consts"]).then_inc(S.const_in, 16)
        sp.dma_start(crow[0:1, :], ins["c_prompt"]).then_inc(S.c_in, 16)
        sp.dma_start(crow[1:NC9, :], ins["c_sample"]).then_inc(S.c_in, 16)
        sp.dma_start(vrow[0:32, :], ins["norm_g"].rearrange("l s (k p) -> (l s k) p", p=P)).then_inc(S.vec_in, 16)
        sp.dma_start(vrow[32:40, :], ins["final_g"].rearrange("(k p) -> k p", p=P)).then_inc(S.vec_in, 16)
        sp.dma_start(vrow[40:41, :], ins["subln_g"]).then_inc(S.vec_in, 16)
        for l in range(2):
            w = ins["conv_w"][l].rearrange("j (t p) -> (j t) p", p=P)
            b = ins["conv_b"][l].rearrange("(t p) -> t p", p=P)
            sp.dma_start(crow2[:, 2 * l, :], w[0:88, :]).then_inc(S.vec_in, 16)
            sp.dma_start(crow2[0:44, 2 * l + 1, :], w[88:132, :]).then_inc(S.vec_in, 16)
            sp.dma_start(crow2[44:88, 2 * l + 1, :], b).then_inc(S.vec_in, 16)
        for j, n in enumerate(("lam_q1", "lam_k1", "lam_q2", "lam_k2")):
            sp.dma_start(lamv[:, j, :], ins[n].broadcast_to([P, HD])).then_inc(S.lam_in, 16)
        sp.dma_start(tab[:, :], ins["rel_bias"][0]).then_inc(S.tab_in, 16)
        sp.dma_start(G.sinkp[:, :], ins["sinks"].broadcast_to([P, 8])).then_inc(S.sink_in, 16)
        for t in range(QB):
            sp.dma_start(xrow[:, t, :], ins["x_prompt"][0, t * P:(t + 1) * P, :]).then_inc(S.x_in[t], 16)
        sp.dma_start(xrow[:, QB, :], ins["x_sample"].rearrange("b t d -> (b t) d")).then_inc(S.x_in[QB], 16)
        for a in range(4):
            for j in range(3):
                for c in range(KT // 2):
                    ring.load(sp, ada_chunk(a, j, c), ada_w[a, j, c], view=("p (k n) -> p k n", dict(k=2)))
        sp.wait_ge(S.rev_made, 2)
        sp.dma_start(G.rev_dram, rev[:, :]).then_inc(S.rev_out, 16)
        sp.wait_ge(S.rev_out, 16)
        sp.dma_start(G.bias_dram, bass.AP(G.rev_dram.tensor, P - 1, [[384, 16], [-1, P], [1, 256]])).then_inc(S.rev_out, 16)
        sp.wait_ge(S.rev_out, 32)

    @block.gpsimd
    def _(pool):
        pool.memset(G.ones[:, :], 1.0).then_inc(S.set_ones, 1)
        pool.memset(G.eps[:, :], EPS).then_inc(S.set_ones, 1)
        pool.memset(cst[:, :, :].bitcast(F32), 0.0).then_inc(S.set_zero, 1)
        pool.memset(cb[:, :, :], 0.0).then_inc(S.set_zero, 1)
        pool.memset(rev[:, 0:P], 0.0).then_inc(S.rev_made, 1)
        pool.memset(G.mhalf[:, :], -0.5).then_inc(S.set_ones, 1)
        for a in range(4):
            if a:
                pool.wait_ge(S.mod_mm, a)
            pool.dma_start(msb[2 * NC9:2 * NC9 + 1, :], ada_b[a:a + 1, :]).then_inc(S.adab_in, 16)

    @block.scalar
    def _(act):
        act.wait_ge(S.c_in, 32)
        act.activation(csil[:, :], crow[:, :], ACT.Silu).then_inc(S.csil, 1)
        act.wait_ge(S.lam_dot, 2)
        act.activation(lams[:, 2:4], lams[:, 0:2], ACT.Exp).then_inc(S.lam_exp, 1)
        act.wait_ge(S.cT_ready, 1)
        act.wait_ge(S.set_zero, 1)
        act.copy(cst[:, :, 0:NC9], cT[:, :].rearrange("p (k c) -> p k c", k=KT)[:, :, 0:NC9]).then_inc(S.c_high, 1)
        for c in range(3):
            ring.split_high(act, c)
        for q in range(18):
            act.wait_ge(S.x_turned, q + 1)
            t, half = q // 2, q % 2
            act.copy(xT[:, 4 * half:4 * half + 4, t * P:(t + 1) * P],
                     ps[:, 6 - 2 * (q % 2), :].rearrange("p (k t) -> p k t", k=4)).then_inc(S.x_evac, 1)
        for a in range(4):
            for j in range(3):
                for k in range(KT // 2):
                    c = ada_chunk(a, j, k)
                    if c + 3 < FBASE:
                        ring.split_high(act, c + 3)
                last = ada_chunk(a, j, KT // 2 - 1)
                act.wait_ge(S.f_used[last % 3], last // 3 + 1)
                if a and j == 0:
                    act.wait_ge(S.mod_mm, a)
                act.copy(msb[0:2 * NC9, j * D:(j + 1) * D],
                         ps[0:2 * NC9, 2 * ((3 * a + j) % 2):2 * ((3 * a + j) % 2) + 2, :]
                         .rearrange("p b n -> p (b n)")).then_inc(S.ada_evac, 1)

    @block.tensor
    def _(pe):
        pe.wait_ge(S.const_in, 16)
        pe.wait_ge(S.csil, 1)
        for k in range(KT):
            mm = pe.transpose(ps[:, 7, 10 * k:10 * k + NC9], csil[:, k * P:(k + 1) * P], ident[0:NC9, 0:NC9])
        mm.then_inc(S.small_ready, 1)
        pe.wait_ge(S.vec_in, 16 * 9)
        pe.wait_ge(S.cT_ready, 1)
        pe.transpose(ps[:, 7, 0:41], vrow[0:41, :], ident[0:41, 0:41])
        for j in range(4):
            mm = pe.transpose(ps[:, 7, 64 + 88 * j:64 + 88 * (j + 1)], crow2[:, j, :], ident[0:88, 0:88])
        mm.then_inc(S.small_ready, 1)
        for q in range(18):
            t, half = q // 2, q % 2
            pe.wait_ge(S.x_in[t], 16)
            if q >= 2:
                pe.wait_ge(S.x_evac, q - 1)
            for k in range(4):
                kk = 4 * half + k
                mm = pe.transpose(ps[:, 6 - 2 * (q % 2), k * P:(k + 1) * P], xrow[:, t, kk * P:(kk + 1) * P], ident)
            mm.then_inc(S.x_turned, 1)
        pe.wait_ge(S.c_low, 2)
        pe.wait_ge(S.small_evac, 1)
        for a in range(4):
            for j in range(3):
                u = 3 * a + j
                if u >= 2:
                    pe.wait_ge(S.ada_evac, u - 1)
                for k in range(KT):
                    c = ada_chunk(a, j, k // 2)
                    w, wl = ring.ready(pe, c)
                    for h in range(2):
                        cols = slice(D * (k % 2) + 512 * h, D * (k % 2) + 512 * (h + 1))
                        pe.matmul(ps[:, 2 * (u % 2) + h, :], cst[:, k, :], w[:, cols], start=(k == 0), stop=False)
                        mm = pe.matmul(ps[:, 2 * (u % 2) + h, :], cb[:, k, :], wl[:, cols],
                                       start=False, stop=(k == KT - 1))
                    if k % 2:
                        mm.then_inc(S.f_used[c % 3], 1)
            pe.wait_ge(S.ada_evac, 3 * (a + 1))
            pe.wait_ge(S.adab_in, 16 * (a + 1))
            if a:
                pe.wait_ge(S.mod_evac, a)
            for n in range(24):
                mm = pe.matmul(ps[:, 7, 10 * n:10 * n + 10], msb[0:2 * NC9 + 1, n * P:(n + 1) * P],
                               K[0:2 * NC9 + 1, C_ADA:C_ADA + 10], start=(n == 0), stop=(n == 23),
                               skip_group_check=True)
            mm.then_inc(S.mod_mm, 1)

    @block.vector
    def _(dve):
        ch = Chain(dve, S.set_step)
        dve.wait_ge(S.lam_in, 64)
        for j in range(2):
            dve.tensor_tensor_reduce(out=lamp[:, j, :], in0=lamv[:, 2 * j, :], in1=lamv[:, 2 * j + 1, :], scale=1.0,
                                     scalar=0.0, op0=ALU.mult, op1=ALU.add,
                                     accum_out=lams[:, j:j + 1]).then_inc(S.lam_dot, 1)
        dve.wait_ge(S.tab_in, 16)
        dve.tensor_scalar(rev[:, P:384], tab[:, 255::-1], tab[:, 256:257], 1.0 / SCALE, ALU.subtract,
                          ALU.mult).then_inc(S.rev_made, 1)
        dve.wait_ge(S.small_ready, 1)
        dve.tensor_copy(cT[:, :].rearrange("p (k c) -> p k c", k=KT)[:, :, 0:NC9],
                        ps[:, 7, 0:80].rearrange("p (k c) -> p k c", k=KT)[:, :, 0:NC9]).then_inc(S.cT_ready, 1)
        dve.wait_ge(S.cT_ready, 1)
        for c in range(3):
            ring.split_low(dve, c)
        dve.wait_ge(S.c_high, 1)
        cT3 = cT[:, :].rearrange("p (k c) -> p k c", k=KT)[:, :, 0:NC9]
        dve.tensor_tensor(cst[:, :, NC9:2 * NC9], cT3, cst[:, :, 0:NC9].bitcast(F32), ALU.subtract).then_inc(S.c_low, 1)
        dve.wait_ge(S.set_zero, 2)
        dve.tensor_copy(cb[:, :, 0:NC9], cst[:, :, 0:NC9].bitcast(F32)).then_inc(S.c_low, 1)
        dve.wait_ge(S.lam_exp, 1)
        ch.then(dve.tensor_tensor(lams[:, 0:1], lams[:, 3:4], lams[:, 2:3], ALU.subtract))
        ch.then(dve.tensor_scalar(G.nlam[:, :], lams[:, 0:1], -LAM_INIT, None, ALU.add))
        dve.wait_ge(S.const_in, 16)
        dve.scalar_tensor_tensor(out=G.cfac[:, :], in0=K[:, C_SEL + 1:C_SEL + 2], scalar=G.nlam[:, 0:1],
                                 in1=K[:, C_SEL:C_SEL + 1], op0=ALU.mult, op1=ALU.add)
        dve.wait_ge(S.sink_in, 16)
        ch.then(dve.tensor_scalar(G.sinks_s[:, :], G.sinkp[:, 0::2], K[:, C_SEL:C_SEL + 1], None, ALU.mult))
        ch.then(dve.scalar_tensor_tensor(out=G.sinks_s[:, :], in0=G.sinkp[:, 1::2], scalar=K[:, C_SEL + 1:C_SEL + 2],
                                         in1=G.sinks_s[:, :], op0=ALU.mult, op1=ALU.add))
        dve.wait_ge(S.small_ready, 2)
        ch.then(dve.tensor_copy(gT[:, :], ps[:, 7, 0:41]))
        ch.then(dve.tensor_copy(cvT[:, :, :, :].rearrange("p l j t -> p (l j t)"), ps[:, 7, 64:416]))
        dve.tensor_scalar(G.gsub[:, :], gT[:, 40:41], 1.0 - LAM_INIT, None, ALU.mult).then_inc(S.small_evac, 1)
        for a in range(4):
            for j in range(3):
                for k in range(KT // 2):
                    c = ada_chunk(a, j, k)
                    if c + 3 < FBASE:
                        ring.split_low(dve, c + 3)
            dve.wait_ge(S.mod_mm, a + 1)
            ch.then(dve.tensor_copy(mod[:, a, :, :],
                                    ps[:, 7, 0:240].rearrange("p (n c) -> p n c", n=24)[:, :, 0:NC9]))
            dve.scalar_tensor_tensor(out=gs[:, a, :, :], in0=mod[:, a, 8:16, :], scalar=1.0,
                                     in1=gT[:, 8 * a:8 * a + 8].unsqueeze(2).broadcast_to([P, 8, NC9]),
                                     op0=ALU.add, op1=ALU.mult).then_inc(S.mod_evac, 1)


def norm_pe(pe, S, G, m, sq):
    for n in range(KT):
        pe.wait_ge(S.sq_ready, KT * m + n + 1)
        for b, (lo, hi) in enumerate(COLS):
            mm = pe.matmul(G.psum[:, b, 0:hi - lo], G.ones[:, :], sq[n % 2][:, lo:hi],
                           start=(n == 0), stop=(n == KT - 1))
        mm.then_inc(S.sq_used, 1)


def norm_act(act, S, G, m, sq, rs):
    for n in range(KT):
        if n >= 2:
            act.wait_ge(S.sq_used, KT * m + n - 1)
        act.activation(sq[n % 2][:, 0:TOK], G.xT[:, n, :], ACT.Square).then_inc(S.sq_ready, 1)
    act.wait_ge(S.sq_used, KT * (m + 1))
    act.activation(rs[:, 0:TOK], G.psum[:, 0:3, :].rearrange("p b n -> p (b n)")[:, 0:TOK], ACT.Sqrt,
                   scale=1.0 / D, bias=G.eps[:, 0:1]).then_inc(S.root, 1)


def mod_act(act, S, G, m, a, tmp, ts):
    act.wait_ge(S.hs_ready, m + 1)
    act.copy(G.h[:, :, SEQ:TOK], ts[:, 0:KT * TS].rearrange("p (k t) -> p k t", k=KT)).then_inc(S.hs_high, 1)
    for k in range(KT):
        act.wait_ge(S.hp_ready, KT * m + k + 1)
        act.activation(G.h[:, k, 0:SEQ], tmp[k % 2][:, 0:SEQ], ACT.Identity,
                       bias=G.mod[:, a, k, 0:1], scale=1.0).then_inc(S.hp_high, 1)


def mod_dve(dve, ch, S, G, m, a, tmp, rs, ts):
    dve.wait_ge(S.root, m + 1)
    ch.then(dve.reciprocal(rs[:, 0:TOK], rs[:, 0:TOK]))
    t4 = ts[:, 0:KT * TS].rearrange("p (k b q) -> p k b q", k=KT, b=NB)
    t3 = ts[:, 0:KT * TS].rearrange("p (k t) -> p k t", k=KT)
    ch.then(dve.tensor_tensor(t3, G.xT[:, :, SEQ:TOK], rs[:, SEQ:TOK].unsqueeze(1).broadcast_to([P, KT, TS]), ALU.mult))
    ch.then(dve.tensor_tensor(t4, t4, G.gs[:, a, :, 1:NC9].unsqueeze(3).broadcast_to([P, KT, NB, NS]), ALU.mult))
    dve.tensor_tensor(t4, t4, G.mod[:, a, 0:KT, 1:NC9].unsqueeze(3).broadcast_to([P, KT, NB, NS]),
                      ALU.add).then_inc(S.hs_ready, 1)

    def scaled(k):
        if k >= 2:
            dve.wait_ge(S.hp_low, KT * m + k - 1)
        dve.scalar_tensor_tensor(out=tmp[k % 2][:, 0:SEQ], in0=G.xT[:, k, 0:SEQ], scalar=G.gs[:, a, k, 0:1],
                                 in1=rs[:, 0:SEQ], op0=ALU.mult, op1=ALU.mult).then_inc(S.hp_ready, 1)

    scaled(0)
    dve.wait_ge(S.hs_high, m + 1)
    dve.tensor_tensor(G.hl[:, :, SEQ:TOK], t3, G.h[:, :, SEQ:TOK].bitcast(F32), ALU.subtract).then_inc(S.hs_low, 1)
    for k in range(KT):
        if k + 1 < KT:
            scaled(k + 1)
        dve.wait_ge(S.hp_high, KT * m + k + 1)
        dve.scalar_tensor_tensor(out=G.hl[:, k, 0:SEQ], in0=tmp[k % 2][:, 0:SEQ], scalar=G.mod[:, a, k, 0:1],
                                 in1=G.h[:, k, 0:SEQ].bitcast(F32), op0=ALU.add,
                                 op1=ALU.subtract).then_inc(S.hp_low, 1)


def h_ready(pe, S, m, k):
    if k == 0:
        pe.wait_ge(S.hs_low, m + 1)
    pe.wait_ge(S.hp_low, KT * m + k + 1)


def residual(dve, ch, S, G, n, a, acc, tmp):
    y = G.psum[:, acc:acc + 3, :].rearrange("p b n -> p (b n)")
    ys = y[:, SEQ:TOK].rearrange("p (b q) -> p b q", b=NB)
    ch.then(dve.tensor_tensor(tmp.rearrange("p (b q) -> p b q", b=NB), ys,
                              G.mod[:, a, 16 + n, 1:NC9].unsqueeze(2).broadcast_to([P, NB, NS]), ALU.mult))
    dve.tensor_tensor(G.xT[:, n, SEQ:TOK], G.xT[:, n, SEQ:TOK], tmp, ALU.add)
    return dve.scalar_tensor_tensor(out=G.xT[:, n, 0:SEQ], in0=y[:, 0:SEQ], scalar=G.mod[:, a, 16 + n, 0:1],
                                    in1=G.xT[:, n, 0:SEQ], op0=ALU.mult, op1=ALU.add)


UP = 2 + SEQ + NB * (NS + 2)
FCH = 6 * (FT // 2)
NG = FT // 2
HALO = FT * P


def ffn(nc, S, G, ins, outs, l):
    ctx = ExitStack()
    with ctx:
        def sb(name, shape, dt=F32):
            return ctx.enter_context(nc.sbuf_tensor(f"{name}{l}", shape, dt))

        ring = Ring(nc, ctx, f"ffn{l}", 3, S.f_landed, S.f_high, S.f_low, S.f_used, first=FBASE // 3)
        actr = sb("actr", [P, 2, TOK], F32R)
        actl = sb("actl", [P, 2, TOK], BF16)
        U = [sb(f"u{j}_", [P, UP]) for j in range(2)]
        Y = [sb(f"y{j}_", [P, UP]) for j in range(2)]
        st_raw = sb("st_raw", [16, 4, P])
        stT = sb("stT", [P, 64])
        so = sb("so", [P, 4, 18])
        sout = sb("sout", [18, 4, P])
        rtmp = sb("rtmp", [P, 2, TS])
        ps, h, hl = G.psum, G.h, G.hl
        ident = G.consts[:, C_ID:C_ID + P]
        m = 2 * l + 1
        fb = FBASE + l * FCH
        block = ctx.enter_context(nc.Block())
        w_up = ins["w_up"][l].rearrange("(k p) n -> p k n", p=P)
        w_down = ins["w_down"][l]
        state = ins["state_conv"][l].rearrange("b r (h f) -> (b r) h f", h=2)
        oprompt = outs["conv_p"][l, 0].rearrange("r (h f) -> r h f", h=2)
        osample = outs["conv_s"][l].rearrange("b r (h f) -> (b r) h f", h=2)
        U_s = [u[:, 2 + SEQ:UP].rearrange("p (b q) -> p b q", b=NB) for u in U]
        Y_s = [y[:, 2 + SEQ:UP].rearrange("p (b q) -> p b q", b=NB) for y in Y]

        def chunks(i):
            if isinstance(i, int):
                return (fb if i == 0 else fb + 4 + 6 * (i - 1)), 0
            return fb + 4, 2 * (i - 1)

        def groups(eng, body):
            body(0)
            with eng.Fori(1, NG - 1) as i:
                body(i)
            body(NG - 1)

        @block.sync
        def _(sp):
            def up(i, c, turns, j, gate):
                ring.load(sp, c, w_up[:, :, bass.ds(gate * HALO + (2 * i + j) * P, P)], turns,
                          ("p (k n) -> p k n", dict(k=KT)))

            def down(i, c, turns, j):
                ring.load(sp, c, w_down[bass.ds((2 * i + j) * P, P), :], turns)

            def body(i):
                c, t = chunks(i)
                up(i, c, t, 0, 0)
                c += 1
                if not (isinstance(i, int) and i == 0):
                    down(i - 1, c, t, 0)
                    down(i - 1, c + 1, t, 1)
                    c += 2
                up(i, c, t, 0, 1)
                up(i, c + 1, t, 1, 0)
                up(i, c + 2, t, 1, 1)

            groups(sp, body)
            c = fb + FCH - 2
            down(NG - 1, c, 0, 0)
            down(NG - 1, c + 1, 0, 1)

        @block.gpsimd
        def _(pool):
            def earlier(i):
                pool.dma_start(st_raw[:, :, :].rearrange("r (h j) f -> r h (j f)", h=2),
                               state[:, :, bass.ds(2 * i * P, 2 * P)]).then_inc(S.st_in, 16)

            def store(i):
                pool.wait_ge(S.so_evac, NG * l + i + 1)
                settle(pool, S)
                v = sout[:, :, :].rearrange("r (h j) f -> r h (j f)", h=2)
                pool.dma_start(oprompt[:, :, bass.ds(2 * i * P, 2 * P)], v[0:2]).then_inc(S.so_out, 16)
                pool.dma_start(osample[:, :, bass.ds(2 * i * P, 2 * P)], v[2:18]).then_inc(S.so_out, 16)

            if l == 0:
                pool.sem_inc(S.so_free, 1)
            earlier(0)

            def body(i):
                first = isinstance(i, int) and i == 0
                last = isinstance(i, int) and i == NG - 1
                n = NG * l + i
                for p in range(4):
                    j, g = p // 2, p % 2
                    pool.wait_ge(S.u_evac, 4 * n + p + 1)
                    settle(pool, S)
                    if p == 0 and not first:
                        pool.wait_ge(S.so_turned, n)
                        settle(pool, S)
                    pool.tensor_copy(so[:, 2 * g + j, 0:2], U[g][:, SEQ:SEQ + 2])
                    pool.tensor_copy(so[:, 2 * g + j, 2:18].rearrange("p (b r) -> p b r", b=NB),
                                     U_s[g][:, :, NS:NS + 2]).then_inc(S.u_last, 1)
                    if p == 0:
                        if not last:
                            pool.wait_ge(S.st_turned, n + 1)
                            settle(pool, S)
                            earlier(i + 1)
                        if not first:
                            store(i - 1)
                if not first:
                    pool.wait_ge(S.so_out, 32 * n)
                    pool.sem_inc(S.so_free, 1)

            groups(pool, body)
            store(NG - 1)
            pool.wait_ge(S.so_out, 32 * NG * (l + 1))
            pool.sem_inc(S.so_free, 1)

        @block.tensor
        def _(pe):
            norm_pe(pe, S, G, m, U)
            ring_used = S.f_used

            def up_tile(c, turns, acc, first=False):
                w, wl = ring.ready(pe, c, turns)
                for k in range(KT):
                    if first:
                        h_ready(pe, S, m, k)
                    for b, (lo, hi) in enumerate(COLS):
                        mm = mm3(pe, ps[:, acc + b, 0:hi - lo], w[:, k * P:(k + 1) * P], wl[:, k * P:(k + 1) * P],
                                 h[:, k, lo:hi], hl[:, k, lo:hi], k == 0, k == KT - 1)
                mm.then_inc(ring_used[c % 3], 1)

            def down(c, turns, i, last=False):
                d = KT * (NG * l + i)
                (w0, wl0), (w1, wl1) = ring.ready(pe, c, turns), ring.ready(pe, c + 1, turns)
                pe.wait_ge(S.act_low_f, 2 * (NG * l + i) + 2)
                for n in range(KT):
                    if n == 0:
                        pe.wait_ge(S.u_evac, 4 * (NG * l + i) + 4)
                    elif n == 1 and not last:
                        pe.wait_ge(S.u_evac, 4 * (NG * l + i) + 5)
                    elif n >= 2:
                        pe.wait_ge(S.d_evac, d + n - 1)
                    acc = 3 * ((1 + n) % 2)
                    for j, (w, wl) in enumerate(((w0, wl0), (w1, wl1))):
                        for b, (lo, hi) in enumerate(COLS):
                            mm = mm3(pe, ps[:, acc + b, 0:hi - lo], w[:, n * P:(n + 1) * P],
                                     wl[:, n * P:(n + 1) * P], actr[:, j, lo:hi], actl[:, j, lo:hi],
                                     j == 0, j == 1)
                        if n == KT - 1:
                            mm.then_inc(ring_used[(c + j) % 3], 1)
                    if n < KT - 1:
                        mm.then_inc(S.d_ready, 1)

            def last_rows(g):
                pe.wait_ge(S.u_last, 4 * g + 4)
                for q in range(4):
                    mm = pe.transpose(ps[0:18, 6, q * P:(q + 1) * P], so[:, q, :], ident)
                mm.then_inc(S.so_turned, 1)

            def body(i):
                c, t = chunks(i)
                first = isinstance(i, int) and i == 0
                g = NG * l + i
                pe.wait_ge(S.st_in, 16 * (g + 1))
                if not (first and l == 0):
                    pe.wait_ge(S.st_evac, g)
                if not first:
                    pe.wait_ge(S.u_evac, 4 * g - 1)
                else:
                    pe.wait_ge(S.root, m + 1)
                up_tile(c, t, 0, first)
                c += 1
                for q in range(4):
                    mm = pe.transpose(ps[:, 7, 16 * q:16 * q + 16], st_raw[:, q, :], ident[0:16, 0:16])
                mm.then_inc(S.st_turned, 1)
                if not first:
                    last_rows(g - 1)
                    down(c, t, i - 1)
                    c += 2
                    pe.wait_ge(S.d_evac, 8 * (g - 1) + 7)
                up_tile(c, t, 3)
                if first:
                    pe.wait_ge(S.u_evac, 4 * g + 1)
                else:
                    pe.wait_ge(S.d_evac, 8 * g)
                up_tile(c + 1, t, 0)
                pe.wait_ge(S.u_evac, 4 * g + 2)
                up_tile(c + 2, t, 3)

            groups(pe, body)
            last_rows(NG * (l + 1) - 1)
            down(fb + FCH - 2, 0, NG - 1, last=True)

        @block.scalar
        def _(act):
            norm_act(act, S, G, m, U, Y[0])
            for s in range(3):
                ring.split_high(act, fb + s)
            mod_act(act, S, G, m, m, U, Y[1])
            act.wait_ge(S.hp_low, KT * (m + 1))
            for j in range(2):
                act.activation(U[j][:, 0:2], G.ones[:, 0:2], ACT.Copy, scale=0.0).then_inc(S.u_zero, 1)

            def body(i):
                c, t = chunks(i)
                first = isinstance(i, int) and i == 0
                last = isinstance(i, int) and i == NG - 1
                g = NG * l + i
                act.wait_ge(S.st_turned, g + 1)
                if not (first and l == 0):
                    act.wait_ge(S.pads, 4 * g)
                act.copy(stT[:, :], ps[:, 7, 0:64]).then_inc(S.st_evac, 1)
                for p in range(4):
                    j, gate = p // 2, p % 2
                    at = p if first else (0, 3, 4, 5)[p]
                    s = (c + at) % 3
                    act.wait_ge(S.f_used[s], (c + at) // 3 + t + 1)
                    if not (first and l == 0 and p < 2):
                        act.wait_ge(S.conv, 4 * g + p - 1)
                        act.wait_ge(S.u_last, 4 * g + p - 1)
                    act.copy(U[gate][:, 2:2 + SEQ], ps[:, 3 * gate:3 * gate + 2, :].rearrange("p b n -> p (b n)"))
                    act.copy(U_s[gate][:, :, 2:2 + NS],
                             ps[:, 3 * gate + 2, 0:TS].rearrange("p (b q) -> p b q", b=NB)).then_inc(S.u_evac, 1)
                    if p == 0:
                        act.wait_ge(S.st_evac, g + 1)
                    q = 2 * gate + j
                    act.copy(U_s[gate][:, :, 0:2],
                             stT[:, 16 * q:16 * q + 16].rearrange("p (b r) -> p b r", b=NB)).then_inc(S.pads, 1)
                    nxt = c + at + 3
                    if not last or nxt < fb + FCH:
                        ring.split_high(act, nxt, t)
                    if p == 0 and not first:
                        last_rows(g - 1)
                        ring.split_high(act, c + 4, t)
                        ring.split_high(act, c + 5, t)
                    if gate:
                        act.wait_ge(S.conv, 4 * g + p + 1)
                        act.activation(Y[1][:, 0:UP - 2], Y[1][:, 0:UP - 2], ACT.Silu).then_inc(S.silu, 1)
                        act.wait_ge(S.prod, 2 * g + j + 1)
                        act.copy(actr[:, j, 0:SEQ], Y[0][:, 0:SEQ])
                        act.copy(actr[:, j, SEQ:TOK].rearrange("p (b q) -> p b q", b=NB),
                                 Y_s[0][:, :, 0:NS]).then_inc(S.act_high_f, 1)

            def last_rows(g):
                act.wait_ge(S.so_turned, g + 1)
                act.wait_ge(S.so_free, g + 1)
                act.copy(sout[:, :, :].rearrange("r q f -> r (q f)"), ps[0:18, 6, :]).then_inc(S.so_evac, 1)

            groups(act, body)
            last_rows(NG * (l + 1) - 1)

        @block.vector
        def _(dve):
            ch = Chain(dve, S.dve_step[m])
            for s in range(3):
                ring.split_low(dve, fb + s)
            mod_dve(dve, ch, S, G, m, m, U, Y[0], Y[1])
            cv = G.cvT

            def body(i):
                c, t = chunks(i)
                first = isinstance(i, int) and i == 0
                last = isinstance(i, int) and i == NG - 1
                g = NG * l + i
                for p in range(4):
                    j, gate = p // 2, p % 2
                    f = gate * FT + 2 * i + j
                    at = p if first else (0, 3, 4, 5)[p]
                    dve.wait_ge(S.pads, 4 * g + p + 1)
                    if not gate and not (first and l == 0 and j == 0):
                        dve.wait_ge(S.act_low_f, 2 * g + j)
                    n = UP - 2
                    u, y = U[gate], Y[gate]
                    ch.then(dve.tensor_scalar(y[:, 0:n], u[:, 2:2 + n], cv[:, l, 2, bass.ds(f, 1)],
                                              cv[:, l, 3, bass.ds(f, 1)], ALU.mult, ALU.add))
                    ch.then(dve.scalar_tensor_tensor(out=y[:, 0:n], in0=u[:, 1:1 + n], scalar=cv[:, l, 1, bass.ds(f, 1)],
                                                     in1=y[:, 0:n], op0=ALU.mult, op1=ALU.add))
                    dve.scalar_tensor_tensor(out=y[:, 0:n], in0=u[:, 0:n], scalar=cv[:, l, 0, bass.ds(f, 1)],
                                             in1=y[:, 0:n], op0=ALU.mult, op1=ALU.add).then_inc(S.conv, 1)
                    nxt = c + at + 3
                    if not last or nxt < fb + FCH:
                        ring.split_low(dve, nxt, t)
                    if p == 0 and not first:
                        down_evac(i - 1, c + 1, t)
                        ring.split_low(dve, c + 4, t)
                        ring.split_low(dve, c + 5, t)
                    if gate:
                        dve.wait_ge(S.silu, 2 * g + j + 1)
                        dve.tensor_tensor(Y[0][:, 0:n], Y[0][:, 0:n], Y[1][:, 0:n], ALU.mult).then_inc(S.prod, 1)
                        dve.wait_ge(S.act_high_f, 2 * g + j + 1)
                        dve.tensor_tensor(actl[:, j, 0:SEQ], Y[0][:, 0:SEQ], actr[:, j, 0:SEQ].bitcast(F32), ALU.subtract)
                        dve.tensor_tensor(actl[:, j, SEQ:TOK].rearrange("p (b q) -> p b q", b=NB), Y_s[0][:, :, 0:NS],
                                          actr[:, j, SEQ:TOK].bitcast(F32).rearrange("p (b q) -> p b q", b=NB),
                                          ALU.subtract).then_inc(S.act_low_f, 1)

            def down_evac(i, c, turns):
                for n in range(KT):
                    if n < KT - 1:
                        dve.wait_ge(S.d_ready, (KT - 1) * (NG * l + i) + n + 1)
                    else:
                        ring.done(dve, c + 1, turns)
                    if n >= 2:
                        dve.wait_ge(S.d_evac, KT * (NG * l + i) + n - 1)
                    residual(dve, ch, S, G, n, m, 3 * ((1 + n) % 2), rtmp[:, n % 2, :]).then_inc(S.d_evac, 1)

            body(0)
            start = ch.n
            with dve.Fori(1, NG - 1) as i:
                per = FFN_DVE_STEPS
                ch.base, ch.n = start + (i - 1) * per, 0
                body(i)
                assert ch.n == per, ch.n
            ch.base, ch.n = start + per * (NG - 2), 0
            body(NG - 1)
            down_evac(NG - 1, fb + FCH - 2, 0)


FFN_DVE_STEPS = 16


WIN = {"A": QB, "B": 1, "C": 4}
FIRST_TILE = {"A": 0, "B": 4, "C": 8}
CACHE_B = {"A": 4, "B": 1, "C": 4}
UNITS = QB + 2
KV_OF_C = 2


def kv(kind, T):
    return T if kind == "A" else 4 + (T - 4) // 2 if kind == "B" else T - KV_OF_C


def new_kv(kind, T):
    return kind != "B" or T % 2 == 0


def width(kind, u):
    return P * (min(u, WIN[kind]) + 1)


def first_key(kind, u):
    return P * max(0, u - WIN[kind])


def stream_width(kind):
    return P * (CACHE_B[kind] + 1)


def tile_steps(kind, fill, out, keys):
    outs = [("OUT", n) for n in range(KT)] if out else []
    steps = [("KT",), ("VT",), ("CQ",)] + outs[0:1] + [("CK",)] + outs[1:2] + [("VS",)] if keys else [("CQ",)] + outs[0:2]
    last = 0 if kind == "A" else 1
    body = []
    for u in range(QB + 1):
        scored = u < QB
        one, two = ((outs[2:4], outs[4:5]), (outs[5:6], outs[6:8]))[u] if u < 2 and out else ([4], [4])
        body += [("FA", u - 1)] if u else []
        body += ([("S", u, 0)] if scored else [("QZ", 0)]) + ([("V", u - 2)] if u > 1 else [])
        body += [("KR",)] if u == 0 and keys else []
        turned, finished = [("T", u - 1, 0)] if u else [], [("N", u - 2)] if u > 1 else []
        body += finished + one + turned if kind == "A" else turned + finished + one
        body += ([("S", u, 1)] if scored else []) + ([("O", u - 2)] if u > 1 else [])
        body += ([("T", u - 1, 1)] if u and last else []) + two
    body += [("V", QB - 1)]
    for g in range(2):
        u = QB + g
        body += [("K", g, 0), ("K", g, 1), 3, ("N", u - 1), ("SK", g, 0), ("K", g, 2), ("O", u - 1), 2, ("SK", g, 1),
                 ("K", g, 3), ("SK", g, 2), 1, ("SK", g, 3), ("VH", g, 0), ("VH", g, 1), ("X", u), 9, ("FA", u),
                 ("VI", g, 0), ("VI", g, 1)] + ([("QZ", 1)] if g == 0 else []) + \
                [("T", u, 0), 4, ("PV", g, 0), ("VH", g, 2), ("VI", g, 2), ("PV", g, 1), ("VH", g, 3), ("VI", g, 3),
                 ("PV", g, 2), 1, ("PV", g, 3), ("V", u)]
    body += [4, ("N", QB + 1), 4, ("O", QB + 1)]
    total = sum(s for s in body if isinstance(s, int))
    todo = [("F", name, k) for name in fill for k in range(KT)]
    seen = sent = 0
    turn, later = [], []
    for s in body:
        if not isinstance(s, int):
            steps.append(s)
            if s == ("OUT", KT - 1):
                turn = [("W",)]
            continue
        seen += s
        upto = -(-len(todo) * seen // total)
        if upto > sent:
            steps += turn
            turn, later = later, []
        steps += todo[sent:upto]
        for f in todo[sent:upto]:
            if f[2] == KT - 1:
                turn += [("W",)]
                later += [("R", f[1])] if f[1] != "v" else []
        sent = upto
    assert sent == len(todo)
    return steps + turn + later


def first_steps():
    f = {n: [("F", n, k) for k in range(KT)] for n in "qkv"}
    return f["q"] + [("W",)] + f["k"] + [("W",), ("R", "q")] + f["v"] + [("W",), ("R", "k")]


def plan(kinds):
    tiles = [(k, T) for k in kinds for T in range(FIRST_TILE[k], FIRST_TILE[k] + {"A": 4, "B": 4, "C": 8}[k])]
    c = 3
    out = []
    for n, (k, T) in enumerate(tiles):
        fill = ""
        if n + 1 < len(tiles):
            fill = "qkv" if new_kv(*tiles[n + 1]) else "q"
        out.append((k, T, fill, c))
        c += len(fill) + (n > 0)
    return out, c + 1


AB_CHUNKS = plan("AB")[1]


def attention(nc, S, G, ins, outs, kinds):
    ctx = ExitStack()
    with ctx:
        def sb(name, shape, dt=F32):
            return ctx.enter_context(nc.sbuf_tensor(f"{name}_{kinds}", shape, dt))

        odd = kinds == "C"
        ring = Ring(nc, ctx, f"att{kinds}", 2, S.t_landed, S.t_high, S.t_low, S.t_used)
        F = {n: sb(f"f_{n}", [P, TOK]) for n in "qkv"}
        sw = sb("sw", [P, TOK])
        q, ql = sb("q", [P, TOK], F32R), sb("ql", [P, TOK], BF16)
        kk, kl = sb("k", [P, TOK], F32R), sb("kl", [P, TOK], BF16)
        v, vl = sb("v", [P, TOK], F32R), sb("vl", [P, TOK], BF16)
        E = sb("E", [P, 2560 if odd else 3072])
        W, Wl = sb("W", [P, 1280], F32R), sb("Wl", [P, 1280], BF16)
        actr, actl = sb("actr", [P, TOK], F32R), sb("actl", [P, TOK], BF16)
        raw = [sb(f"raw{s}", [P, 4, P]) if odd or s < 2 else
               E[:, 512 * s + 1024:512 * s + 1536].rearrange("p (j d) -> p j d", d=P) for s in range(4)]
        kc = [sb(f"kc{s}", [P, 512], F32R) for s in range(2)]
        kcl = [sb(f"kcl{s}", [P, 512], BF16) for s in range(2)]
        Qz, Qzl = sb("Qz", [P, 5, P], F32R), sb("Qzl", [P, 5, P], BF16)
        osb, osb2 = sb("osb", [P, P]), sb("osb2", [P, P])
        st = [sb(f"st{j}", [P, 11]) for j in range(2)]
        fin = sb("fin", [P, 3])
        ss, ms, rstd = fin[:, 0:1], fin[:, 1:2], fin[:, 2:3]
        if odd:
            bt, bs = sb("bt", [P, 2, 256]), sb("bs", [P, 144])
        else:
            rope = sb("rope", [P, 2, ROPE_N])
        ps, h, hl, K = G.psum, G.h, G.hl, G.consts
        ident = K[:, C_ID:C_ID + P]
        m = 2 if odd else 0
        a = m
        tiles, total = plan(kinds)
        cb = AB_CHUNKS if odd else 0
        assert cb % 2 == 0
        T0 = tiles[0][1]
        block = ctx.enter_context(nc.Block())
        s_banks = ps[:, 3:5, :].rearrange("p b n -> p (b n)")
        t_banks = ps[:, 5:7, :].rearrange("p b n -> p (b n)")
        w_in = ins["w_in_odd" if odd else "w_in_even"][0].rearrange("(k p) n -> p k n", p=P)
        w_out = ins["w_out_odd" if odd else "w_out_even"][0]

        def un(T, u):
            return UNITS * T + u + 1

        def s_no(T, u, z=0):
            return 18 * T + (2 * u + z if u < QB else QB + u) + 1

        def t_no(kind, T, u, z=0):
            return UNITS * T + u + 1 if kind == "A" else 4 * UNITS + s_no(T - 4, u, z)

        def t_last(kind, T, u):
            return t_no(kind, T, u, 1 if kind != "A" and u < QB else 0)

        def rows_of(u):
            t = st[u % 2]
            return t[:, 0:2], t[:, 2:4], t[:, 4:6], t[:, 6:8], t[:, 8:10], t[:, 10:11]

        def e_at(kind, u, z=0):
            if kind == "A":
                return 2048 if z else 1024 * (u % 2)
            n = 256 if kind == "B" else 640
            return 2 * n * (u % 2) + z * n

        def item(T, g, x):
            return 16 * T + 8 * g + x

        def turned_o(kind, T, u):
            return UNITS * T + u + 1 if kind == "A" else UNITS * 4 + QB * (T - 4) + u + 1

        def run(eng, do):
            do_steps(do, "A" if not odd else "C", T0 - 1, first_steps(), cb, 0)
            if not odd:
                for n, (kind, T, fill, c) in enumerate(tiles):
                    do_steps(do, kind, T, tile_steps(kind, fill, n > 0, new_kv(kind, T)), cb + c, 0)
            else:
                do_steps(do, "C", T0, tile_steps("C", "qkv", False, True), cb + 3, 0)
                with eng.Fori(T0 + 1, T0 + 7) as T:
                    do_steps(do, "C", T, tile_steps("C", "qkv", True, True), cb + 6, 2 * (T - T0 - 1), loop=True)
                do_steps(do, "C", T0 + 7, tile_steps("C", "", True, True), cb + 30, 0)

        def do_steps(do, kind, T, steps, c, turns, loop=False):
            if loop:
                do("LOOP", kind, T, (0,), c, turns)
            for s in steps:
                do(s[0], kind, T, s, c, turns)
                if s == ("OUT", KT - 1) or s[0] == "F" and s[2] == KT - 1:
                    c += 1
            if loop:
                do("END", kind, T, (0,), c, turns)

        def next_tile(kind, T):
            if not isinstance(T, int) or odd:
                return kind, T + 1
            return ("A" if T + 1 < 4 else "B"), T + 1

        def rope_no(kind, T, isq):
            n = kv(kind, T)
            if isq:
                return T + (n if new_kv(kind, T) else n + 1) + 1
            return T + n + 2

        def w_free(eng, kind, T, u):
            if u == 0:
                eng.wait_ge(S.item_used, 16 * T)
            elif u <= QB:
                eng.wait_ge(S.pv, QB * T + u)
            else:
                eng.wait_ge(S.item_used, item(T, 0, 7) + 1)

        def probs_at(kind, u, z):
            if u >= QB:
                return 0, 320 if kind == "A" else stream_width(kind)
            return 640 * z, width(kind, u)

        @block.sync
        def _(sp):
            if not odd:
                sp.dma_start(rope[:, :, :], ins["rope"]).then_inc(S.rope_in, 16)

            twice = [0]

            def w_cols(name, kind, T):
                if kind == "A":
                    off = {"q": 0, "k": 512, "v": 1024}[name] + T * P
                elif kind == "B":
                    if name == "q":
                        off = 1536 + (T - 4) * P
                    else:
                        off = {"k": 2048, "v": 2176}[name] + (T - 4) // 2 * HD
                        return w_in[:, :, off:off + HD]
                else:
                    off = {"q": 0, "k": 1024, "v": 2048}[name] + (T - 8) * P
                return w_in[:, :, bass.ds(off, P)]

            def do(what, kind, T, s, c, turns):
                if s == ("OUT", 0):
                    row = (T - 1 - (8 if odd else 0)) * P
                    ring.load(sp, c, w_out[bass.ds(row, P), :], turns)
                elif what == "F" and s[2] == KT - 1:
                    nk, nT = next_tile(kind, T)
                    src = w_cols(s[1], nk, nT)
                    if nk == "B" and s[1] != "q":
                        sl, n = ring.at(c)
                        sp.wait_ge(ring.low[sl], n)
                        both = ring.raw[sl][:, :].rearrange("p (k z n) -> p k z n", k=KT, z=2)
                        sp.dma_start(both[:, :, 0, :], src).then_inc(S.dup_in, 16)
                        twice[0] += 1
                        sp.wait_ge(S.dup_in, 16 * twice[0])
                        sp.dma_start(both[:, :, 1, :], src).then_inc(ring.landed[sl], 16)
                    else:
                        ring.load(sp, c, src, turns, ("p (k n) -> p k n", dict(k=KT)))

            run(sp, do)
            ring.load(sp, cb + total - 1, w_out[7 * P:8 * P, :])

        @block.gpsimd
        def _(pool):
            pool.memset(Qz[:, :, :].bitcast(F32), 0.0).then_inc(S.qz_zero, 1)
            pool.memset(Qzl[:, :, :], 0.0).then_inc(S.qz_zero, 1)
            pool.wait_ge(S.qz_zero, 4 if odd else 2)
            settle(pool, S)

            def cached(kind, T, m_, slot, cache, b):
                if kind == "A":
                    return ins[f"cache_a_{cache}"][0, b, :, T, :].rearrange("(j p) d -> p j d", p=P)
                if kind == "B":
                    src = ins[f"cache_b_{cache}"][0, b, :, (T - 4) // 2, :]
                    return bass.AP(src.tensor, src.offset, [[2 * HD, P], [0, 2], [1, HD]])
                return ins[f"cache_c_{cache}"][0, b].rearrange("(j p) h d -> p j (h d)", p=P)[
                    :, :, bass.ds((T - 8) * P, P)]

            def load_item(kind, T, g, x):
                it = item(T, g, x)
                slot = x % 4
                if not (isinstance(T, int) and T == 0 and g == 0 and x < 4):
                    pool.wait_ge(S.item_low, it - 3)
                    settle(pool, S)
                if kind == "A" and g == 0 and x == 2:
                    pool.wait_ge(S.probs, un(T, QB - 1))
                src = cached(kind, T, it, slot, "kv"[x // 4], 4 * g + x % 4)
                dst = raw[slot][:, 0, :].rearrange("p (z d) -> p z d", z=2) if kind == "B" else raw[slot][:, :, :]
                pool.dma_start(dst, src).then_inc(S.raw_in[slot], 16)

            def store(kind, T, which):
                n = kv(kind, T)
                rows = sw[:, :].rearrange("p (t d) -> p t d", d=P)
                pool.wait_ge(S.k_rows if which == "k" else S.v_rows, n + 1)
                settle(pool, S)
                if kind == "A":
                    dp = outs[f"a{which}_p"][0, 0, :, T, :].rearrange("(t p) d -> p t d", p=P)
                    ds_ = outs[f"a{which}_s"][0, :, :, T, :]
                    sp_, ss_ = rows[:, 0:QB, :], rows[:, QB, :]
                elif kind == "B":
                    hh = (T - 4) // 2
                    dp = outs[f"b{which}_p"][0, 0, :, hh, :]
                    ds_ = outs[f"b{which}_s"][0, :, P - NS:P, hh, :]
                    sp_, ss_ = rows[:, QB - 1, 0:HD], rows[:, QB, 0:HD]
                else:
                    cols = bass.ds((T - 8) * P, P)
                    dp = outs[f"c{which}_p"][0, 0].rearrange("(t p) h d -> p t (h d)", p=P)[:, :, cols]
                    ds_ = outs[f"c{which}_s"][0, :, PAST - NS:PAST].rearrange("b q h d -> b q (h d)")[:, :, cols]
                    sp_, ss_ = rows[:, 4:QB, :], rows[:, QB, :]
                pool.dma_start(dp, sp_).then_inc(S.stored, 16)
                pool.dma_start(ds_, ss_).then_inc(S.stored, 16)

            def load_bias(T):
                two = G.bias_dram[bass.ds((T - 8) * 2, 2), :, :]
                pool.dma_start(bt[:, :, :], two.rearrange("h i j -> i h j")).then_inc(S.bias_in, 16)
                for b in range(4):
                    pool.dma_start(bs[32 * b:32 * b + 32, :], two[:, 0:NS, 0:P + NS]).then_inc(S.bias_in, 16)

            def keep(T):
                if odd:
                    for w in "kv":
                        pool.dma_start(outs[f"c{w}_s"][0, bass.ds(T - 8, 1), 0:PAST - NS].rearrange("b q h d -> (b q) (h d)"),
                                       ins[f"cache_c_{w}"][0, bass.ds(T - 8, 1), NS:PAST].rearrange(
                                           "b q h d -> (b q) (h d)")).then_inc(S.kept, 16)
                else:
                    for w in "kv":
                        pool.dma_start(outs[f"b{w}_s"][0, T, 0:P - NS].rearrange("q h d -> q (h d)"),
                                       ins[f"cache_b_{w}"][0, T, NS:P].rearrange("q h d -> q (h d)")).then_inc(S.kept, 16)

            def do(what, kind, T, s, c, turns):
                if what == "CQ":
                    if odd:
                        if not (isinstance(T, int) and T == T0):
                            pool.wait_ge(S.nmax, s_no(T, 0) - 1)
                            settle(pool, S)
                        load_bias(T)
                elif what == "S" and s[1:] == (0, 0):
                    keep(T)
                elif what == "VT":
                    store(kind, T, "v")
                elif what == "KR":
                    store(kind, T, "k")
                elif what == "S" and s[1:] == (QB - 1, 0):
                    for x in range(2 if kind == "A" else 4):
                        load_item(kind, T, 0, x)
                elif what == "T" and s[1] == QB - 1 and kind == "A":
                    for x in range(2, 4):
                        load_item(kind, T, 0, x)
                elif what == "K":
                    load_item(kind, T, s[1], s[2] + 4)
                elif what == "VI" and s[1] == 0:
                    load_item(kind, T, 1, s[2])
                elif what == "QZ":
                    g = s[1]
                    pool.wait_ge(S.q_low, T + 1)
                    settle(pool, S)
                    if not (isinstance(T, int) and T == T0 and g == 0):
                        pool.wait_ge(S.stream_scores, 2 * T + g)
                        settle(pool, S)
                    if not odd:
                        pool.wait_ge(S.rstd, min(un(T, QB - 3 + 2 * g), 4 * UNITS))
                    for z in range(2):
                        r = slice(HD * z, HD * z + HD)
                        for dst, src in ((Qz, q), (Qzl, ql)):
                            s3 = src[r, SEQ + 64 * g:SEQ + 64 * g + 64].rearrange("p (b q) -> p b q", b=4)
                            flat = dst[r, :, :].rearrange("p c n -> p (c n)")
                            diag = flat[:, 0:4 * (P + 32)].rearrange("p (b x) -> p b x", b=4)[:, :, z * NS:z * NS + NS]
                            all_ = dst[r, 4, :].rearrange("p (b x) -> p b x", b=4)[:, :, z * NS:z * NS + NS]
                            if dst is Qz:
                                s3 = s3.bitcast(F32)
                            pool.tensor_copy(diag, s3)
                            last = pool.tensor_copy(all_, s3)
                    last.then_inc(S.qz, 1)
                elif what == "N" and kind == "A":
                    pool.wait_ge(S.ms, un(T, s[1]))
                    settle(pool, S)
                    done = 2 * T + (s[1] >= QB - 2) + (s[1] >= QB)
                    if done:
                        pool.wait_ge(S.qz, done)
                    pool.tensor_tensor(rstd, ms, G.mhalf[:, :], ALU.pow).then_inc(S.rstd, 1)
                elif what == "F" and s[2] == KT - 1 and s[1] != "v" and not odd:
                    nk, nT = next_tile(kind, T)
                    name = s[1]
                    n_kv = kv(nk, nT)
                    if name == "q":
                        pool.wait_ge(S.q_evac, nT + 1)
                        settle(pool, S)
                        if nT > 0:
                            prev = kv(kind, T) + 1
                            pool.wait_ge(S.stored, 64 * prev)
                            pool.wait_ge(S.roped, nT + (n_kv if new_kv(nk, nT) else n_kv + 1))
                            settle(pool, S)
                    else:
                        pool.wait_ge(S.k_evac, n_kv + 1)
                        pool.wait_ge(S.roped, nT + 1 + n_kv)
                        settle(pool, S)
                    for z in range(4):
                        y = z ^ 1
                        pool.dma_start(sw[32 * z:32 * z + 32, :], F[name][32 * y:32 * y + 32, :]).then_inc(S.swapped, 16)

            run(pool, do)
            pool.wait_ge(S.stored, 64 * (kv(*tiles[-1][:2]) + 1))
            pool.wait_ge(S.kept, 16 * 16 * (2 if odd else 1))
            settle(pool, S)

        @block.tensor
        def _(pe):
            norm_pe(pe, S, G, m, [F["q"], F["k"]])

            def do(what, kind, T, s, c, turns):
                n = kv(kind, T)
                first = isinstance(T, int) and T == T0
                if what == "F":
                    nk, nT = next_tile(kind, T)
                    name, k = s[1:]
                    w, wl = ring.ready(pe, c, turns) if k == 0 else (ring.w[c % 2][:, :], ring.wl[c % 2][:, :])
                    if k == 0:
                        if isinstance(T, int) and T == T0 - 1:
                            if name == "q":
                                pe.wait_ge(S.root, m + 1)
                            elif name == "k":
                                pe.wait_ge(S.q_evac, nT + 1)
                            else:
                                pe.wait_ge(S.k_evac, kv(nk, nT) + 1)
                        elif name == "q":
                            if first:
                                pe.wait_ge(S.v_rows, n + 1)
                            else:
                                pe.wait_ge(S.out_evac, 3 * KT * T)
                        elif name == "k":
                            pe.wait_ge(S.q_evac, nT + 1)
                        else:
                            pe.wait_ge(S.k_evac, kv(nk, nT) + 1)
                    if isinstance(T, int) and T == T0 - 1 and name == "q":
                        h_ready(pe, S, m, k)
                    for b, (lo, hi) in enumerate(COLS):
                        mm = mm3(pe, ps[:, b, 0:hi - lo], w[:, k * P:(k + 1) * P], wl[:, k * P:(k + 1) * P],
                                 h[:, k, lo:hi], hl[:, k, lo:hi], k == 0, k == KT - 1)
                    if k == KT - 1:
                        mm.then_inc(S.t_used[c % 2], 1)
                elif what == "VT":
                    pe.wait_ge(S.v_evac, n + 1)
                    for t in range(TB):
                        mm = pe.transpose(ps[:, t // 4, (t % 4) * P:(t % 4 + 1) * P], F["v"][:, t * P:(t + 1) * P], ident)
                    mm.then_inc(S.v_turned, 1)
                elif what == "KT":
                    if odd:
                        pe.wait_ge(S.k_evac, n + 1)
                    else:
                        pe.wait_ge(S.roped, T + n + 2)
                    if not first:
                        pe.wait_ge(S.act_low, un(T, 0) - 1)
                    for t in range(TB):
                        dst = t_banks[:, t * P:(t + 1) * P] if t < QB else ps[:, 7, 3 * P:4 * P]
                        mm = pe.transpose(dst, F["k"][:, t * P:(t + 1) * P], ident)
                    mm.then_inc(S.k_turned, 1)
                elif what == "OUT":
                    out_piece(T - 1, s[1], c, turns)
                elif what == "S":
                    scores(kind, T, s[1], s[2], n)
                elif what == "K":
                    g, b = s[1:]
                    it = item(T, g, b)
                    pe.wait_ge(S.raw_in[b], 16 * (4 * T + 2 * g + 1))
                    if not (isinstance(T, int) and T == 0 and g == 0 and b < 2):
                        pe.wait_ge(S.item_low, it - 1)
                    if b == 0:
                        pe.wait_ge(S.w_low, t_last(kind, T, QB + g - 1))
                    for j in range(CACHE_B[kind]):
                        mm = pe.transpose(ps[:, 5 + b % 2, j * P:(j + 1) * P], raw[b][:, j, :], ident)
                    mm.then_inc(S.kc_turned, 1)
                elif what == "SK":
                    g, b = s[1:]
                    nk = CACHE_B[kind] * P
                    it = item(T, g, b)
                    pe.wait_ge(S.item_low, it + 1)
                    if b == 0:
                        pe.wait_ge(S.qz, 2 * T + g + 1)
                        pe.wait_ge(S.exps, s_no(T, QB + g - 1, 1 - g))
                    mm = mm3(pe, ps[:, 3, 0:nk], Qz[:, b, :], Qzl[:, b, :], kc[b % 2][:, 0:nk], kcl[b % 2][:, 0:nk],
                             b == 0, b == 3)
                    mm.then_inc(S.item_used, 1)
                    if b == 3:
                        new = s_banks[:, nk:nk + P]
                        mm3(pe, new, Qz[:, 4, :], Qzl[:, 4, :], kk[:, SEQ:TOK], kl[:, SEQ:TOK], True, False)
                        pe.matmul(new, K[0:NB, C_MB + g * P:C_MB + (g + 1) * P], K[0:NB, C_RB:C_RB + P],
                                  start=False, stop=True, skip_group_check=True).then_inc(S.stream_scores, 1)
                elif what == "T":
                    u, z = s[1:]
                    if u == 0 and z == 0:
                        pe.wait_ge(S.k_rows, n + 1)
                    if kind == "A" or u >= QB:
                        pe.wait_ge(S.probs, un(T, u))
                    else:
                        pe.wait_ge(S.exps, s_no(T, u, z))
                    if not (isinstance(T, int) and T == 0 and u == 0):
                        pe.wait_ge(S.w_low, t_no(kind, T, u, z) - 1)
                    e0 = e_at(kind, u, z)
                    if u >= QB and kind == "A":
                        for j in range(5):
                            mm = pe.matmul(t_banks[:, 64 * j:64 * j + 64], E[:, e0 + j * P:e0 + (j + 1) * P],
                                           K[:, C_CA:C_CA + 64], start=(j == 0), stop=(j == 4), skip_group_check=True)
                    else:
                        wd = width(kind, u) if u < QB else stream_width(kind)
                        for j in range(wd // P):
                            mm = pe.transpose(t_banks[:, j * P:(j + 1) * P], E[:, e0 + j * P:e0 + (j + 1) * P], ident)
                    mm.then_inc(S.turned, 1)
                elif what == "V" and s[1] < QB:
                    u = s[1]
                    pe.wait_ge(S.w_low, t_last(kind, T, u))
                    if u == 0:
                        pe.wait_ge(S.v_low, n + 1)
                    if not (first and u == 0):
                        o_bank_free(kind, T, u)
                    k0 = first_key(kind, u) // P
                    nb = width(kind, u) // P
                    for z in range(1 if kind == "A" else 2):
                        cols = slice(0, P) if kind == "A" else slice(HD * z, HD * z + HD)
                        for j in range(nb):
                            x = slice(z * 640 + j * P, z * 640 + (j + 1) * P)
                            y = slice((k0 + j) * P + cols.start, (k0 + j) * P + cols.stop)
                            mm = mm3(pe, ps[:, 7, cols], W[:, x], Wl[:, x], v[:, y], vl[:, y], j == 0, j == nb - 1)
                    mm.then_inc(S.pv, 1)
                elif what == "V" and kind == "A":
                    pe.wait_ge(S.od, 2 * T + s[1] - QB + 1)
                    pe.transpose(ps[0:64, 7, P:2 * P], E[:, 1664:1664 + 64], ident).then_inc(S.od_turned, 1)
                elif what == "PV":
                    g, b = s[1:]
                    it = item(T, g, 4 + b)
                    rows = NS if kind == "A" else 2 * NS
                    all_ = 4 * rows
                    nc_ = CACHE_B[kind]
                    if b == 0:
                        pe.wait_ge(S.w_low, t_no(kind, T, QB + g))
                        o_bank_free(kind, T, QB + g)
                        mm3(pe, ps[:, 7, 0:all_], v[:, QB * P:TOK], vl[:, QB * P:TOK], W[:, nc_ * all_:(nc_ + 1) * all_],
                            Wl[:, nc_ * all_:(nc_ + 1) * all_], True, False)
                    pe.wait_ge(S.item_low, it + 1)
                    for j in range(nc_):
                        x = slice(j * all_ + b * rows, j * all_ + (b + 1) * rows)
                        mm = mm3(pe, ps[:, 7, b * rows:(b + 1) * rows], kc[b % 2][:, j * P:(j + 1) * P],
                                 kcl[b % 2][:, j * P:(j + 1) * P], W[:, x], Wl[:, x], False, b == 3 and j == nc_ - 1)
                    mm.then_inc(S.item_used, 1)
                elif what == "O" and (s[1] < QB or kind == "A"):
                    u = s[1]
                    rows = P if u < QB else 64
                    pe.wait_ge(S.o_rows, turned_o(kind, T, u))
                    pe.transpose(ps[:, 7, 256:256 + rows], (osb2 if kind == "A" else osb)[0:rows, :],
                                 ident[0:rows, 0:rows]).then_inc(S.o_turned, 1)

            def o_bank_free(kind, T, u):
                pe.wait_ge(S.act_low, un(T, u) - 1)

            def out_piece(T, n, c, turns):
                w, wl = ring.ready(pe, c, turns) if n == 0 else (ring.w[c % 2][:, :], ring.wl[c % 2][:, :])
                if n == 0:
                    pe.wait_ge(S.act_low, un(T, UNITS - 1))
                    pe.wait_ge(S.v_rows, v_rows_before_out(T))
                for b, (lo, hi) in enumerate(COLS):
                    if n:
                        pe.wait_ge(S.out_evac, 3 * (KT * T + n - 1) + b + 1)
                    mm = mm3(pe, ps[:, b, 0:hi - lo], w[:, n * P:(n + 1) * P], wl[:, n * P:(n + 1) * P],
                             actr[:, lo:hi], actl[:, lo:hi], True, True)
                    mm.then_inc(*((S.t_used[c % 2], 1) if (n, b) == (KT - 1, 2) else (S.out_ready, 1)))

            def v_rows_before_out(T):
                if odd:
                    return T + 1 - KV_OF_C + 1 if not (isinstance(T, int) and T == 15) else 14
                return min(kv(*next_tile("A", T)), 5) + 1

            def scores(kind, T, u, z, n):
                if u == 0 and z == 0:
                    pe.wait_ge(S.q_low, T + 1)
                    pe.wait_ge(S.k_low, n + 1)
                if not (isinstance(T, int) and T == T0 and u == z == 0):
                    pe.wait_ge(S.exps, s_no(T, u, z) - 1)
                k0, wd = first_key(kind, u), width(kind, u)
                qs = slice(u * P, (u + 1) * P)
                r = slice(HD * z, HD * z + HD)
                for lo in range(0, wd, 512):
                    hi = min(lo + 512, wd)
                    diag = hi == wd
                    early = kind != "A" and u >= WIN[kind] and lo == 0
                    mm = mm3(pe, s_banks[:, lo:hi], q[r, qs], ql[r, qs], kk[r, k0 + lo:k0 + hi],
                             kl[r, k0 + lo:k0 + hi], True, not diag and not early)
                    if diag:
                        mm = pe.matmul(s_banks[:, wd - CHUNK:wd], K[0:1, C_L:C_L + P], K[0:1, C_R:C_R + CHUNK],
                                       start=False, stop=not early, skip_group_check=True)
                    if early:
                        mm = pe.matmul(s_banks[:, 0:CHUNK], K[0:1, C_L + P:C_L + 2 * P], K[0:1, C_R:C_R + CHUNK],
                                       start=False, stop=True, skip_group_check=True)
                mm.then_inc(S.scores, 1)

            run(pe, do)
            for n in range(KT):
                out_piece(T0 + 7, n, cb + total - 1, 0)

        @block.scalar
        def _(act):
            norm_act(act, S, G, m, [F["q"], F["k"]], F["v"])
            for c in range(2):
                ring.split_high(act, cb + c)
            mod_act(act, S, G, m, a, [F["q"], F["k"]], sw)
            act.wait_ge(S.hp_low, KT * (m + 1))
            ch = Chain(act, S.act_step[m // 2])
            acc0 = ps[:, 0:3, :].rearrange("p b n -> p (b n)")[:, 0:TOK]
            start = [0]

            def split(c, turns):
                if c + 2 < cb + total or not isinstance(turns, int):
                    ring.split_high(act, c + 2, turns)

            def do(what, kind, T, s, c, turns):
                n = kv(kind, T)
                first = isinstance(T, int) and T == T0
                if what == "LOOP":
                    start[0] = ch.n
                    ch.base, ch.n = start[0] + (T - T0 - 1) * C_ACT_STEPS, 0
                elif what == "END":
                    assert ch.n == C_ACT_STEPS, ("C_ACT_STEPS", ch.n)
                    ch.base, ch.n = start[0] + 6 * C_ACT_STEPS, 0
                elif what == "F" and s[2] == KT - 1:
                    nk, nT = next_tile(kind, T)
                    name = s[1]
                    ring.done(act, c, turns)
                    if not (isinstance(T, int) and T == T0 - 1):
                        if name == "q":
                            act.wait_ge(S.q_low, T + 1)
                        elif name == "k":
                            act.wait_ge(S.k_low, n + 1)
                            act.wait_ge(S.k_turned, n + 1)
                        else:
                            act.wait_ge(S.v_turned, n + 1)
                    act.copy(F[name][:, :], acc0).then_inc({"q": S.q_evac, "k": S.k_evac, "v": S.v_evac}[name], 1)
                elif what == "W":
                    split(c - 1, turns)
                elif what in ("CQ", "CK"):
                    isq = what == "CQ"
                    src, dst = (F["q"], q) if isq else (F["k"], kk)
                    if odd:
                        act.wait_ge(S.q_evac if isq else S.k_evac, (T if isq else n) + 1)
                    else:
                        act.wait_ge(S.roped, rope_no(kind, T, isq))
                    if not first:
                        act.wait_ge(S.stream_scores, 2 * T)
                    act.copy(dst[:, :], src[:, :]).then_inc(S.q_high if isq else S.k_high, 1)
                elif what == "VT":
                    act.wait_ge(S.v_turned, n + 1)
                    if n_before(n):
                        act.wait_ge(S.stored, 64 * n)
                        act.wait_ge(S.pv, QB * T)
                        act.wait_ge(S.item_used, 16 * T)
                    if not odd:
                        act.wait_ge(S.roped, rope_no(kind, T, False))
                    act.copy(sw[:, :], acc0).then_inc(S.v_rows, 1)
                elif what == "VS":
                    act.wait_ge(S.v_rows, n + 1)
                    act.copy(v[:, :], sw[:, :]).then_inc(S.v_high, 1)
                elif what == "KR":
                    act.wait_ge(S.k_turned, n + 1)
                    act.wait_ge(S.stored, 64 * n + 32)
                    act.wait_ge(S.v_low, n + 1)
                    act.copy(sw[:, 0:SEQ], t_banks)
                    act.copy(sw[:, SEQ:TOK], ps[:, 7, 3 * P:4 * P]).then_inc(S.k_rows, 1)
                elif what == "S":
                    softmax(kind, T, s[1], s[2], width(kind, s[1]))
                elif what == "X":
                    softmax(kind, T, s[1], 0, stream_width(kind))
                elif what == "T":
                    u, z = s[1:]
                    act.wait_ge(S.turned, t_no(kind, T, u, z))
                    if z == 0 and not (first and u == 0):
                        w_free(act, kind, T, u)
                    w0, wn = probs_at(kind, u, z)
                    i_ = act.copy(W[:, w0:w0 + wn], t_banks[:, 0:wn])
                    i_.then_inc(S.w_high, 1)
                elif what == "K":
                    g, b = s[1:]
                    it = item(T, g, b)
                    nk = CACHE_B[kind] * P
                    act.wait_ge(S.kc_turned, 8 * T + 4 * g + b + 1)
                    if not (isinstance(T, int) and T == 0 and g == 0 and b < 2):
                        act.wait_ge(S.item_used, it - 1)
                    act.copy(kc[b % 2][:, 0:nk], ps[:, 5 + b % 2, 0:nk]).then_inc(S.item_high, 1)
                elif what == "VH":
                    g, b = s[1:]
                    it = item(T, g, 4 + b)
                    nk = CACHE_B[kind]
                    act.wait_ge(S.raw_in[b], 16 * (4 * T + 2 * g + 2))
                    act.wait_ge(S.item_used, it - 1)
                    act.copy(kc[b % 2][:, 0:nk * P], raw[b][:, 0:nk, :].rearrange("p j d -> p (j d)")).then_inc(
                        S.item_high, 1)
                elif what == "V":
                    outputs(kind, T, s[1])
                elif what == "N" and kind == "A":
                    u = s[1]
                    rows = P if u < QB else 64
                    act.wait_ge(S.rstd, un(T, u))
                    act.activation(osb2[0:rows, :], osb[0:rows, :], ACT.Copy, scale=rstd[0:rows, :]).then_inc(S.o_rows, 1)
                elif what == "O" and (s[1] < QB or kind == "A"):
                    u = s[1]
                    rows = P if u < QB else 64
                    act.wait_ge(S.o_turned, turned_o(kind, T, u))
                    if u == 0 and not first:
                        act_free(T, c, turns)
                    lo = u * P if u < QB else SEQ + 64 * (u - QB)
                    act.activation(actr[:, lo:lo + rows], ps[:, 7, 256:256 + rows], ACT.Copy,
                                   scale=G.gsub[:, 0:1] if kind == "A" else 1.0).then_inc(S.act_high, 1)

            def n_before(n):
                return not (isinstance(n, int) and n == (6 if odd else 0))

            def act_free(T, c, turns):
                act.wait_ge(S.out_evac, 3 * KT * T)

            def softmax(kind, T, u, z, wd):
                act.wait_ge(S.nmax, s_no(T, u, z))
                mx, nm, sm, rc, es, coef = rows_of(u)
                off = e_at(kind, u, z)
                i_ = act.activation(E[:, off:off + wd], s_banks[:, 0:wd], ACT.Exp, bias=nm[:, z:z + 1], scale=SCALE,
                                    accum_out=sm[:, z:z + 1])
                if kind == "B":
                    sink = G.sinkp[:, 2 * (T - 4) + z:2 * (T - 4) + z + 1] if u < QB else G.sinks_s[:, T - 4:T - 3]
                    i_ = act.activation(es[:, z:z + 1], sink, ACT.Exp, bias=nm[:, z:z + 1], scale=1.0)
                i_.then_inc(S.exps, 1)

            def outputs(kind, T, u):
                rc = rows_of(u)[3]
                act.wait_ge(S.probs, un(T, u))
                if u < QB:
                    act.wait_ge(S.pv, QB * T + u + 1)
                    if kind == "A":
                        ch.then(act.activation(osb[:, :], ps[:, 7, 0:P], ACT.Copy, scale=rc[:, 0:1]))
                    else:
                        act.activation(osb[:, 0:HD], ps[:, 7, 0:HD], ACT.Copy, scale=rc[:, 0:1])
                        act.activation(osb[:, HD:P], ps[:, 7, HD:P], ACT.Copy, scale=rc[:, 1:2]).then_inc(S.o_rows, 1)
                    rows = P
                else:
                    g = u - QB
                    act.wait_ge(S.item_used, item(T, g, 7) + 1)
                    if kind == "A":
                        act.copy(E[:, 1664:1664 + 64], ps[:, 7, 0:64]).then_inc(S.od, 1)
                        act.wait_ge(S.od_turned, 2 * T + g + 1)
                        ch.then(act.copy(osb[0:64, :], ps[0:64, 7, P:2 * P]))
                    else:
                        for z in range(2):
                            r = slice(HD * z, HD * z + HD)
                            src = ps[r, 7, 0:P].rearrange("p (b x) -> p b x", b=4)[:, :, z * NS:z * NS + NS]
                            i_ = act.copy(actr[r, SEQ + 64 * g:SEQ + 64 * g + 64].rearrange("p (b q) -> p b q", b=4), src)
                        i_.then_inc(S.act_high, 1)
                    rows = 64
                if kind == "A":
                    act.activation(osb2[0:rows, :], osb[0:rows, :], ACT.Square,
                                   accum_out=ss[0:rows, :]).then_inc(S.squares, 1)

            run(act, do)

        @block.vector
        def _(dve):
            ch = Chain(dve, S.dve_step[m])
            for c in range(2):
                ring.split_low(dve, cb + c)
            mod_dve(dve, ch, S, G, m, a, [F["q"], F["k"]], F["v"], sw)
            start = [0]
            def split(c, turns):
                if c + 2 < cb + total or not isinstance(turns, int):
                    ring.split_low(dve, c + 2, turns)

            def do(what, kind, T, s, c, turns):
                n = kv(kind, T)
                first = isinstance(T, int) and T == T0
                if what == "LOOP":
                    start[0] = ch.n
                    ch.base, ch.n = start[0] + (T - T0 - 1) * C_DVE_STEPS, 0
                elif what == "END":
                    assert ch.n == C_DVE_STEPS, ("C_DVE_STEPS", ch.n)
                    ch.base, ch.n = start[0] + 6 * C_DVE_STEPS, 0
                elif what == "W":
                    split(c - 1, turns)
                elif what == "R" and not odd:
                    rotate(s[1], *next_tile(kind, T))
                elif what == "OUT":
                    out_evac(T - 1, s[1], c, turns)
                elif what == "CQ":
                    dve.wait_ge(S.q_high, T + 1)
                    dve.tensor_tensor(ql[:, :], F["q"][:, :], q[:, :].bitcast(F32), ALU.subtract).then_inc(S.q_low, 1)
                elif what == "CK":
                    dve.wait_ge(S.k_high, n + 1)
                    dve.tensor_tensor(kl[:, :], F["k"][:, :], kk[:, :].bitcast(F32), ALU.subtract).then_inc(S.k_low, 1)
                elif what == "VS":
                    dve.wait_ge(S.v_high, n + 1)
                    dve.tensor_tensor(vl[:, :], sw[:, :], v[:, :].bitcast(F32), ALU.subtract).then_inc(S.v_low, 1)
                elif what == "S":
                    maxima(kind, T, s[1], s[2], width(kind, s[1]))
                elif what == "X":
                    maxima(kind, T, s[1], 0, stream_width(kind))
                elif what == "T":
                    u, z = s[1:]
                    dve.wait_ge(S.w_high, t_no(kind, T, u, z))
                    w0, wn = probs_at(kind, u, z)
                    i_ = dve.tensor_tensor(Wl[:, w0:w0 + wn], t_banks[:, 0:wn], W[:, w0:w0 + wn].bitcast(F32), ALU.subtract)
                    i_.then_inc(S.w_low, 1)
                elif what == "FA":
                    factors(kind, T, s[1])
                elif what in ("K", "VI"):
                    g, b = s[1:]
                    it = item(T, g, b + (4 if what == "VI" else 0))
                    nk = CACHE_B[kind] * P
                    dve.wait_ge(S.item_high, it + 1)
                    src = ps[:, 5 + b % 2, 0:nk] if what == "K" else \
                        raw[b][:, 0:CACHE_B[kind], :].rearrange("p j d -> p (j d)")
                    dve.tensor_tensor(kcl[b % 2][:, 0:nk], src, kc[b % 2][:, 0:nk].bitcast(F32),
                                      ALU.subtract).then_inc(S.item_low, 1)
                elif what == "V" and kind == "A":
                    u = s[1]
                    rows = P if u < QB else 64
                    dve.wait_ge(S.squares, un(T, u))
                    dve.tensor_scalar(ms[0:rows, :], ss[0:rows, :], 1.0 / P, EPS, ALU.mult, ALU.add).then_inc(S.ms, 1)
                elif what == "O":
                    u = s[1]
                    dve.wait_ge(S.act_high, un(T, u))
                    if u < QB or kind == "A":
                        rows = P if u < QB else 64
                        lo = u * P if u < QB else SEQ + 64 * (u - QB)
                        dst, src, hi = actl[:, lo:lo + rows], ps[:, 7, 256:256 + rows], actr[:, lo:lo + rows].bitcast(F32)
                        if kind == "A":
                            i_ = dve.scalar_tensor_tensor(out=dst, in0=src, scalar=G.gsub[:, 0:1], in1=hi, op0=ALU.mult,
                                                          op1=ALU.subtract)
                        else:
                            i_ = dve.tensor_tensor(dst, src, hi, ALU.subtract)
                    else:
                        g = u - QB
                        cs = slice(SEQ + 64 * g, SEQ + 64 * g + 64)
                        for z in range(2):
                            r = slice(HD * z, HD * z + HD)
                            src = ps[r, 7, 0:P].rearrange("p (b x) -> p b x", b=4)[:, :, z * NS:z * NS + NS]
                            i_ = dve.tensor_tensor(actl[r, cs].rearrange("p (b q) -> p b q", b=4), src,
                                                   actr[r, cs].bitcast(F32).rearrange("p (b q) -> p b q", b=4), ALU.subtract)
                    i_.then_inc(S.act_low, 1)

            def rotate(name, nk, nT):
                f = F[name]
                no = rope_no(nk, nT, name == "q")
                if nT == 0 and name == "q":
                    dve.wait_ge(S.rope_in, 16)
                dve.wait_ge(S.swapped, 64 * no)
                for x, j in ((f, 0), (sw, 1)):
                    dve.tensor_tensor(x[:, 0:SEQ], x[:, 0:SEQ], rope[:, j, 0:SEQ], ALU.mult)
                    x3 = x[:, SEQ:TOK].rearrange("p (b q) -> p b q", b=NB)
                    i_ = dve.tensor_tensor(x3, x3, rope[:, j, SEQ:ROPE_N].unsqueeze(1).broadcast_to([P, NB, NS]), ALU.mult)
                ch.then(i_)
                dve.tensor_tensor(f[:, :], f[:, :], sw[:, :], ALU.add).then_inc(S.roped, 1)

            def maxima(kind, T, u, z, wd):
                mx, nm, sm, rc, es, coef = rows_of(u)
                if u < QB:
                    dve.wait_ge(S.scores, 2 * (QB * T + u) + z + 1)
                else:
                    dve.wait_ge(S.stream_scores, 2 * T + u - QB + 1)
                if kind == "C":
                    if u < QB:
                        if u == 0 and z == 0:
                            dve.wait_ge(S.bias_in, bias_no(T))
                        n = min(wd, 256)
                        x = s_banks[:, wd - n:wd]
                        ch.then(dve.tensor_tensor(x, x, bt[:, z, 256 - n:256], ALU.add))
                    else:
                        x = s_banks[:, 384:512]
                        dve.tensor_tensor(x, x, bs[:, 0:P], ALU.add)
                        x = s_banks[:, 512:640].rearrange("p (b q) -> p b q", b=NB)
                        ch.then(dve.tensor_tensor(x, x, bs[:, P:P + NS].unsqueeze(1).broadcast_to([P, NB, NS]), ALU.add))
                mz = mx[:, z:z + 1]
                ch.then(dve.tensor_reduce(mz, s_banks[:, 0:wd], AX.X, ALU.max))
                if kind == "B":
                    sink = G.sinkp[:, 2 * (T - 4) + z:2 * (T - 4) + z + 1] if u < QB else G.sinks_s[:, T - 4:T - 3]
                    ch.then(dve.scalar_tensor_tensor(out=mz, in0=mz, scalar=SCALE, in1=sink, op0=ALU.mult, op1=ALU.max))
                dve.tensor_scalar(nm[:, z:z + 1], mz, -1.0 if kind == "B" else -SCALE, None,
                                  ALU.mult).then_inc(S.nmax, 1)

            def factors(kind, T, u):
                mx, nm, sm, rc, es, coef = rows_of(u)
                dve.wait_ge(S.exps, s_no(T, u, 1 if u < QB else 0))
                z = 2 if u < QB else 1
                if kind == "B":
                    ch.then(dve.tensor_tensor(sm[:, 0:z], sm[:, 0:z], es[:, 0:z], ALU.add))
                if kind != "A" and u < QB:
                    dve.reciprocal(rc, sm).then_inc(S.probs, 1)
                    return
                ch.then(dve.reciprocal(rc[:, 0:z], sm[:, 0:z]))
                x = E[:, e_at(kind, u):e_at(kind, u) + (width(kind, u) if u < QB else stream_width(kind))]
                if u < QB:
                    ch.then(dve.scalar_tensor_tensor(out=coef, in0=rc[:, 1:2], scalar=sm[:, 0:1], in1=G.nlam[:, 0:1],
                                                     op0=ALU.mult, op1=ALU.mult))
                    y = e_at(kind, u, 1)
                    dve.scalar_tensor_tensor(out=x, in0=E[:, y:y + width(kind, u)], scalar=coef, in1=x,
                                             op0=ALU.mult, op1=ALU.add).then_inc(S.probs, 1)
                else:
                    dve.tensor_scalar(x, x, rc[:, 0:1], G.cfac[:, 0:1] if kind == "A" else None,
                                      ALU.mult, ALU.mult if kind == "A" else ALU.bypass).then_inc(S.probs, 1)

            def bias_no(T):
                return 16 * BIAS_DMAS * (T - T0 + 1)

            def out_evac(T, n, c, turns):
                for b, (lo, hi) in enumerate(COLS):
                    if (n, b) == (KT - 1, 2):
                        ring.done(dve, c, turns)
                    else:
                        dve.wait_ge(S.out_ready, (3 * KT - 1) * T + 3 * n + b + 1)
                    y, x = ps[:, b, 0:hi - lo], G.xT[:, n, lo:hi]
                    if b < 2:
                        i_ = dve.scalar_tensor_tensor(out=x, in0=y, scalar=G.mod[:, a, 16 + n, 0:1], in1=x,
                                                      op0=ALU.mult, op1=ALU.add)
                    else:
                        if n >= 2:
                            dve.wait_ge(S.out_evac, 3 * (KT * T + n - 1))
                        tmp = rtmp[n % 2]
                        ch.then(dve.tensor_tensor(tmp.rearrange("p (b q) -> p b q", b=NB),
                                                  y.rearrange("p (b q) -> p b q", b=NB),
                                                  G.mod[:, a, 16 + n, 1:NC9].unsqueeze(2).broadcast_to([P, NB, NS]),
                                                  ALU.mult))
                        i_ = dve.tensor_tensor(x, x, tmp, ALU.add)
                    i_.then_inc(S.out_evac, 1)

            r0 = 2304 if odd else 1792
            rtmp = E[:, r0:r0 + TS], E[:, r0 + TS:r0 + 2 * TS]
            run(dve, do)
            for n in range(KT):
                out_evac(T0 + 7, n, cb + total - 1, 0)


BIAS_DMAS = 5
C_ACT_STEPS = 0
C_DVE_STEPS = 46


def finish(nc, S, G, outs):
    ctx = ExitStack()
    with ctx:
        def sb(name, shape, dt=F32):
            return ctx.enter_context(nc.sbuf_tensor(name, shape, dt))

        sq = [sb(f"fin_sq{j}", [P, TOK]) for j in range(2)]
        rs = sb("fin_rs", [P, TOK])
        rows = [sb(f"fin_rows{j}", [P, D]) for j in range(3)]
        ps, xT = G.psum, G.xT
        ident = G.consts[:, C_ID:C_ID + P]
        block = ctx.enter_context(nc.Block())

        @block.tensor
        def _(pe):
            norm_pe(pe, S, G, 4, sq)
            pe.wait_ge(S.root, 5)
            for t in range(TB):
                if t == 0:
                    pe.wait_ge(S.fin_scaled, KT)
                if t >= 4:
                    pe.wait_ge(S.fin_rows, t - 3)
                for k in range(KT):
                    mm = pe.transpose(ps[:, 2 * (t % 4) + k // 4, (k % 4) * P:(k % 4 + 1) * P],
                                      xT[:, k, t * P:(t + 1) * P], ident)
                mm.then_inc(S.fin_turned, 1)

        @block.scalar
        def _(act):
            norm_act(act, S, G, 4, sq, rs)
            for t in range(TB):
                act.wait_ge(S.fin_turned, t + 1)
                if t >= 3:
                    act.wait_ge(S.fin_out[t % 3], 16 * (t // 3))
                act.copy(rows[t % 3][:, :], ps[:, 2 * (t % 4):2 * (t % 4) + 2, :].rearrange("p b n -> p (b n)")).then_inc(
                    S.fin_rows, 1)

        @block.vector
        def _(dve):
            dve.wait_ge(S.root, 5)
            dve.reciprocal(rs[:, :], rs[:, :]).then_inc(S.dve_step[4], 1)
            dve.wait_ge(S.dve_step[4], 1)
            for k in range(KT):
                dve.scalar_tensor_tensor(out=xT[:, k, :], in0=xT[:, k, :], scalar=G.gT[:, 32 + k:33 + k], in1=rs[:, :],
                                         op0=ALU.mult, op1=ALU.mult).then_inc(S.fin_scaled, 1)

        @block.sync
        def _(sp):
            y = outs["y_s"].rearrange("b q d -> (b q) d")
            for t in range(TB):
                sp.wait_ge(S.fin_rows, t + 1)
                dst = outs["y_p"][0, t * P:(t + 1) * P, :] if t < QB else y
                sp.dma_start(dst, rows[t % 3][:, :]).then_inc(S.fin_out[t % 3], 16)
            for j in range(3):
                sp.wait_ge(S.fin_out[j], 48)


class Semaphores:

    def __init__(self, nc, ctx):
        def make(names):
            return [ctx.enter_context(nc.semaphore(n)) for n in names.split()]

        def several(name, n):
            return [ctx.enter_context(nc.semaphore(f"{name}{j}")) for j in range(n)]

        (self.settled, self.const_in, self.c_in, self.vec_in, self.lam_in, self.tab_in, self.sink_in, self.rev_made) = make(
            "settled const_in c_in vec_in lam_in tab_in sink_in rev_made")
        (self.rev_out, self.set_ones, self.set_zero, self.adab_in, self.csil, self.lam_dot, self.lam_exp) = make(
            "rev_out set_ones set_zero adab_in csil lam_dot lam_exp")
        (self.cT_ready, self.c_high, self.c_low, self.x_turned, self.x_evac, self.ada_evac, self.small_ready, self.small_evac) = make(
            "cT_ready c_high c_low x_turned x_evac ada_evac small_ready small_evac")
        (self.mod_mm, self.mod_evac, self.set_step) = make(
            "mod_mm mod_evac set_step")
        (self.sq_ready, self.sq_used, self.root, self.hs_ready, self.hs_high, self.hs_low, self.hp_ready, self.hp_high) = make(
            "sq_ready sq_used root hs_ready hs_high hs_low hp_ready hp_high")
        (self.hp_low,) = make(
            "hp_low")
        (self.st_in, self.st_turned, self.st_evac, self.pads, self.u_evac, self.u_last, self.u_zero, self.so_turned) = make(
            "st_in st_turned st_evac pads u_evac u_last u_zero so_turned")
        (self.so_evac, self.so_out, self.so_free, self.conv, self.silu, self.prod, self.act_high_f, self.act_low_f) = make(
            "so_evac so_out so_free conv silu prod act_high_f act_low_f")
        (self.d_ready, self.d_evac) = make(
            "d_ready d_evac")
        (self.rope_in, self.dup_in, self.qz_zero, self.q_evac, self.k_evac, self.v_evac, self.q_high, self.q_low) = make(
            "rope_in dup_in qz_zero q_evac k_evac v_evac q_high q_low")
        (self.k_high, self.k_low, self.v_high, self.v_low, self.v_rows, self.k_rows, self.v_turned, self.k_turned) = make(
            "k_high k_low v_high v_low v_rows k_rows v_turned k_turned")
        (self.stored,) = make(
            "stored")
        (self.swapped, self.roped, self.bias_in, self.kept, self.kc_turned, self.item_high, self.item_low, self.item_used) = make(
            "swapped roped bias_in kept kc_turned item_high item_low item_used")
        (self.qz, self.scores, self.stream_scores, self.nmax, self.exps, self.probs, self.turned) = make(
            "qz scores stream_scores nmax exps probs turned")
        (self.w_high, self.w_low, self.pv, self.od, self.od_turned, self.squares, self.ms, self.rstd) = make(
            "w_high w_low pv od od_turned squares ms rstd")
        (self.o_rows, self.o_turned, self.act_high, self.act_low, self.out_ready, self.out_evac) = make(
            "o_rows o_turned act_high act_low out_ready out_evac")
        (self.fin_scaled, self.fin_turned, self.fin_rows) = make(
            "fin_scaled fin_turned fin_rows")
        self.ada_landed = several("ada_landed", 6)
        self.f_landed = several("f_landed", 3)
        self.f_high = several("f_high", 3)
        self.f_low = several("f_low", 3)
        self.f_used = several("f_used", 3)
        self.t_landed = several("t_landed", 2)
        self.t_high = several("t_high", 2)
        self.t_low = several("t_low", 2)
        self.t_used = several("t_used", 2)
        self.raw_in = several("raw_in", 4)
        self.x_in = several("x_in", TB)
        self.dve_step = several("dve_step", 5)
        self.act_step = several("act_step", 2)
        self.fin_out = several("fin_out", 3)


class Shared:
    pass


def encoder(nc, ins, outs):
    ctx = ExitStack()
    with ctx:
        S, G = Semaphores(nc, ctx), Shared()

        def sb(name, shape, dt=F32):
            return ctx.enter_context(nc.sbuf_tensor(name, shape, dt))

        G.xT = sb("xT", [P, KT, TOK])
        G.mod = sb("mod", [P, 4, 24, NC9])
        G.gs = sb("gs", [P, 4, KT, NC9])
        G.gT = sb("gT", [P, 41])
        G.cvT = sb("cvT", [P, 2, 4, 2 * FT])
        G.consts = sb("consts", [P, C_N])
        G.ones = sb("ones", [P, P])
        columns = sb("columns", [P, 5])
        G.eps, G.mhalf, G.nlam, G.cfac, G.gsub = (columns[:, j:j + 1] for j in range(5))
        G.sinkp, G.sinks_s = sb("sinkp", [P, 8]), sb("sinks_s", [P, 4])
        G.psum = ctx.enter_context(nc.psum_tensor("psum", [P, 8, 512], F32))
        G.rev_dram = nc.dram_tensor("rev_dram", (16, 384), F32, kind="Internal").ap()
        G.bias_dram = nc.dram_tensor("bias_dram", (16, P, 256), F32, kind="Internal").ap()
        with ExitStack() as c:
            setup(nc, S, G, ins, c)
        G.h = sb("h", [P, KT, TOK], F32R)
        G.hl = sb("hl", [P, KT, TOK], BF16)
        attention(nc, S, G, ins, outs, "AB")
        ffn(nc, S, G, ins, outs, 0)
        attention(nc, S, G, ins, outs, "C")
        ffn(nc, S, G, ins, outs, 1)
        finish(nc, S, G, outs)


INS = ["x_prompt", "x_sample", "c_prompt", "c_sample", "cache_a_k", "cache_a_v", "cache_b_k", "cache_b_v",
       "cache_c_k", "cache_c_v", "state_conv", "ada_w", "ada_b", "norm_g", "final_g", "w_in_even", "w_out_even",
       "lam_q1", "lam_k1", "lam_q2", "lam_k2", "subln_g", "sinks", "w_in_odd", "w_out_odd", "rel_bias",
       "w_up", "conv_w", "conv_b", "w_down"]
OUTS = [("y_p", (1, SEQ, D)), ("y_s", (NB, NS, D)),
        ("ak_p", (1, 1, SEQ, 4, P)), ("av_p", (1, 1, SEQ, 4, P)), ("ak_s", (1, NB, NS, 4, P)), ("av_s", (1, NB, NS, 4, P)),
        ("bk_p", (1, 1, P, 2, HD)), ("bv_p", (1, 1, P, 2, HD)), ("bk_s", (1, NB, P, 2, HD)), ("bv_s", (1, NB, P, 2, HD)),
        ("ck_p", (1, 1, PAST, 16, HD)), ("cv_p", (1, 1, PAST, 16, HD)), ("ck_s", (1, NB, PAST, 16, HD)),
        ("cv_s", (1, NB, PAST, 16, HD)),
        ("conv_p", (2, 1, 2, 2 * DFF)), ("conv_s", (2, NB, 2, 2 * DFF))]


def kernel(**inputs):
    import numpy as _np
    import concourse.bacc as _bacc
    from concourse.bass_utils import run_bass_kernel_spmd as _run

    nc = _bacc.Bacc("TRN2", target_bir_lowering=False, num_devices=1)
    arrays, ins, outs = {}, {}, {}
    table, rope = shape_constants()
    given = {n: _np.ascontiguousarray(inputs[n]) for n in INS}
    given["consts"], given["rope"] = table, rope
    for name, arr in given.items():
        arrays[f"in_{name}"] = arr
        ins[name] = nc.dram_tensor(f"in_{name}", arr.shape, mybir.dt.from_np(arr.dtype), kind="ExternalInput").ap()
    for name, shape in OUTS:
        outs[name] = nc.dram_tensor(f"out_{name}", shape, F32, kind="ExternalOutput").ap()
    encoder(nc, ins, outs)
    r = _run(nc, [arrays], core_ids=[0])
    return tuple(r.results[0][f"out_{name}"] for name, _ in OUTS)
```
